# Optimizing a Trainium2 kernel written in Bass

```python
import jax, jax.numpy as jnp
from jax import lax
import numpy as np

D_MODEL = 1024
BATCH = 1
SEQ = 256
DEPTH = 2

RET_HEAD_DIM = 128
RET_WIDTH = D_MODEL // 2
RET_HEADS = RET_WIDTH // RET_HEAD_DIM
HGRN_HEAD_DIM = 128
HGRN_WIDTH = D_MODEL - RET_WIDTH
HGRN_HEADS = HGRN_WIDTH // HGRN_HEAD_DIM
MIX_WIDTH = RET_WIDTH + HGRN_WIDTH
IN_WIDTHS = [RET_WIDTH] * 4 + [HGRN_WIDTH] * 5
IN_COLS = sum(IN_WIDTHS)
RET_CHUNK = 128
HGRN_CHUNK = 64
ROPE_BASE = 10000.0
N_EXPERTS = 16
CAPACITY_FACTOR = 2
EXPERT_FF = 1024
NORM_EPS = 1e-6


def rms_normalize(x):
    xf = x.astype(jnp.float32)
    return (xf * lax.rsqrt(jnp.mean(xf * xf, axis=-1, keepdims=True) + NORM_EPS)).astype(x.dtype)

def rms_norm(x, g):
    return rms_normalize(x) * g.astype(x.dtype)

def to_heads(t, n_heads):
    b, s, _ = t.shape
    return t.reshape(b, s, n_heads, -1).transpose(0, 2, 1, 3)

def from_heads(t):
    b, h, s, d = t.shape
    return t.transpose(0, 2, 1, 3).reshape(b, s, h * d)

def to_chunks(t, chunk):
    b, h, s, d = t.shape
    return t.reshape(b, h, s // chunk, chunk, d).transpose(2, 0, 1, 3, 4)

def from_chunks(t):
    n, b, h, c, d = t.shape
    return t.transpose(1, 2, 0, 3, 4).reshape(b, h, n * c, d)

def rotary(x, pos):
    half = x.shape[-1] // 2
    inv_freq = ROPE_BASE ** (-jnp.arange(half, dtype=jnp.float32) / half)
    ang = pos.astype(jnp.float32)[:, None] * inv_freq[None, :]
    cos = jnp.cos(ang).astype(x.dtype)
    sin = jnp.sin(ang).astype(x.dtype)
    x1, x2 = x[..., :half], x[..., half:]
    return jnp.concatenate([x1 * cos - x2 * sin, x1 * sin + x2 * cos], axis=-1)

def retention_scan(q, k, v, log_gamma, include_diag):
    b, h, s, dk = q.shape
    dv = v.shape[-1]
    dt = q.dtype
    L = RET_CHUNK
    t = jnp.arange(L, dtype=jnp.float32)
    diff = t[:, None] - t[None, :]
    mask = (diff >= 0) if include_diag else (diff > 0)
    lg = log_gamma[:, None, None]
    intra_decay = jnp.where(mask, jnp.exp(lg * jnp.maximum(diff, 0.0)), 0.0).astype(dt)
    q_decay = jnp.exp(log_gamma[:, None] * (t + 1.0))[:, :, None].astype(dt)
    k_decay = jnp.exp(log_gamma[:, None] * (L - 1.0 - t))[:, :, None].astype(dt)
    chunk_decay = jnp.exp(log_gamma * L)[:, None, None].astype(dt)

    def step(state, inp):
        qc, kc, vc = inp
        scores = jnp.einsum('bhid,bhjd->bhij', qc, kc) * intra_decay
        out = (jnp.einsum('bhij,bhjv->bhiv', scores, vc)
               + jnp.einsum('bhid,bhdv->bhiv', qc * q_decay, state))
        state = chunk_decay * state + jnp.einsum('bhjd,bhjv->bhdv', kc * k_decay, vc)
        return state, out

    state0 = jnp.zeros((b, h, dk, dv), dt)
    _, out = lax.scan(step, state0, (to_chunks(q, L), to_chunks(k, L), to_chunks(v, L)))
    return from_chunks(out)

def hgrn2_scan(q, k, v, log_f):
    b, h, s, dk = q.shape
    dv = v.shape[-1]
    dt = q.dtype
    L = HGRN_CHUNK
    causal = jnp.tril(jnp.ones((L, L), dtype=bool))[:, :, None]

    def step(state, inp):
        qc, kc, vc, gc = inp
        cum = jnp.cumsum(gc, axis=2)
        rel = jnp.exp(jnp.where(causal, cum[:, :, :, None, :] - cum[:, :, None, :, :], -jnp.inf)).astype(dt)
        scores = jnp.einsum('bhtd,bhsd,bhtsd->bhts', qc, kc, rel)
        out = (jnp.einsum('bhts,bhsv->bhtv', scores, vc)
               + jnp.einsum('bhtd,bhdv->bhtv', qc * jnp.exp(cum).astype(dt), state))
        cum_end = cum[:, :, -1, :]
        k_to_end = kc * jnp.exp(cum_end[:, :, None, :] - cum).astype(dt)
        state = (jnp.exp(cum_end).astype(dt)[..., None] * state
                 + jnp.einsum('bhsd,bhsv->bhdv', k_to_end, vc))
        return state, out

    state0 = jnp.zeros((b, h, dk, dv), dt)
    _, out = lax.scan(step, state0, (to_chunks(q, L), to_chunks(k, L), to_chunks(v, L), to_chunks(log_f, L)))
    return from_chunks(out)

def flip_seq(t):
    return jnp.flip(t, axis=2)

def hybrid_mixer(xn, w_in, ret_g, hgrn_g, w_out, lb):
    b, s, _ = xn.shape
    dt = xn.dtype
    proj = xn @ w_in
    splits = np.cumsum(IN_WIDTHS)[:-1].tolist()
    rq, rk, rv, rg, hq, hf_fwd, hf_bwd, hi, hg = jnp.split(proj, splits, axis=-1)

    pos = jnp.arange(s)
    q = rotary(to_heads(rq, RET_HEADS), pos)
    k = rotary(to_heads(rk, RET_HEADS), pos) * (RET_HEAD_DIM ** -0.5)
    v = to_heads(rv, RET_HEADS)
    log_gamma = jnp.log1p(-(2.0 ** (-5.0 - jnp.arange(RET_HEADS, dtype=jnp.float32))))
    r_out = (retention_scan(q, k, v, log_gamma, True)
             + flip_seq(retention_scan(flip_seq(q), flip_seq(k), flip_seq(v), log_gamma, False)))
    r_out = from_heads(rms_normalize(r_out)) * ret_g.astype(dt) * jax.nn.silu(rg)

    q2 = jax.nn.silu(to_heads(hq, HGRN_HEADS)) * (HGRN_HEAD_DIM ** -0.5)
    v2 = to_heads(hi, HGRN_HEADS)

    def forget(z):
        z = z.astype(jnp.float32)
        if lb is None:
            return jax.nn.log_sigmoid(z), jax.nn.sigmoid(-z).astype(dt)
        lbh = lb.astype(jnp.float32).reshape(HGRN_HEADS, 1, HGRN_HEAD_DIM)
        f = lbh + (1.0 - lbh) * jax.nn.sigmoid(z)
        return jnp.log(f), ((1.0 - lbh) * jax.nn.sigmoid(-z)).astype(dt)

    logf_f, k_f = forget(to_heads(hf_fwd, HGRN_HEADS))
    logf_b, k_b = forget(to_heads(hf_bwd, HGRN_HEADS))
    h_out = (hgrn2_scan(q2, k_f, v2, logf_f)
             + flip_seq(hgrn2_scan(flip_seq(q2), flip_seq(k_b), flip_seq(v2), flip_seq(logf_b))))
    h_out = rms_norm(from_heads(h_out), hgrn_g) * jax.nn.silu(hg)

    return jnp.concatenate([r_out, h_out], axis=-1) @ w_out

def expert_choice_ffn(xn, w_router, w_gate, w_up, w_down):
    b, s, d = xn.shape
    cap = CAPACITY_FACTOR * s // N_EXPERTS
    affinity = jax.nn.softmax((xn @ w_router).astype(jnp.float32), axis=-1)
    gate, idx = lax.top_k(jnp.swapaxes(affinity, 1, 2), cap)
    xe = jax.vmap(lambda xb, ib: xb[ib])(xn, idx)
    hid = (jax.nn.silu(jnp.einsum('becd,edf->becf', xe, w_gate))
           * jnp.einsum('becd,edf->becf', xe, w_up))
    ye = jnp.einsum('becf,efd->becd', hid, w_down) * gate[..., None].astype(xn.dtype)
    return jax.vmap(lambda yb, ib: jnp.zeros((s, d), yb.dtype).at[ib.reshape(-1)].add(yb.reshape(-1, d)))(ye, idx)

def first_inputs(seed: int = 0) -> dict:
    key = jax.random.key(seed)
    ks = jax.random.split(key, 14)
    f32 = jnp.float32
    x = jax.random.normal(ks[0], (BATCH, SEQ, D_MODEL), f32)
    norm1_g = 1.0 + 0.02 * jax.random.normal(ks[1], (DEPTH, D_MODEL), f32)
    w_in = jax.random.normal(ks[2], (DEPTH, D_MODEL, IN_COLS), f32) * D_MODEL ** -0.5
    ret_norm_g = 1.0 + 0.02 * jax.random.normal(ks[3], (DEPTH, RET_WIDTH), f32)
    hgrn_norm_g = 1.0 + 0.02 * jax.random.normal(ks[4], (DEPTH, HGRN_WIDTH), f32)
    w_out = jax.random.normal(ks[5], (DEPTH, MIX_WIDTH, D_MODEL), f32) * MIX_WIDTH ** -0.5
    lower_bounds = 0.1 * jax.random.normal(ks[6], (DEPTH, HGRN_WIDTH), f32)
    norm2_g = 1.0 + 0.02 * jax.random.normal(ks[7], (DEPTH, D_MODEL), f32)
    w_router = jax.random.normal(ks[8], (DEPTH, D_MODEL, N_EXPERTS), f32) * D_MODEL ** -0.5
    w_gate = jax.random.normal(ks[9], (DEPTH, N_EXPERTS, D_MODEL, EXPERT_FF), f32) * D_MODEL ** -0.5
    w_up = jax.random.normal(ks[10], (DEPTH, N_EXPERTS, D_MODEL, EXPERT_FF), f32) * D_MODEL ** -0.5
    w_down = jax.random.normal(ks[11], (DEPTH, N_EXPERTS, EXPERT_FF, D_MODEL), f32) * EXPERT_FF ** -0.5
    final_norm_g = 1.0 + 0.02 * jax.random.normal(ks[12], (D_MODEL,), f32)
    return {"x": x, "norm1_g": norm1_g, "w_in": w_in, "ret_norm_g": ret_norm_g,
            "hgrn_norm_g": hgrn_norm_g, "w_out": w_out, "lower_bounds": lower_bounds,
            "norm2_g": norm2_g, "w_router": w_router, "w_gate": w_gate, "w_up": w_up,
            "w_down": w_down, "final_norm_g": final_norm_g}

def first_block(x, norm1_g, w_in, ret_norm_g, hgrn_norm_g, w_out, lower_bounds,
              norm2_g, w_router, w_gate, w_up, w_down, final_norm_g):
    lbs = jax.nn.softmax(lower_bounds.astype(jnp.float32), axis=0)
    lbs = jnp.cumsum(lbs, axis=0) - lbs[0]
    h = x
    for layer in range(DEPTH):
        lb = lbs[layer] if layer > 0 else None
        h = h + hybrid_mixer(rms_norm(h, norm1_g[layer]), w_in[layer], ret_norm_g[layer],
                             hgrn_norm_g[layer], w_out[layer], lb)
        h = h + expert_choice_ffn(rms_norm(h, norm2_g[layer]), w_router[layer],
                                  w_gate[layer], w_up[layer], w_down[layer])
    return rms_norm(h, final_norm_g)


GRID_W = 64
CTX_LEN = 256
N_MIXERS = 2
N_POOL_GROUPS = 4
POOL_WINDOWS = (2, 4, 8, 16)
POOL_GROUP_DIM = D_MODEL // N_POOL_GROUPS
HEAD_DIM = 128
N_Q_HEADS = D_MODEL // HEAD_DIM
N_KV_HEADS = 2
Q_PER_KV = N_Q_HEADS // N_KV_HEADS
QKV_DIM = (N_Q_HEADS + 2 * N_KV_HEADS) * HEAD_DIM
ROPE_THETA = 10000.0
Q_BLOCK = 128
D_FF = 4 * D_MODEL
N_MOD = 6
EPS = 1e-6
N_POOL_LAYERS = (DEPTH + 1) // 2
N_ATTN_LAYERS = DEPTH // 2


def rms_norm_2(x, g):
    xf = x.astype(jnp.float32)
    y = xf * lax.rsqrt(jnp.mean(xf * xf, axis=-1, keepdims=True) + EPS)
    return (y * g.astype(jnp.float32)).astype(x.dtype)

def ada_mods(cond, w, b):
    m = (jax.nn.silu(cond) @ w + b)[..., None, :]
    return jnp.split(m, N_MOD, axis=-1)

def modulate(h, shift, scale):
    return h * (1.0 + scale) + shift

def pool_mixer(h, w_pool, pool_scale):
    B, L, D = h.shape
    t = jnp.arange(L)
    hf = h.astype(jnp.float32)
    cs = jnp.concatenate([jnp.zeros((B, 1, D), jnp.float32), jnp.cumsum(hf, axis=1)], axis=1)
    outs = []
    for g, w in enumerate(POOL_WINDOWS):
        sl = slice(g * POOL_GROUP_DIM, (g + 1) * POOL_GROUP_DIM)
        lo = jnp.clip(t - w // 2, 0, L)
        hi = jnp.clip(t + w - w // 2, 0, L)
        csg = cs[..., sl]
        cnt = (hi - lo).astype(jnp.float32)[:, None]
        mean = (jnp.take(csg, hi, axis=1) - jnp.take(csg, lo, axis=1)) / cnt
        diff = (mean - hf[..., sl]).astype(h.dtype)
        outs.append(diff @ w_pool[g])
    return jnp.concatenate(outs, axis=-1) * pool_scale

def axial_rope_tables(L):
    rows = L // GRID_W
    row = jnp.broadcast_to(jnp.arange(rows)[:, None], (rows, GRID_W)).reshape(L).astype(jnp.float32)
    col = jnp.broadcast_to(jnp.arange(GRID_W)[None, :], (rows, GRID_W)).reshape(L).astype(jnp.float32)
    half = HEAD_DIM // 2
    inv_freq = jnp.power(jnp.float32(ROPE_THETA), -jnp.arange(0, half, 2, dtype=jnp.float32) / half)
    ang_r = row[:, None] * inv_freq
    ang_c = col[:, None] * inv_freq
    return (jnp.cos(ang_r)[:, None, :], jnp.sin(ang_r)[:, None, :],
            jnp.cos(ang_c)[:, None, :], jnp.sin(ang_c)[:, None, :])

def _rotate(x, cos, sin):
    x1, x2 = jnp.split(x, 2, axis=-1)
    return jnp.concatenate([x1 * cos - x2 * sin, x2 * cos + x1 * sin], axis=-1)

def apply_axial_rope(x, tables):
    cr, sr, cc, sc = tables
    xf = x.astype(jnp.float32)
    half = HEAD_DIM // 2
    out = jnp.concatenate([_rotate(xf[..., :half], cr, sr), _rotate(xf[..., half:], cc, sc)], axis=-1)
    return out.astype(x.dtype)

def qkv_project(h, w_qkv, g_q, g_k):
    B, L, _ = h.shape
    qkv = h @ w_qkv
    q = qkv[..., :N_Q_HEADS * HEAD_DIM].reshape(B, L, N_Q_HEADS, HEAD_DIM)
    k = qkv[..., N_Q_HEADS * HEAD_DIM:(N_Q_HEADS + N_KV_HEADS) * HEAD_DIM].reshape(B, L, N_KV_HEADS, HEAD_DIM)
    v = qkv[..., (N_Q_HEADS + N_KV_HEADS) * HEAD_DIM:].reshape(B, L, N_KV_HEADS, HEAD_DIM)
    return rms_norm_2(q, g_q), rms_norm_2(k, g_k), v

def attend(q, k, v):
    s = jnp.einsum('bqhgd,bkhd->bhgqk', q, k).astype(jnp.float32) * (HEAD_DIM ** -0.5)
    p = jax.nn.softmax(s, axis=-1).astype(v.dtype)
    return jnp.einsum('bhgqk,bkhd->bqhgd', p, v)

def attention_mixer(h_lat, h_ctx, w_qkv, g_q, g_k, w_o, need_ctx_out):
    B, L, D = h_lat.shape
    C = h_ctx.shape[1]
    tables = axial_rope_tables(L)
    q_l, k_l, v_l = qkv_project(h_lat, w_qkv, g_q, g_k)
    q_l = apply_axial_rope(q_l, tables)
    k_l = apply_axial_rope(k_l, tables)
    q_c, k_c, v_c = qkv_project(h_ctx, w_qkv, g_q, g_k)
    k_all = jnp.concatenate([k_c, k_l], axis=1)
    v_all = jnp.concatenate([v_c, v_l], axis=1)
    nb = L // Q_BLOCK
    qb = q_l.reshape(B, nb, Q_BLOCK, N_KV_HEADS, Q_PER_KV, HEAD_DIM).transpose(1, 0, 2, 3, 4, 5)
    o_blocks = lax.map(lambda qblk: attend(qblk, k_all, v_all), qb)
    o_lat = o_blocks.transpose(1, 0, 2, 3, 4, 5).reshape(B, L, D) @ w_o
    o_ctx = None
    if need_ctx_out:
        qc = q_c.reshape(B, C, N_KV_HEADS, Q_PER_KV, HEAD_DIM)
        o_ctx = attend(qc, k_c, v_c).reshape(B, C, D) @ w_o
    return o_lat, o_ctx

def sq_relu_mlp(h, w_in, w_out):
    return jnp.square(jax.nn.relu(h @ w_in)) @ w_out

def second_inputs(seed: int = 0) -> dict:
    key = jax.random.key(seed)
    ks = jax.random.split(key, 20)
    f32 = jnp.float32
    nrm = lambda k, shape: jax.random.normal(k, shape, f32)
    gain = lambda k, shape: 1.0 + 0.05 * nrm(k, shape)
    return {
        'x': nrm(ks[0], (BATCH, SEQ, D_MODEL)),
        'c': nrm(ks[1], (BATCH, D_MODEL)),
        'ctx': nrm(ks[2], (BATCH, CTX_LEN, D_MODEL)),
        'c_ctx': nrm(ks[3], (D_MODEL,)),
        'w_ada': nrm(ks[4], (DEPTH, D_MODEL, N_MOD * D_MODEL)) * (0.5 * D_MODEL ** -0.5),
        'b_ada': 0.01 * nrm(ks[5], (DEPTH, N_MOD * D_MODEL)),
        'g_mix_pre': gain(ks[6], (DEPTH, D_MODEL)),
        'g_mix_post': gain(ks[7], (DEPTH, D_MODEL)),
        'g_mlp_pre': gain(ks[8], (DEPTH, D_MODEL)),
        'g_mlp_post': gain(ks[9], (DEPTH, D_MODEL)),
        'w_pool': nrm(ks[10], (N_POOL_LAYERS, N_POOL_GROUPS, POOL_GROUP_DIM, POOL_GROUP_DIM)) * POOL_GROUP_DIM ** -0.5,
        'pool_scale': 1.0 + 0.1 * nrm(ks[11], (N_POOL_LAYERS, D_MODEL)),
        'w_qkv': nrm(ks[12], (N_ATTN_LAYERS, D_MODEL, QKV_DIM)) * D_MODEL ** -0.5,
        'g_q': gain(ks[13], (N_ATTN_LAYERS, HEAD_DIM)),
        'g_k': gain(ks[14], (N_ATTN_LAYERS, HEAD_DIM)),
        'w_o': nrm(ks[15], (N_ATTN_LAYERS, D_MODEL, D_MODEL)) * D_MODEL ** -0.5,
        'w_mlp_in': nrm(ks[16], (DEPTH, D_MODEL, D_FF)) * D_MODEL ** -0.5,
        'w_mlp_out': nrm(ks[17], (DEPTH, D_FF, D_MODEL)) * D_FF ** -0.5,
    }

def second_block(x, c, ctx, c_ctx, w_ada, b_ada, g_mix_pre, g_mix_post, g_mlp_pre, g_mlp_post,
              w_pool, pool_scale, w_qkv, g_q, g_k, w_o, w_mlp_in, w_mlp_out):
    for i in range(DEPTH):
        last = i == DEPTH - 1
        j = i // N_MIXERS
        sh1, sc1, gt1, sh2, sc2, gt2 = ada_mods(c, w_ada[i], b_ada[i])
        csh1, csc1, cgt1, csh2, csc2, cgt2 = ada_mods(c_ctx, w_ada[i], b_ada[i])
        h_lat = modulate(rms_norm_2(x, g_mix_pre[i]), sh1, sc1)
        h_ctx = modulate(rms_norm_2(ctx, g_mix_pre[i]), csh1, csc1)
        if i % N_MIXERS == 0:
            y_lat = pool_mixer(h_lat, w_pool[j], pool_scale[j])
            y_ctx = None if last else pool_mixer(h_ctx, w_pool[j], pool_scale[j])
        else:
            y_lat, y_ctx = attention_mixer(h_lat, h_ctx, w_qkv[j], g_q[j], g_k[j], w_o[j], not last)
        x = x + gt1 * rms_norm_2(y_lat, g_mix_post[i])
        m_lat = sq_relu_mlp(modulate(rms_norm_2(x, g_mlp_pre[i]), sh2, sc2), w_mlp_in[i], w_mlp_out[i])
        x = x + gt2 * rms_norm_2(m_lat, g_mlp_post[i])
        if not last:
            ctx = ctx + cgt1 * rms_norm_2(y_ctx, g_mix_post[i])
            m_ctx = sq_relu_mlp(modulate(rms_norm_2(ctx, g_mlp_pre[i]), csh2, csc2), w_mlp_in[i], w_mlp_out[i])
            ctx = ctx + cgt2 * rms_norm_2(m_ctx, g_mlp_post[i])
    return x


def setup_inputs(seed=0):
    out = dict(first_inputs(seed))
    for name, value in second_inputs(seed + 1).items():
        if name != "x":
            out[name + "_2"] = value
    return out


def reference(
    x, norm1_g, w_in, ret_norm_g, hgrn_norm_g, w_out, lower_bounds, norm2_g, w_router, w_gate,
    w_up, w_down, final_norm_g, c_2, ctx_2, c_ctx_2, w_ada_2, b_ada_2, g_mix_pre_2,
    g_mix_post_2, g_mlp_pre_2, g_mlp_post_2, w_pool_2, pool_scale_2, w_qkv_2, g_q_2, g_k_2,
    w_o_2, w_mlp_in_2, w_mlp_out_2,
):
    x = first_block(
        x, norm1_g, w_in, ret_norm_g, hgrn_norm_g, w_out, lower_bounds, norm2_g, w_router,
        w_gate, w_up, w_down, final_norm_g,
    )
    return second_block(
        x, c_2, ctx_2, c_ctx_2, w_ada_2, b_ada_2, g_mix_pre_2, g_mix_post_2, g_mlp_pre_2,
        g_mlp_post_2, w_pool_2, pool_scale_2, w_qkv_2, g_q_2, g_k_2, w_o_2, w_mlp_in_2,
        w_mlp_out_2,
    )


_drawn_inputs = setup_inputs


def setup_inputs(seed=0):
    import zlib

    import numpy as np

    out = dict(_drawn_inputs(seed))
    spreads = {}
    factors = {'ret_norm_g': 3.622,
     'hgrn_norm_g': 3.33,
     'lower_bounds': 7.72,
     'norm2_g': 2.814,
     'final_norm_g': 2.946,
     'g_mix_pre_2': 3.313,
     'g_mlp_post_2': 2.847,
     'g_q_2': 8.0,
     'g_k_2': 8.0,
     'g_mix_post_2': 5.041,
     'pool_scale_2': 2.768}
    for name, (base, spread) in spreads.items():
        noise = np.random.default_rng([zlib.crc32(name.encode()), seed]).standard_normal(out[name].shape)
        drawn = base * np.exp(spread * noise) if base else spread * noise
        out[name] = __import__('jax').numpy.asarray(drawn.astype(out[name].dtype))
    for name, factor in factors.items():
        out[name] = (out[name] * factor).astype(out[name].dtype)
    return out
```

```python
from contextlib import ExitStack

import numpy as np

import concourse.bass as bass
from concourse import mybir

ALU = mybir.AluOpType
ACT = mybir.ActivationFunctionType
F32 = mybir.dt.float32
BF16 = mybir.dt.bfloat16
U8 = mybir.dt.uint8
U32 = mybir.dt.uint32
AX = mybir.AxisListType

P = 128
D = 1024
KC = D // P
S = 256
NT = S // P
DEPTH = 2
H4 = 4
W4 = H4 * P
IN_COLS = 9 * W4
NEXP = 16
CAP = 2 * S // NEXP
FF = 1024
DFF = 4096
NMOD = 6
NQ, NKV = 8, 2
EPS = 1e-6
HEAD_SCALE = float(P) ** -0.5
WINDOWS = (2, 4, 8, 16)
GRID_W = 64
SLOT = 4096
RING1, RING2 = 6, 4
LEVELS = (1, 2, 4, 8, 16, 32, 64)

COLS = {}
_n = 0
for _name, _w in (("norm1_g", 16), ("norm2_g", 16), ("ret_g", 8), ("hgrn_g", 8), ("lower", 8),
                  ("b_ada", 96), ("g_mix_pre", 16), ("g_mix_post", 16), ("g_mlp_pre", 16),
                  ("g_mlp_post", 16), ("c", 8), ("c_ctx", 8)):
    COLS[_name] = (_n, _n + _w)
    _n += _w
NCOLS = _n
CONSTS = {}
_n = 0
for _name, _w in (("ident", P), ("cos", NT * P), ("sin", NT * P), ("decay", H4 * 3 * P),
                  ("sel", 2), ("token", NT), ("delta", NEXP)):
    CONSTS[_name] = (_n, _n + _w)
    _n += _w
NCONST = _n

RQ, RK, RV, RG, HQ, HFF, HFB, HI, HG = range(9)
ADA = "ada"


def mixer_items():
    return [RQ, RK, HFF, HFB, HQ, RV, ADA, HI, ADA, ADA, RG, ADA, ADA, HG, ADA, ADA,
            ADA, ADA, ADA, ADA, ADA]


def build_program(nc, x, cols, w_in, w_out, w_router, w_gate, w_up, w_down, final_g, ctx_x, w_ada,
                  w_pool, pool_scale, w_qkv, g_qk, w_o, w_mlp_in, w_mlp_out, consts, masks,
                  bands, rope2, out):
    es = ExitStack()
    at = [16512]
    here = {}

    def place(name, shape, dtype=F32, where=None):
        size = int(np.prod(shape[1:])) * (1 if dtype == U8 else 2 if dtype == BF16 else 4)
        offset = at[0] if where is None else here[where]
        here[name] = offset
        if where is None:
            at[0] += (size + 31) // 32 * 32
        return nc.alloc_sbuf_tensor_at(name, list(shape), dtype, offset=offset)

    ring = place("ring", [P, RING1, SLOT])
    ring_end = at[0]
    ident_all = place("consts_sb", [P, NCONST])
    col = place("cols_sb", [P, NCOLS])
    mods = place("mods", [P, DEPTH, NMOD * KC, 2])
    mod_gain = place("mod_gain", [P, DEPTH, 2, 2, KC])
    cT = place("silu_c", [P, KC, 32])
    ones = place("ones", [P, P])
    lb = place("lower_bound", [P, 3, DEPTH, H4])
    eps = place("eps", [P, 1])
    ssq = place("ssq", [P, 4])
    std = place("std", [P, 4])
    rinv = place("rinv", [P, 4])
    zeros = place("zeros", [P, P], BF16)
    mask = place("mask_sb", [P, len(LEVELS), 2, P // 2], U8)
    h = place("h", [P, NT, D])
    h_at = here["h"]

    first_at = at[0]
    xs = place("xs", [P, NT, D])
    xT = place("xT", [P, KC, S])
    r_at = at[0]
    rot = place("rot", [P, 2, NT, W4])
    RS_ = place("ret_scores", [P, NT, H4, S], where="rot")
    ret_v = place("ret_v", [P, NT, W4])
    ret_gate = place("ret_gate", [P, NT, W4])
    hg_v = place("hgrn_v", [P, NT, W4])
    hg_gate = place("hgrn_gate", [P, NT, W4])
    retT = place("retT", [P, 2, H4, S])
    kdec = place("kdec", [P, 2, H4, S], where="retT")
    hq = place("hgrn_q", [P, H4, S])
    hf = place("hgrn_f", [P, 2, H4, S])
    hk = place("hgrn_k", [P, 2, H4, S])
    hx = place("hgrn_x", [P, 2, H4, S])
    qdec = place("qdec", [P, 2, H4, P])
    rope_t = place("rope_tmp", [P, 2, W4], where="qdec")
    AD = place("hgrn_diag", [P, 2 * H4, P])
    AO = place("hgrn_off", [P, 2, H4, P])
    ada_s = place("ada_rows", [P, 512])
    rstat = place("ret_stat", [P, 3, NT, H4])
    sq = place("square", [P, NT, W4], where="qdec")
    save = at[0]
    at[0] = r_at
    wr = place("router_sb", [P, KC, NEXP])
    logit = place("logit", [P, NT, NEXP])
    aff = place("affinity", [P, NT, NEXP])
    rstats = place("router_stat", [P, NT, 4])
    affT = place("affinityT", [NEXP, 2, S])
    top = place("top_gate", [NEXP, CAP])
    topi = place("top_index", [NEXP, CAP], U32)
    topf = place("top_index_f", [NEXP, CAP])
    spread = place("spread", [NEXP, 2, NEXP, CAP])
    onehot = place("onehot", [P, NT, NEXP * CAP])
    gated = place("gated", [P, NT, NEXP * CAP])
    gsel = place("gate_sel", [P, NT, 4, CAP])
    GT = place("gate_T", [P, S])
    xeT = place("xeT", [P, KC, CAP])
    silu_g = place("silu_g", [P, 256])
    hidE = place("hid_e", [P, 256])
    hidT = place("hid_T", [P, 2, P])
    Y = place("y_e", [P, D])
    gfin = place("final_g_row", [P, D])
    assert at[0] <= save
    top_of_first = save

    at[0] = h_at
    x4 = place("x4", [P, 2 * NT, D])
    at[0] = max(at[0], first_at)
    ys = place("y2", [P, 2 * NT, D])
    xs2 = place("xs2", [P, 2 * NT, D])
    xT2 = place("xT2", [P, KC, 2 * S])
    band = place("band_sb", [P, 4, NT, S])
    rope_c = place("rope2_sb", [P, 2, NT, P])
    gqk = place("gqk_sb", [P, 2, P])
    rope_g = place("rope_gained", [P, 2, 2, NT, P])
    gate_col = place("gate_col", [P, KC])
    kv = place("kv", [P, 2 * NT, 2, 2 * P])
    kT2 = place("kT2", [P, NKV, 2 * S])
    soft = place("softmax_stat", [P, 4, 4])
    qst = place("q_stat", [P, 3, NT * NQ])
    kst = place("k_stat", [P, 3, 2 * NT * NKV])
    assert at[0] <= 229344, at[0]
    end = at[0]
    at[0] = here["ring"] + RING2 * SLOT * 4
    hid = place("hid2", [P, 2, 4, 2 * S])
    rows = place("gate_rows", [P, 3, D])
    dg = place("diag", [P, KC, P])
    assert at[0] <= ring_end
    diffT = place("diffT", [P, KC, 2 * S], where="hid2")
    qr = place("q_rot", [P, NT, D], where="y2")
    q_raw = place("q_raw", [P, NT, D], where="hid2")
    at[0] = here["y2"] + NT * D * 4
    q_tmp = place("q_tmp", [P, 2, D])
    at[0] = here["xs2"]
    qT2 = place("qT2", [P, NQ, S])
    pr = place("prob", [P, 2, 2 * S])
    prT = place("probT", [P, 4, S])
    assert at[0] <= here["xT2"]
    oT = place("oT", [P, NQ, S], where="hid2")

    psum = [es.enter_context(nc.psum_tensor(f"bank{i}", [P, 512], F32)) for i in range(8)]
    sems = {}

    def S_(name):
        if name not in sems:
            sems[name] = es.enter_context(nc.semaphore(name))
        return sems[name]

    landed = [S_(f"landed{i}") for i in range(RING1)]
    weights_used = S_("weights_used")
    bank_full = [S_(f"bank_full{i}") for i in range(8)]
    bank_free = [S_(f"bank_free{i}") for i in range(8)]

    def C(name, i=None, n=1):
        a, b = COLS[name]
        return col[:, a:b] if i is None else col[:, a + i:a + i + n]

    def K(name):
        a, b = CONSTS[name]
        return ident_all[:, a:b]

    ident = K("ident")

    items, count = {}, [0, [0] * RING1]

    def item(name, slot, dmas):
        count[1][slot] += 16 * dmas
        items[name] = (slot, count[0], count[1][slot])
        count[0] += 1

    slot = 0
    for layer in range(DEPTH):
        for n, kind in enumerate(mixer_items()):
            item(("mix", layer, n), slot, 1)
            slot = (slot + 1) % RING1
        for n in range(2):
            item(("w_out", layer, n), slot, 1)
            slot = (slot + 1) % RING1
        for e in range(NEXP):
            for n in range(6):
                item(("moe", layer, e, n), slot, 2 if n < 4 else 1)
                slot = (slot + 1) % RING1
    assert slot == 4
    slot = 0
    for layer in range(DEPTH):
        for n in range(1 if layer == 0 else 5):
            item(("mix2", layer, n), slot, 1)
            slot = (slot + 1) % RING2
        for n in range(16):
            item(("mlp", layer, n), slot, 1)
            slot = (slot + 1) % RING2

    def wait_landed(pe, name):
        slot, _, value = items[name]
        pe.wait_ge(landed[slot], value)
        return ring[:, slot, :]

    filled, frees, where_is, read_by = [0] * 8, [0] * 8, {}, {}

    def take(pe, name, bank, readers=1):
        if frees[bank]:
            pe.wait_ge(bank_free[bank], frees[bank])
        frees[bank] += readers
        read_by[name] = (bank_free[bank], frees[bank])
        where_is[name] = (bank, None, None)
        return psum[bank]

    def fill(ins, name):
        bank = where_is[name][0]
        filled[bank] += 1
        where_is[name] = (bank, bank_full[bank], filled[bank])
        ins.then_inc(bank_full[bank], 1)

    def fill_and_release(ins, name, item_name):
        where_is[name] = (where_is[name][0], weights_used, items[item_name][1] + 1)
        ins.then_inc(weights_used, 1)

    def full(eng, name):
        bank, sem, value = where_is[name]
        eng.wait_ge(sem, value)
        return psum[bank]

    def freed(eng, name):
        eng.wait_ge(*read_by[name])

    def free(ins, name):
        ins.then_inc(bank_free[where_is[name][0]], 1)

    class InTurn:

        def __init__(self, eng, step_name):
            self.eng, self.step, self.mine, self.totals = eng, S_(step_name), None, {}

        def __call__(self, op):
            def run(*args, **kw):
                assert self.mine != "none", "the instruction before signals nothing"
                if self.mine:
                    self.eng.wait_ge(*self.mine)
                self.ins, self.mine = op(*args, **kw), "none"
                return self
            return run

        def then_inc(self, sem, n, value=None):
            self.ins.then_inc(sem, n)
            self.totals[id(sem)] = self.totals.get(id(sem), 0) + n
            self.mine = (sem, value or self.totals[id(sem)])

        def tick(self, _=None):
            self.then_inc(self.step, 1)

        def free(self, _, name):
            self.then_inc(read_by[name][0], 1, read_by[name][1])

    units = [(m, d) for m in LEVELS for d in range(2)] + [(P, 0), (P, 1)]
    moe_base = [items[("moe", l, 0, 0)][1] for l in range(DEPTH)]
    mlp_base = [items[("mlp", l, 0)][1] for l in range(DEPTH)]
    hid_done, out_done = [0, 4 * 8], [0, 8 * 8]

    block = es.enter_context(nc.Block())

    @block.tensor
    def _(pe):
        mm, turn = nc.tensor.matmul, nc.tensor.transpose
        turned = [None]

        def transposes(tag, src, ready):
            for t in range(NT):
                ready(t)
                for b in range(4):
                    ps = take(pe, (tag, b), 4 + b) if t == 0 else psum[4 + b]
                    for c in (2 * b, 2 * b + 1):
                        at_ = (c % 2) * S + t * P
                        ins = turn(ps[:, at_:at_ + P], src(t)[:, c * P:(c + 1) * P], ident)
                    if t == NT - 1:
                        fill(ins, (tag, b))
            turned[0] = tag

        def wait_turned(c=KC - 1):
            freed(pe, (turned[0], c // 2))

        def rows_ready(name):
            seen = [0]

            def ready(t):
                seen[0] += 1
                pe.wait_ge(S_(name), seen[0])
            return ready

        xs_ready, xs2_ready = rows_ready("xs_ready"), rows_ready("xs2_ready")

        def ada_item(layer, l_item, n, tag):
            w = wait_landed(pe, l_item).rearrange("p (c n) -> p c n", c=KC)
            if n == 0 and layer == 0:
                pe.wait_ge(S_("silu_c_ready"), 2)
            ps = take(pe, tag, 6)
            for k in range(2):
                for g in range(4):
                    ins = mm(ps[32 * g:32 * g + 32, :], cT[:, 2 * g + k, :], w[:, 2 * g + k, :],
                             start=k == 0, stop=k == 1)
            fill_and_release(ins, tag, l_item)

        def ada_columns(layer, n, tag):
            freed(pe, ("ada", layer, n))
            ps = take(pe, tag, 7)
            for j in range(4):
                ins = mm(ps[:, 2 * j:2 * j + 2], ada_s[:, j * P:(j + 1) * P], K("sel"),
                         start=True, stop=True)
            fill(ins, tag)

        pe.wait_ge(S_("consts"), 16)
        pe.wait_ge(S_("ones_ready"), 1)

        for l in range(DEPTH):
            transposes(("x1", l), lambda t: xs[:, t, :], xs_ready)
            proj_bank = [0]

            def take_proj(name, readers=1):
                b = proj_bank[0]
                proj_bank[0] = (b + 1) % 4
                return take(pe, name, b, readers)

            def project_rows(n, kind, t):
                it = ("mix", l, n)
                w = wait_landed(pe, it).rearrange("p (c n) -> p c n", c=KC)
                name = ("proj", l, kind, t)
                ps = take_proj(name)
                for c in range(KC):
                    if n == 0 and t == 0:
                        wait_turned(c)
                    ins = mm(ps[:, :], xT[:, c, t * P:(t + 1) * P], w[:, c, :], start=c == 0,
                             stop=c == KC - 1)
                if t == NT - 1:
                    fill_and_release(ins, name, it)
                else:
                    fill(ins, name)

            def project_features(n, kind):
                it = ("mix", l, n)
                w = wait_landed(pe, it).rearrange("p (c n) -> p c n", c=KC)
                for pair in range(2):
                    name = ("proj", l, kind, pair)
                    ps = take_proj(name)
                    for head in (2 * pair, 2 * pair + 1):
                        for c in range(KC):
                            ins = mm(ps[:, (head % 2) * S:(head % 2 + 1) * S],
                                     w[:, c, head * P:(head + 1) * P], xT[:, c, :],
                                     start=c == 0, stop=c == KC - 1)
                    if pair == 1:
                        fill_and_release(ins, name, it)
                    else:
                        fill(ins, name)

            def turn_ret(i):
                pe.wait_ge(S_("rot_ready"), (2 * l + i) * NT + NT)
                for pair in range(2):
                    name = ("retT", l, i, pair)
                    ps = take(pe, name, 4 + 2 * i + pair)
                    for head in (2 * pair, 2 * pair + 1):
                        for t in range(NT):
                            at_ = (head % 2) * S + t * P
                            ins = turn(ps[:, at_:at_ + P], rot[:, i, t, head * P:(head + 1) * P],
                                       ident)
                    fill(ins, name)

            def ret_scores():
                for i in range(2):
                    for pair in range(2):
                        freed(pe, ("retT", l, i, pair))
                for head in range(H4):
                    name = ("ret_s", l, head)
                    ps = take(pe, name, 4 + head)
                    for t in range(NT):
                        ins = mm(ps[:, t * S:(t + 1) * S], retT[:, 1, head, t * P:(t + 1) * P],
                                 retT[:, 0, head, :], start=True, stop=True)
                    fill(ins, name)

            def hgrn_same():
                pe.wait_ge(S_("k_sum_ready"), l + 1)
                for pair in range(2):
                    freed(pe, ("proj", l, HQ, pair))
                for t in range(2):
                    name = ("same", l, t)
                    ps = take(pe, name, 4 + t)
                    for j in range(H4):
                        head, tile = (4 * t + j) // 2, j % 2
                        part = slice(tile * P, (tile + 1) * P)
                        ins = mm(ps[:, j * P:(j + 1) * P], hx[:, 0, head, part], hq[:, head, part],
                                 start=True, stop=True)
                    fill(ins, name)

            def hgrn_unit(u):
                m, d = units[u]
                name = ("unit", l, u)
                pe.wait_ge(S_("level_ready"), len(units) * l + u + 1)
                ps = take(pe, name, 4 + u % 2)
                for head in range(H4):
                    if m == P:
                        ins = mm(ps[:, head * P:(head + 1) * P],
                                 kdec[:, d, head, d * P:(d + 1) * P], qdec[:, d, head, :],
                                 start=True, stop=True)
                        continue
                    for t in range(NT):
                        j = 2 * head + t
                        key = (hk if m == 1 else kdec)[:, d, head, t * P:(t + 1) * P]
                        ins = mm(ps[:, j * 64:(j + 1) * 64], key,
                                 qdec[:, d, head, t * 64:(t + 1) * 64], start=True, stop=True)
                fill(ins, name)

            def ret_out():
                for head in range(H4):
                    freed(pe, ("ret_s", l, head))
                for t in range(NT):
                    freed(pe, ("proj", l, RV, t))
                for t in range(NT):
                    name = ("ret_o", l, t)
                    ps = take_proj(name)
                    for head in range(H4):
                        part = slice(head * P, (head + 1) * P)
                        for j in range(NT):
                            ins = mm(ps[:, part], RS_[:, j, head, t * P:(t + 1) * P],
                                     ret_v[:, j, part], start=j == 0, stop=j == NT - 1)
                    fill(ins, name)

            def hgrn_out():
                for u in range(len(units) - 4, len(units)):
                    freed(pe, ("unit", l, u))
                for t in range(NT):
                    freed(pe, ("proj", l, HI, t))
                for t in range(NT):
                    name = ("hgrn_o", l, t)
                    ps = take_proj(name)
                    for head in range(H4):
                        part = slice(head * P, (head + 1) * P)
                        mm(ps[:, part], AD[:, 2 * head + t, :], hg_v[:, t, part],
                           start=True, stop=False)
                        ins = mm(ps[:, part], AO[:, 1 - t, head, :], hg_v[:, 1 - t, part],
                                 start=False, stop=True)
                    fill(ins, name)

            fill_u, ada_n, pending = [0], [0], []

            def some_units(n):
                for _ in range(n):
                    if fill_u[0] < len(units):
                        hgrn_unit(fill_u[0])
                        fill_u[0] += 1

            for n, kind in enumerate(mixer_items()):
                if kind == ADA:
                    if pending:
                        ada_columns(l, pending[0], ("ada_c", l, pending.pop()))
                    ada_item(l, ("mix", l, n), ada_n[0], ("ada", l, ada_n[0]))
                    pending.append(ada_n[0])
                    ada_n[0] += 1
                elif kind in (HQ, HFF, HFB):
                    project_features(n, kind)
                    if kind == HFF:
                        turn_ret(0)
                    elif kind == HFB:
                        turn_ret(1)
                    else:
                        ret_scores()
                        hgrn_same()
                else:
                    for t in range(NT):
                        project_rows(n, kind, t)
                        if n > 4:
                            some_units(2)
                if kind == HG:
                    some_units(len(units))
                    ret_out()
                    hgrn_out()
            ada_columns(l, pending[0], ("ada_c", l, pending.pop()))

            def mix_ready(t):
                freed(pe, ("ret_o", l, t))
                freed(pe, ("hgrn_o", l, t))

            transposes(("mix", l), lambda t: xs[:, t, :], mix_ready)
            for n in range(2):
                it = ("w_out", l, n)
                w = wait_landed(pe, it).rearrange("p (c n) -> p c n", c=KC)
                for t in range(NT):
                    name = ("w_out", l, n, t)
                    ps = take(pe, name, 2 * n + t)
                    for c in range(KC):
                        if n == 0 and t == 0:
                            wait_turned(c)
                        ins = mm(ps[:, :], xT[:, c, t * P:(t + 1) * P], w[:, c, :],
                                 start=c == 0, stop=c == KC - 1)
                    if t == NT - 1:
                        fill_and_release(ins, name, it)
                    else:
                        fill(ins, name)

            transposes(("x2", l), lambda t: xs[:, t, :], xs_ready)
            for c in range(0, KC, 2):
                wait_turned(c)
            name = ("logit", l)
            ps = take(pe, name, 4)
            pe.wait_ge(S_("router_landed"), 16 * (l + 1))
            for t in range(NT):
                for c in range(KC):
                    ins = mm(ps[:, t * NEXP:(t + 1) * NEXP], xT[:, c, t * P:(t + 1) * P],
                             wr[:, c, :], start=c == 0, stop=c == KC - 1)
            fill(ins, name)
            pe.wait_ge(S_("affinity_ready"), NT * (l + 1))
            name = ("affT", l)
            ps = take(pe, name, 5)
            for t in range(NT):
                ins = turn(ps[0:NEXP, t * P:(t + 1) * P], aff[:, t, :], ident)
            fill(ins, name)
            for b in range(4):
                ps = take(pe, ("moe", l, b), b)
                mm(ps[:, :], zeros[:, :], zeros[:, :].unsqueeze(1).broadcast_to([P, 4, P]),
                   start=True, stop=False,
                   skip_group_check=True)
            for i in range(2):
                pe.wait_ge(S_("spread_ready"), 2 * l + i + 1)
                name = ("spread", l, i)
                ps = take(pe, name, 6 + i, 1)
                ins = mm(ps[:, :], ones[0:NEXP, :], spread[:, i, :, :].rearrange("e a b -> e (a b)"),
                         start=True, stop=True)
                fill(ins, name)
            for b in range(4, 8):
                pe.wait_ge(bank_free[b], frees[b])
            start_slot = items[("moe", l, 0, 0)][0]
            land = [items[("moe", l, 0, n)] for n in range(6)]
            with pe.Fori(0, NEXP) as e:
                done = l * NEXP + e
                pe.wait_ge(S_("gate_sel_ready"), done + 1)
                for t in range(NT):
                    ins = turn(psum[5][:, t * P:(t + 1) * P],
                               gsel[:, t, :, :].rearrange("p a b -> p (a b)"), ident)
                ins.then_inc(S_("gate_T_full"), 1)
                for c in range(KC):
                    for t in range(NT):
                        ins = mm(psum[7][:, c * CAP:(c + 1) * CAP],
                                 xs[:, t, c * P:(c + 1) * P],
                                 onehot[:, t, bass.ds(e * CAP, CAP)], start=t == 0,
                                 stop=t == NT - 1, skip_group_check=True)
                ins.then_inc(S_("gathered"), 1)
                pe.wait_ge(S_("xeT_ready"), done + 1)
                for n in range(4):
                    sl, _, value = land[n]
                    pe.wait_ge(landed[sl], value + 32 * e)
                    w = ring[:, sl, :].rearrange("p (k a f) -> p k a f", k=2, a=2)
                    for k in range(2):
                        for g in range(4):
                            ins = mm(psum[4][32 * g:32 * g + 32, :], xeT[:, 2 * n + k, :],
                                     w[:, k, :, 256 * g:256 * (g + 1)],
                                     start=n == 0 and k == 0, stop=n == 3 and k == 1,
                                     skip_group_check=True)
                    ins.then_inc(weights_used, 1)
                pe.wait_ge(S_("gate_T_ready"), done + 1)
                pe.wait_ge(S_("hid_e_ready"), done + 1)
                for j in range(2):
                    ins = turn(psum[6][:, j * P:(j + 1) * P], hidE[:, j * P:(j + 1) * P], ident)
                ins.then_inc(S_("hid_T_full"), 1)
                pe.wait_ge(S_("hid_T_ready"), done + 1)
                for n in range(2):
                    sl, _, value = land[4 + n]
                    pe.wait_ge(landed[sl], value + 16 * e)
                    w = ring[:, sl, :].rearrange("p (g d) -> p g d", g=4)
                    for half in range(2):
                        for g in range(4):
                            ins = mm(psum[5 + half][32 * g:32 * g + 32, :],
                                     hidT[:, n, 32 * g:32 * g + 32],
                                     w[:, g, half * 512:(half + 1) * 512],
                                     start=n == 0, stop=n == 1, skip_group_check=True)
                    ins.then_inc(weights_used, 1)
                pe.wait_ge(S_("y_left_ready"), done + 1)
                pe.wait_ge(S_("y_right_ready"), done + 1)
                for half in range(2):
                    for t in range(NT):
                        ins = mm(psum[2 * half + t][:, :], GT[:, t * P:(t + 1) * P],
                                 Y[:, half * 512:(half + 1) * 512], start=False, stop=False,
                                 skip_group_check=True)
                ins.then_inc(S_("scattered"), 1)

        def post_rows(tag, n):
            for i in range(n):
                pe.wait_ge(S_("diag_ready"), rows_done[0] + 1)
                for half in range(2):
                    name = (tag, i, half)
                    ps = take(pe, name, 2 * (i % 2) + half)
                    ins = mm(ps[:, :], ones[:, :],
                             dg[:, 4 * half:4 * half + 4, :].rearrange("p a b -> p (a b)"),
                             start=True, stop=True)
                    fill(ins, name)
                rows_done[0] += 1

        rows_done = [0]

        def mlp(l, streams):
            T = streams * S
            tiles = streams * NT
            first = [items[("mlp", l, n)] for n in range(4)]
            base_h, base_o = hid_done[l], out_done[l]
            with pe.Fori(0, 4) as i:
                for b in range(2):
                    sl, _, value = first[b]
                    pe.wait_ge(landed[sl], value + 16 * i)
                    w = ring[:, sl, :].rearrange("p (c n) -> p c n", c=KC)
                    for j in range(4):
                        k = 4 * b + j
                        pe.wait_ge(S_("relu_ready"), i * 8 + (base_h + k + 1))
                        for c in range(KC):
                            ins = mm(psum[k % 2][:, 0:T], w[:, c, j * P:(j + 1) * P],
                                     xT2[:, c, 0:T], start=c == 0, stop=c == KC - 1,
                                     skip_group_check=True)
                        if j < 3:
                            ins.then_inc(S_("hidden_full"), 1)
                        else:
                            ins.then_inc(weights_used, 1)
                for b in range(2):
                    sl, _, value = first[2 + b]
                    pe.wait_ge(landed[sl], value + 16 * i)
                    w = ring[:, sl, :].rearrange("p (c n) -> p c n", c=4)
                    pe.wait_ge(S_("hidden_ready"), i * 8 + (base_h + 4 * (b + 1)))
                    for t in range(tiles):
                        for half in range(2):
                            k = (b * tiles + t) * 2 + half
                            pe.wait_ge(S_("out_added"), i * (4 * tiles) + (base_o + k + 5))
                            for c in range(4):
                                ins = mm(psum[2 + k % 4][:, :], hid[:, b, c, t * P:(t + 1) * P],
                                         w[:, c, half * 512:(half + 1) * 512],
                                         start=c == 0, stop=c == 3, skip_group_check=True)
                            if (t, half) == (tiles - 1, 1):
                                ins.then_inc(weights_used, 1)
                            else:
                                ins.then_inc(S_("out_full"), 1)

        pe.wait_ge(S_("bands_landed"), 16)
        for s in range(2):
            for t in range(NT):
                xs2_ready(t)
            for c in range(KC):
                name = (("pool_d", s), c // 2)
                ps = take(pe, name, 4 + c // 2) if c % 2 == 0 else ps
                for t in range(NT):
                    ins = mm(ps[:, (c % 2) * S:(c % 2 + 1) * S],
                             xs2[:, 2 * s + t, c * P:(c + 1) * P], band[:, c // 2, t, :],
                             start=t == 0, stop=t == NT - 1)
                if c % 2:
                    fill(ins, name)
        w = wait_landed(pe, ("mix2", 0, 0))[:, 0:2048].rearrange("p (g k e) -> p g k e", g=4, k=2)
        for t in range(2 * NT):
            for b in range(4):
                freed(pe, (("pool_d", t // 2), b))
            for half in range(2):
                name = ("pool_y", t, half)
                ps = take(pe, name, 2 * (t % 2) + half)
                for g in (2 * half, 2 * half + 1):
                    for k in range(2):
                        ins = mm(ps[:, (g % 2) * S:(g % 2 + 1) * S],
                                 diffT[:, 2 * g + k, t * P:(t + 1) * P], w[:, g, k, :],
                                 start=k == 0, stop=k == 1)
                if (t, half) == (2 * NT - 1, 1):
                    fill_and_release(ins, name, ("mix2", 0, 0))
                else:
                    fill(ins, name)
        post_rows("rows_mix0", 2)
        for s in range(2):
            transposes(("xm0", s), lambda t, s=s: xs2[:, 2 * s + t, :], xs2_ready)
        for b in range(8):
            pe.wait_ge(bank_free[b], frees[b])
        mlp(0, 2)
        pe.wait_ge(S_("out_added"), out_done[1] + 8)
        post_rows("rows_mlp0", 2)

        for s in range(2):
            transposes(("xa", s), lambda t, s=s: xs2[:, 2 * s + t, :], xs2_ready)
        for b in range(4):
            wait_turned(2 * b)
        for n in range(2):
            it = ("mix2", 1, n)
            w = wait_landed(pe, it).rearrange("p (c n) -> p c n", c=KC)
            for t in range(NT):
                name = ("q", n, t)
                ps = take(pe, name, 2 * n + t)
                for c in range(KC):
                    ins = mm(ps[:, :], xT2[:, c, t * P:(t + 1) * P], w[:, c, :], start=c == 0,
                             stop=c == KC - 1)
                if t == 1:
                    fill_and_release(ins, name, it)
                else:
                    fill(ins, name)
        it = ("mix2", 1, 2)
        w = wait_landed(pe, it).rearrange("p (c n) -> p c n", c=KC)
        for t in range(2 * NT):
            name = ("kv", t)
            ps = take(pe, name, 4 + t)
            for c in range(KC):
                ins = mm(ps[:, :], xT2[:, c, t * P:(t + 1) * P], w[:, c, :], start=c == 0,
                         stop=c == KC - 1)
            if t == 3:
                fill_and_release(ins, name, it)
            else:
                fill(ins, name)
        pe.wait_ge(S_("q_rot_ready"), NT)
        for pair in range(4):
            name = ("qT", pair)
            ps = take(pe, name, pair)
            for head in (2 * pair, 2 * pair + 1):
                for t in range(NT):
                    at_ = (head % 2) * S + t * P
                    ins = turn(ps[:, at_:at_ + P], qr[:, t, head * P:(head + 1) * P], ident)
            fill(ins, name)
        pe.wait_ge(S_("k_rot_ready"), 2 * NT)
        for g in range(NKV):
            name = ("kT", g)
            ps = take(pe, name, 4 + g)
            for t in range(2 * NT):
                ins = turn(ps[:, t * P:(t + 1) * P], kv[:, t, 0, g * P:(g + 1) * P], ident)
            fill(ins, name)
        for pair in range(4):
            freed(pe, ("qT", pair))
        for g in range(NKV):
            freed(pe, ("kT", g))

        def scores(u):
            head, t = divmod(u, NT)
            name = ("s", u)
            ps = take(pe, name, u % 2)
            ins = mm(ps[:, :], qT2[:, head, t * P:(t + 1) * P], kT2[:, head // 4, :],
                     start=True, stop=True)
            fill(ins, name)

        def turn_probs(u):
            name = ("pT", u)
            pe.wait_ge(S_("prob_ready"), u + 1)
            ps = take(pe, name, 2 + u % 2)
            for j in range(4):
                ins = turn(ps[:, j * P:(j + 1) * P], pr[:, u % 2, j * P:(j + 1) * P], ident)
            fill(ins, name)

        def values(head):
            name = ("o", head)
            freed(pe, ("pT", 2 * head))
            freed(pe, ("pT", 2 * head + 1))
            ps = take(pe, name, 4 + head % 2)
            g = head // 4
            for j in range(4):
                ins = mm(ps[:, 0:S], kv[:, j, 1, g * P:(g + 1) * P], prT[:, j, :],
                         start=j == 0, stop=j == 3)
            fill(ins, name)

        scores(0)
        for u in range(NQ * NT):
            if u + 1 < NQ * NT:
                scores(u + 1)
            turn_probs(u)
            if u % 2:
                values(u // 2)
        freed(pe, ("o", NQ - 2))
        freed(pe, ("o", NQ - 1))
        for n in range(2):
            it = ("mix2", 1, 3 + n)
            w = wait_landed(pe, it).rearrange("p (c n) -> p c n", c=KC)
            for t in range(NT):
                name = ("wo", n, t)
                ps = take(pe, name, 2 * n + t)
                for c in range(KC):
                    ins = mm(ps[:, :], oT[:, c, t * P:(t + 1) * P], w[:, c, :], start=c == 0,
                             stop=c == KC - 1)
                if t == 1:
                    fill_and_release(ins, name, it)
                else:
                    fill(ins, name)
        post_rows("rows_mix1", 1)
        transposes(("xm1", 0), lambda t: xs2[:, t, :], xs2_ready)
        for b in range(8):
            pe.wait_ge(bank_free[b], frees[b])
        mlp(1, 1)
        pe.wait_ge(S_("out_added"), out_done[1] + 32 + 8)
        post_rows("rows_mlp1", 1)

    @block.scalar
    def _(act):
        turn = InTurn(act, "act_step")
        raw = nc.scalar.activation
        f, step, free = turn(raw), turn.tick, turn.free
        seen = {}

        def expect(name, k=1):
            seen[name] = seen.get(name, 0) + k
            act.wait_ge(S_(name), seen[name])

        def norm_stats(tiles, ready, src, junk, width=D, first=0):
            for t in range(tiles):
                ready(t)
                step(f(junk(t), src(t), ACT.Square, accum_out=ssq[:, first + t:first + t + 1]))
            cols_ = slice(first, first + tiles)
            f(std[:, cols_], ssq[:, cols_], ACT.Sqrt, bias=eps[:, :],
              scale=1.0 / width).then_inc(S_("std_ready"), 1)

        def odd_chunks(tag, out, gain, shift=None):
            for b in (1, 3):
                ps = full(act, (tag, b))
                for c in (2 * b, 2 * b + 1):
                    kw = {} if shift is None else {"bias": shift(c)}
                    at_ = (c % 2) * S
                    ins = f(out(c), ps[:, at_:at_ + S], ACT.Identity, scale=gain(c), **kw)
                    if c % 2 == 0:
                        step(ins)
                free(ins, (tag, b))

        act.dma_start(ident_all[:, :], consts).then_inc(S_("consts"), 16)
        act.dma_start(col[:, :], cols).then_inc(S_("cols"), 16)
        act.dma_start(AD[:, :, :].rearrange("p a b -> p (a b)")[:, 0:len(LEVELS) * P],
                      masks).then_inc(S_("masks"), 16)
        act.wait_ge(S_("ones_ready"), 1)
        act.wait_ge(S_("cols"), 16)
        expect("lower_shifted")
        f(lb[:, 2, :, :], lb[:, 2, :, :], ACT.Exp).then_inc(S_("lower_exp"), 1)
        for i, name in enumerate(("c", "c_ctx")):
            f(cT[:, :, i], C(name), ACT.Silu).then_inc(S_("silu_c_ready"), 1)

        def x_tile_ready(l):
            def ready(t):
                if l == 0:
                    act.wait_ge(S_("x_landed"), 16)
                else:
                    for half in range(2):
                        freed(act, ("moe", l - 1, 2 * half + t))
            return ready

        for l in range(DEPTH):
            norm_stats(NT, x_tile_ready(l), lambda t: h[:, t, :], lambda t: xs[:, t, :])
            odd_chunks(("x1", l), lambda c: xT[:, c, :], lambda c: C("norm1_g", KC * l + c))
            for d, kind in enumerate((HFF, HFB)):
                for pair in range(2):
                    name = ("proj", l, kind, pair)
                    ps = full(act, name)
                    part = slice(2 * pair, 2 * pair + 2)
                    z = ps[:, :].rearrange("p (a t) -> p a t", a=2)
                    step(f(hf[:, d, part, :], z, ACT.Sigmoid))
                    free(f(hk[:, d, part, :], z, ACT.Sigmoid, scale=-1.0), name)
                if l == 0 and d == 0:
                    expect("lower_ready")
                for head in range(H4):
                    step(f(hf[:, d, head, :], hf[:, d, head, :], ACT.Identity,
                           scale=lb[:, 1, l, head:head + 1], bias=lb[:, 0, l, head:head + 1]))
                    ins = f(hk[:, d, head, :], hk[:, d, head, :], ACT.Identity,
                            scale=lb[:, 2, l, head:head + 1])
                    if head < H4 - 1:
                        step(ins)
                ins.then_inc(S_("forget_ready"), 1)
                for pair in range(2):
                    name = ("retT", l, d, pair)
                    ps = full(act, name)
                    free(f(retT[:, d, 2 * pair:2 * pair + 2, :],
                           ps[:, :].rearrange("p (a t) -> p a t", a=2), ACT.Copy), name)
            for pair in range(2):
                name = ("proj", l, HQ, pair)
                ps = full(act, name)
                free(f(hq[:, 2 * pair:2 * pair + 2, :],
                       ps[:, :].rearrange("p (a t) -> p a t", a=2), ACT.Silu), name)
            act.wait_ge(S_("masks_ready"), 1)
            for t in range(2):
                name = ("same", l, t)
                ps = full(act, name)
                free(f(AD[:, 4 * t:4 * t + 4, :], ps[:, :].rearrange("p (a t) -> p a t", a=4),
                       ACT.Copy), name)
            where = {RV: ret_v, HI: hg_v, RG: ret_gate, HG: hg_gate}
            u, ada_n = 0, 0
            for n, kind in enumerate(mixer_items()):
                if kind == ADA:
                    name = ("ada", l, ada_n)
                    ps = full(act, name)
                    free(f(ada_s[:, :], ps[:, :], ACT.Copy), name)
                    ada_n += 1
                elif kind in where:
                    for t in range(NT):
                        name = ("proj", l, kind, t)
                        ps = full(act, name)
                        func = ACT.Silu if kind in (RG, HG) else ACT.Copy
                        free(f(where[kind][:, t, :], ps[:, :], func), name)
                        for _ in range(2):
                            if units[u][0] == P:
                                name = ("unit", l, u)
                                ps = full(act, name)
                                free(f(AO[:, units[u][1], :, :],
                                       ps[:, :].rearrange("p (a t) -> p a t", a=H4),
                                       ACT.Copy), name)
                            u += 1
                if kind == HG:
                    for t in range(NT):
                        name = ("ret_o", l, t)
                        ps = full(act, name)
                        f(sq[:, t, :], ps[:, :], ACT.Square).then_inc(S_("ret_sq_ready"), 1)
                    for t in range(NT):
                        name = ("hgrn_o", l, t)
                        ps = full(act, name)
                        step(f(xs[:, t, W4:D], ps[:, :], ACT.Square,
                               accum_out=ssq[:, t:t + 1]))
                    f(std[:, 0:NT], ssq[:, 0:NT], ACT.Sqrt, bias=eps[:, :],
                      scale=1.0 / W4).then_inc(S_("std_ready"), 1)
                    expect("ret_sum_ready")
                    f(rstat[:, 1, :, :], rstat[:, 0, :, :], ACT.Sqrt, bias=eps[:, :],
                      scale=1.0 / P).then_inc(S_("ret_std_ready"), 1)

            def mix_gain(c):
                return C("ret_g", H4 * l + c) if c < H4 else C("hgrn_g", H4 * l + c - H4)

            odd_chunks(("mix", l), lambda c: xT[:, c, :], mix_gain)

            def out_ready(t):
                for n in range(2):
                    freed(act, ("w_out", l, n, t))

            norm_stats(NT, out_ready, lambda t: h[:, t, :], lambda t: xs[:, t, :])
            odd_chunks(("x2", l), lambda c: xT[:, c, :], lambda c: C("norm2_g", KC * l + c))
            expect("router_max_ready")
            name = ("logit", l)
            ps = full(act, name)
            for t in range(NT):
                ins = f(logit[:, t, :], ps[:, t * NEXP:(t + 1) * NEXP], ACT.Exp,
                        bias=rstats[:, t, 1:2], accum_out=rstats[:, t, 2:3])
                if t == 0:
                    step(ins)
            free(ins, name)
            with act.Fori(0, NEXP) as e:
                done = l * NEXP + e
                act.wait_ge(S_("gate_T_full"), done + 2)
                act.wait_ge(S_("scattered"), done + 1)
                raw(GT[:, :], psum[5][:, 0:S], ACT.Copy).then_inc(S_("gate_T_ready"), 1)
                act.wait_ge(weights_used, 6 * e + (moe_base[l] + 4))
                raw(silu_g[:, :], psum[4][:, 0:256], ACT.Silu).then_inc(S_("silu_g_ready"), 1)
                act.wait_ge(S_("hid_T_full"), done + 1)
                raw(hidT[:, :, :], psum[6][:, 0:S].rearrange("p (a b) -> p a b", a=2),
                  ACT.Copy).then_inc(S_("hid_T_ready"), 1)
                act.wait_ge(weights_used, 6 * e + (moe_base[l] + 6))
                raw(Y[:, 0:512], psum[5][:, :], ACT.Copy).then_inc(S_("y_left_ready"), 1)

        norm_stats(NT, x_tile_ready(DEPTH), lambda t: h[:, t, :], lambda t: xs2[:, t, :])

        def rows_of(tag, n):
            for i in range(n):
                for half in range(2):
                    name = (tag, i, half)
                    ps = full(act, name)
                    free(f(rows[:, i, half * 512:(half + 1) * 512], ps[:, :], ACT.Copy), name)

        def next_rows(t):
            expect("x4_ready")

        def pre_norm(streams):
            for s in range(streams):
                norm_stats(NT, next_rows, lambda t, s=s: x4[:, 2 * s + t, :],
                           lambda t, s=s: xs2[:, 2 * s + t, :], first=2 * s)

        def post_norm(streams):
            for s in range(streams):
                norm_stats(NT, lambda t: expect("ys_ready"), lambda t, s=s: ys[:, 2 * s + t, :],
                           lambda t, s=s: xs2[:, 2 * s + t, :], first=2 * s)

        def odd_modulated(tag, s, l, which):
            odd_chunks((tag, s), lambda c: xT2[:, c, s * S:(s + 1) * S],
                       lambda c: mod_gain[:, l, which, s, c:c + 1],
                       lambda c: mods[:, l, 3 * which * KC + c, s:s + 1])

        def relus(l, T):
            base_h, base_i = hid_done[l], mlp_base[l]
            with act.Fori(0, 4) as i:
                for b in range(2):
                    act.wait_ge(weights_used, 4 * i + (base_i - 1 + b))
                    for j in range(4):
                        if j < 3:
                            act.wait_ge(S_("hidden_full"), 6 * i + (24 * l + 3 * b + j + 1))
                        else:
                            act.wait_ge(weights_used, 4 * i + (base_i + b + 1))
                        raw(hid[:, b, j, 0:T], psum[(4 * b + j) % 2][:, 0:T],
                          ACT.Relu).then_inc(S_("relu_ready"), 1)

        norm_stats(NT, next_rows, lambda t: x4[:, t, :], lambda t: xs2[:, t, :])
        act.wait_ge(S_("ctx_landed"), 16)
        norm_stats(NT, lambda t: None, lambda t: x4[:, 2 + t, :], lambda t: xs2[:, 2 + t, :],
                   first=2)
        for s in range(2):
            odd_chunks(("pool_d", s), lambda c, s=s: diffT[:, c, s * S:(s + 1) * S],
                       lambda c, s=s: mod_gain[:, 0, 0, s, c:c + 1])
        rows_of("rows_mix0", 2)
        post_norm(2)
        pre_norm(2)
        for s in range(2):
            odd_modulated("xm0", s, 0, 1)
        relus(0, 2 * S)
        rows_of("rows_mlp0", 2)
        post_norm(2)
        pre_norm(2)
        for s in range(2):
            odd_modulated("xa", s, 1, 0)
        for n in range(2):
            for t in range(NT):
                name = ("q", n, t)
                ps = full(act, name)
                part = slice(n * 512, (n + 1) * 512)
                step(f(q_raw[:, t, part], ps[:, :], ACT.Copy))
                free(f(q_tmp[:, t, part], ps[:, :], ACT.Square), name)
        for t in range(2 * NT):
            name = ("kv", t)
            ps = full(act, name)
            step(f(kv[:, t, :, :], ps[:, :].rearrange("p (a b) -> p a b", a=2), ACT.Copy))
            free(f(xs2[:, t, 0:2 * P], ps[:, 0:2 * P], ACT.Square), name)
        expect("q_sum_ready")
        f(qst[:, 1, :], qst[:, 0, :], ACT.Sqrt, bias=eps[:, :],
          scale=1.0 / P).then_inc(S_("q_std_ready"), 1)
        expect("k_sum2_ready")
        f(kst[:, 1, :], kst[:, 0, :], ACT.Sqrt, bias=eps[:, :],
          scale=1.0 / P).then_inc(S_("k_std_ready"), 1)
        for pair in range(4):
            name = ("qT", pair)
            ps = full(act, name)
            free(f(qT2[:, 2 * pair:2 * pair + 2, :], ps[:, :].rearrange("p (a t) -> p a t", a=2),
                   ACT.Copy), name)

        def exponentials(u):
            expect("score_max_ready")
            name = ("s", u)
            ps = full(act, name)
            free(f(pr[:, u % 2, :], ps[:, :], ACT.Exp, bias=soft[:, u % 4, 1:2],
                   scale=HEAD_SCALE, accum_out=soft[:, u % 4, 2:3]), name)

        exponentials(0)
        for u in range(NQ * NT):
            if u + 1 < NQ * NT:
                exponentials(u + 1)
            name = ("pT", u)
            ps = full(act, name)
            t = u % NT
            free(f(prT[:, :, t * P:(t + 1) * P], ps[:, :].rearrange("p (a t) -> p a t", a=4),
                   ACT.Copy), name)
        for n in range(2):
            for t in range(NT):
                name = ("wo", n, t)
                ps = full(act, name)
                free(f(ys[:, t, n * 512:(n + 1) * 512], ps[:, :], ACT.Copy), name)
        rows_of("rows_mix1", 1)
        norm_stats(NT, lambda t: freed(act, ("wo", 1, t)), lambda t: ys[:, t, :],
                   lambda t: xs2[:, t, :])
        pre_norm(1)
        odd_modulated("xm1", 0, 1, 1)
        relus(1, S)
        rows_of("rows_mlp1", 1)
        post_norm(1)

    @block.vector
    def _(dve):
        turn = InTurn(dve, "dve_step")
        tick, step, free = turn.tick, turn.tick, turn.free
        v = nc.vector
        tt, ts, stt = turn(v.tensor_tensor), turn(v.tensor_scalar), turn(v.scalar_tensor_tensor)
        copy, reciprocal, reduce = turn(v.tensor_copy), turn(v.reciprocal), turn(v.tensor_reduce)
        memset, top8, top8_at = turn(v.memset), turn(v.max), turn(v.max_index)
        replace, copy_where = turn(v.match_replace), turn(v.copy_predicated)
        seen = {}

        def expect(name, k=1):
            seen[name] = seen.get(name, 0) + k
            dve.wait_ge(S_(name), seen[name])

        def normalise(tiles, src, out, signal, first=0):
            expect("std_ready")
            step(reciprocal(rinv[:, first:first + tiles], std[:, first:first + tiles]))
            for t in range(tiles):
                ts(out(t), src(t), rinv[:, first + t:first + t + 1], None,
                   ALU.mult).then_inc(S_(signal), 1)

        def even_chunks(tag, out, gain, shift=None):
            for b in (0, 2):
                ps = full(dve, (tag, b))
                for c in (2 * b, 2 * b + 1):
                    at_ = (c % 2) * S
                    if shift is None:
                        ins = ts(out(c), ps[:, at_:at_ + S], gain(c), None, ALU.mult)
                    else:
                        ins = ts(out(c), ps[:, at_:at_ + S], gain(c), shift(c), ALU.mult,
                                 ALU.add)
                    if c % 2 == 0:
                        tick(ins)
                free(ins, (tag, b))

        dve.wait_ge(S_("cols"), 16)
        low = C("lower").rearrange("p (l h) -> p l h", l=DEPTH)
        step(tt(lb[:, 0, 0, :], low[:, 0, :], low[:, 1, :], ALU.max))
        tt(lb[:, 2, :, :], low, lb[:, 0, 0:1, :].broadcast_to([P, DEPTH, H4]),
           ALU.subtract).then_inc(S_("lower_shifted"), 1)
        expect("lower_exp")
        step(tt(lb[:, 0, 0, :], lb[:, 2, 0, :], lb[:, 2, 1, :], ALU.add))
        step(reciprocal(lb[:, 0, 1, :], lb[:, 0, 0, :]))
        step(tt(lb[:, 1, :, :], lb[:, 2, :, :], lb[:, 0, 1:2, :].broadcast_to([P, DEPTH, H4]),
                ALU.mult))
        step(tt(lb[:, 0, 1, :], lb[:, 1, 0, :], lb[:, 1, 1, :], ALU.add))
        tick(tt(lb[:, 0, 0, :], lb[:, 1, 0, :], lb[:, 1, 0, :], ALU.subtract))
        step(tt(lb[:, 0, 1, :], lb[:, 0, 1, :], lb[:, 1, 0, :], ALU.subtract))
        step(ts(lb[:, 1, :, :], lb[:, 0, :, :], -1.0, 1.0, ALU.mult, ALU.add))
        ts(lb[:, 2, :, :], lb[:, 1, :, :], HEAD_SCALE, None,
           ALU.mult).then_inc(S_("lower_ready"), 1)
        dve.wait_ge(S_("masks"), 16)
        copy(mask[:, :, :, :].rearrange("p a b c -> p (a b c)"),
             AD[:, :, :].rearrange("p a b -> p (a b)")[:, 0:len(LEVELS) * P]).then_inc(
            S_("masks_ready"), 1)
        dve.wait_ge(S_("x_landed"), 16)

        for l in range(DEPTH):
            normalise(NT, lambda t: h[:, t, :], lambda t: xs[:, t, :], "xs_ready")
            even_chunks(("x1", l), lambda c: xT[:, c, :], lambda c: C("norm1_g", KC * l + c))
            dve.wait_ge(S_("consts"), 16)
            cos = K("cos").rearrange("p (t d) -> p t d", t=NT)
            sin = K("sin").rearrange("p (t b d) -> p t b d", t=NT, b=2)
            for i, kind in enumerate((RQ, RK)):
                for t in range(NT):
                    name = ("proj", l, kind, t)
                    ps = full(dve, name)
                    rows_ = ps[:, :].rearrange("p (h d) -> p h d", h=H4)
                    halves = ps[:, :].rearrange("p (h b d) -> p h b d", h=H4, b=2)
                    tick(tt(rope_t[:, 0, :].rearrange("p (h d) -> p h d", h=H4), rows_,
                            cos[:, t, :].unsqueeze(1).broadcast_to([P, H4, P]), ALU.mult))
                    for b in range(2):
                        ins = tt(rope_t[:, 1, :].rearrange("p (h b d) -> p h b d", h=H4, b=2)
                                 [:, :, b, :], halves[:, :, 1 - b, :],
                                 sin[:, t, b, :].unsqueeze(1).broadcast_to([P, H4, 64]), ALU.mult)
                        if b == 0:
                            tick(ins)
                    free(ins, name)
                    tt(rot[:, i, t, :], rope_t[:, 0, :], rope_t[:, 1, :],
                       ALU.add).then_inc(S_("rot_ready"), 1)
            expect("forget_ready", 2)
            tt(hx[:, 0, :, :], hk[:, 0, :, :], hk[:, 1, :, :],
               ALU.add).then_inc(S_("k_sum_ready"), 1)
            decay = K("decay").rearrange("p (h c) -> p h c", h=H4)
            for head in range(H4):
                name = ("ret_s", l, head)
                ps = full(dve, name)
                tick(tt(RS_[:, 0, head, :], ps[:, 0:S], decay[:, head, P:3 * P], ALU.mult))
                free(tt(RS_[:, 1, head, :], ps[:, S:2 * S], decay[:, head, 0:2 * P], ALU.mult),
                     name)

            def split(x, m):
                return x.rearrange("p h (n b m) -> p (h n) b m", b=2, m=m)

            def prepare(u):
                m, d = units[u]
                q_half, k_half = (1, 0) if d == 0 else (0, 1)
                if m > 1:
                    if u == 2:
                        expect("kdec_ready")
                    if m == P:
                        part = slice(k_half * P, (k_half + 1) * P)
                        tick(tt(kdec[:, d, :, part], hk[:, d, :, part], hx[:, d, :, part],
                                ALU.mult))
                    else:
                        tick(tt(split(kdec[:, d, :, :], m)[:, :, k_half, :],
                                split(hk[:, d, :, :], m)[:, :, k_half, :],
                                split(hx[:, d, :, :], m)[:, :, k_half, :], ALU.mult))
                if m == P:
                    part = slice(q_half * P, (q_half + 1) * P)
                    ins = tt(qdec[:, d, :, :], hq[:, :, part], hf[:, d, :, part], ALU.mult)
                else:
                    ins = tt(qdec[:, d, :, :].rearrange("p h (n m) -> p (h n) m", m=m),
                             split(hq[:, :, :], m)[:, :, q_half, :],
                             split(hf[:, d, :, :], m)[:, :, q_half, :], ALU.mult)
                ins.then_inc(S_("level_ready"), 1)

            def widen(u):
                m, d = units[u]
                q_half, k_half = (1, 0) if d == 0 else (0, 1)
                prod, excl = split(hf[:, d, :, :], m), split(hx[:, d, :, :], m)
                shape = [P, H4 * S // (2 * m), m]
                end = m - 1 if d == 0 else 0
                whole_q = prod[:, :, q_half, end:end + 1]
                whole_k = prod[:, :, k_half, end:end + 1]
                if m == 1:
                    tick(memset(excl[:, :, q_half, :], 1.0))
                    tick(copy(excl[:, :, k_half, :], whole_q))
                else:
                    tick(tt(excl[:, :, k_half, :], excl[:, :, k_half, :],
                            whole_q.broadcast_to(shape), ALU.mult))
                tick(tt(prod[:, :, q_half, :], prod[:, :, q_half, :],
                                  whole_k.broadcast_to(shape), ALU.mult))

            def merge(u):
                m, d = units[u]
                name = ("unit", l, u)
                ps = full(dve, name)
                q_half = 1 if d == 0 else 0
                blocks = P // (2 * m)
                outs = AD[:, :, :].rearrange("p a (n b m) -> p a n b m", b=2, m=m)
                wide = [P, 2 * H4, blocks, m]
                where = mask[:, LEVELS.index(m), d, :].rearrange("p (n m) -> p n m", m=m)
                free(copy_where(outs[:, :, :, q_half, :],
                                       where.unsqueeze(1).broadcast_to(wide),
                                       ps[:, :].rearrange("p (a n m) -> p a n m", a=2 * H4, m=m)),
                     name)

            def ada_bias(n):
                name = ("ada_c", l, n)
                ps = full(dve, name)
                bias = C("b_ada", NMOD * KC * l + 4 * n, 4)
                free(tt(mods[:, l, 4 * n:4 * n + 4, :],
                        ps[:, 0:8].rearrange("p (a b) -> p a b", b=2),
                        bias.unsqueeze(2).broadcast_to([P, 4, 2]), ALU.add), name)

            for pair in range(2):
                freed(dve, ("proj", l, HQ, pair))
                freed(dve, ("same", l, pair))
            u, ada_n = 0, 0

            def one_unit(u):
                prepare(u)
                if units[u][0] < P:
                    widen(u)
                if 1 <= u <= 2 * len(LEVELS):
                    merge(u - 1)

            for kind in mixer_items()[5:]:
                if kind == ADA:
                    if ada_n:
                        ada_bias(ada_n - 1)
                    ada_n += 1
                else:
                    for _ in range(4):
                        one_unit(u)
                        u += 1
                if kind == HG:
                    for t in range(NT):
                        expect("ret_sq_ready")
                        ins = reduce(rstat[:, 0, t, :],
                                              sq[:, t, :].rearrange("p (h d) -> p h d", h=H4),
                                              AX.X, ALU.add)
                        if t == 0:
                            tick(ins)
                    ins.then_inc(S_("ret_sum_ready"), 1)
                    expect("std_ready")
                    step(reciprocal(rinv[:, 0:NT], std[:, 0:NT]))
                    for t in range(NT):
                        name = ("hgrn_o", l, t)
                        ps = full(dve, name)
                        freed(dve, ("proj", l, HG, t))
                        free(stt(xs[:, t, W4:D], ps[:, :], rinv[:, t:t + 1], hg_gate[:, t, :],
                                 ALU.mult, ALU.mult), name)
                    expect("ret_std_ready")
                    step(reciprocal(rstat[:, 2, :, :], rstat[:, 1, :, :]))
                    for t in range(NT):
                        freed(dve, ("proj", l, RG, t))
                        gate = ret_gate[:, t, :].rearrange("p (h d) -> p h d", h=H4)
                        step(tt(gate, gate, rstat[:, 2, t, :].unsqueeze(2)
                                .broadcast_to([P, H4, P]), ALU.mult))
                        name = ("ret_o", l, t)
                        free(tt(xs[:, t, 0:W4], psum[where_is[name][0]][:, :],
                                ret_gate[:, t, :], ALU.mult), name)
            ada_bias(ada_n - 1)
            if l == DEPTH - 1:
                for l2 in range(DEPTH):
                    for which, pre in enumerate(("g_mix_pre", "g_mlp_pre")):
                        for s in range(2):
                            at_ = (3 * which + 1) * KC
                            tick(stt(mod_gain[:, l2, which, s, :],
                                     mods[:, l2, at_:at_ + KC, s], 1.0, C(pre, KC * l2, KC),
                                     ALU.add, ALU.mult))

            def mix_gain(c):
                return C("ret_g", H4 * l + c) if c < H4 else C("hgrn_g", H4 * l + c - H4)

            even_chunks(("mix", l), lambda c: xT[:, c, :], mix_gain)
            for n in range(2):
                for t in range(NT):
                    name = ("w_out", l, n, t)
                    ps = full(dve, name)
                    part = slice(n * 512, (n + 1) * 512)
                    free(tt(h[:, t, part], h[:, t, part], ps[:, :], ALU.add), name)

            normalise(NT, lambda t: h[:, t, :], lambda t: xs[:, t, :], "xs_ready")
            even_chunks(("x2", l), lambda c: xT[:, c, :], lambda c: C("norm2_g", KC * l + c))
            name = ("logit", l)
            ps = full(dve, name)
            step(reduce(rstats[:, :, 0], ps[:, 0:NT * NEXP]
                                 .rearrange("p (t e) -> p t e", t=NT), AX.X, ALU.max))
            ts(rstats[:, :, 1], rstats[:, :, 0], -1.0, None,
               ALU.mult).then_inc(S_("router_max_ready"), 1)
            freed(dve, name)
            step(reciprocal(rstats[:, :, 3], rstats[:, :, 2]))
            for t in range(NT):
                ts(aff[:, t, :], logit[:, t, :], rstats[:, t, 3:4], None,
                   ALU.mult).then_inc(S_("affinity_ready"), 1)
            name = ("affT", l)
            ps = full(dve, name)
            free(copy(affT[:, 0, :], ps[0:NEXP, 0:S]), name)
            freed(dve, name)
            for r in range(CAP // 8):
                part = slice(8 * r, 8 * r + 8)
                a, b = affT[:, r % 2, :], affT[:, 1 - r % 2, :]
                step(top8(top[:, part], a))
                tick(top8_at(topi[:, part], top[:, part], a))
                if r < CAP // 8 - 1:
                    tick(replace(b, top[:, part], a, -1.0))
            step(copy(topf[:, :], topi[:, :]))
            delta = K("delta")[0:NEXP, :].unsqueeze(2).broadcast_to([NEXP, NEXP, CAP])
            for i, what in enumerate((topf, top)):
                tt(spread[:, i, :, :], what[:, :].unsqueeze(1).broadcast_to([NEXP, NEXP, CAP]),
                   delta, ALU.mult).then_inc(S_("spread_ready"), 1)
            name = ("spread", l, 0)
            ps = full(dve, name)
            for t in range(NT):
                ins = ts(onehot[:, t, :], ps[:, :], K("token")[:, t:t + 1], None, ALU.is_equal)
                if t == 0:
                    tick(ins)
            free(ins, name)
            freed(dve, name)
            name = ("spread", l, 1)
            ps = full(dve, name)
            for t in range(NT):
                ins = tt(gated[:, t, :], onehot[:, t, :], ps[:, :], ALU.mult)
                if t == 0:
                    tick(ins)
            free(ins, name)
            freed(dve, name)
            gain2 = C("norm2_g", KC * l, KC).unsqueeze(2).broadcast_to([P, KC, CAP])
            with dve.Fori(0, NEXP) as e:
                done = l * NEXP + e
                dve.wait_ge(S_("gate_T_full"), done + 1)
                nc.vector.tensor_copy(gsel[:, :, :, :], gated[:, :, bass.ds(e * CAP, CAP)].unsqueeze(2)
                              .broadcast_to([P, NT, 4, CAP])).then_inc(S_("gate_sel_ready"), 1)
                dve.wait_ge(S_("gathered"), done + 1)
                nc.vector.tensor_tensor(xeT[:, :, :], psum[7][:, 0:S].rearrange("p (c s) -> p c s", c=KC), gain2,
                   ALU.mult).then_inc(S_("xeT_ready"), 1)
                dve.wait_ge(S_("silu_g_ready"), done + 1)
                dve.wait_ge(weights_used, 6 * e + (moe_base[l] + 4))
                nc.vector.tensor_tensor(hidE[:, :], silu_g[:, :], psum[4][:, 256:512],
                   ALU.mult).then_inc(S_("hid_e_ready"), 1)
                dve.wait_ge(weights_used, 6 * e + (moe_base[l] + 6))
                nc.vector.tensor_copy(Y[:, 512:D], psum[6][:, :]).then_inc(S_("y_right_ready"), 1)
            dve.wait_ge(S_("scattered"), (l + 1) * NEXP + 1)
            for t in range(NT):
                for half in range(2):
                    b = 2 * half + t
                    part = slice(half * 512, (half + 1) * 512)
                    free(tt(h[:, t, part], h[:, t, part], psum[b][:, :], ALU.add), ("moe", l, b))

        expect("std_ready")
        step(reciprocal(rinv[:, 0:NT], std[:, 0:NT]))
        dve.wait_ge(S_("final_g_landed"), 16)
        for t in range(NT):
            stt(x4[:, t, :], h[:, t, :], rinv[:, t:t + 1], gfin[:, :], ALU.mult,
                ALU.mult).then_inc(S_("x4_ready"), 1)

        def normalise_stream(s):
            normalise(NT, lambda t: x4[:, 2 * s + t, :], lambda t: xs2[:, 2 * s + t, :],
                      "xs2_ready", first=2 * s)

        def even_modulated(tag, s, l, which):
            even_chunks((tag, s), lambda c: xT2[:, c, s * S:(s + 1) * S],
                        lambda c: mod_gain[:, l, which, s, c:c + 1],
                        lambda c: mods[:, l, 3 * which * KC + c, s:s + 1])

        def diagonals(l, which, post, n, tag):
            for s in range(n):
                at_ = (3 * which + 2) * KC
                step(tt(gate_col[:, :], mods[:, l, at_:at_ + KC, s], C(post, KC * l, KC),
                        ALU.mult))
                if s:
                    full(dve, (tag, s - 1, 1))
                tt(dg[:, :, :], ident.unsqueeze(1).broadcast_to([P, KC, P]),
                   gate_col[:, :].unsqueeze(2).broadcast_to([P, KC, P]),
                   ALU.mult).then_inc(S_("diag_ready"), 1)

        def add_branch(tag, streams):
            for s in range(streams):
                freed(dve, (tag, s, 0))
                freed(dve, (tag, s, 1))
                expect("std_ready")
                step(reciprocal(rinv[:, 2 * s:2 * s + 2], std[:, 2 * s:2 * s + 2]))
                for t in (2 * s, 2 * s + 1):
                    tick(stt(ys[:, t, :], ys[:, t, :], rinv[:, t:t + 1], rows[:, s, :],
                             ALU.mult, ALU.mult))
                    tt(x4[:, t, :], x4[:, t, :], ys[:, t, :],
                       ALU.add).then_inc(S_("x4_ready"), 1)

        def mlp(l, streams):
            T, tiles = streams * S, streams * NT
            base_h, base_o, base_i = hid_done[l], out_done[l], mlp_base[l]
            with dve.Fori(0, 4) as i:
                for b in range(2):
                    for j in range(4):
                        dve.wait_ge(S_("relu_ready"), 8 * i + (base_h + 4 * b + j + 3))
                        nc.vector.tensor_tensor(hid[:, b, j, 0:T], hid[:, b, j, 0:T], hid[:, b, j, 0:T],
                           ALU.mult).then_inc(S_("hidden_ready"), 1)
                for b in range(2):
                    for t in range(tiles):
                        for half in range(2):
                            k = (b * tiles + t) * 2 + half
                            if (t, half) == (tiles - 1, 1):
                                dve.wait_ge(weights_used, 4 * i + (base_i + 3 + b))
                            else:
                                full_base = 8 * 7 * l
                                dve.wait_ge(S_("out_full"), (4 * tiles - 2) * i
                                            + (full_base + k - b + 1))
                            dve.wait_ge(S_("out_added"), 4 * tiles * i
                                        + (base_o + 9 + k - 2 * tiles))
                            part = slice(half * 512, (half + 1) * 512)
                            nc.vector.tensor_tensor(ys[:, t, part], ys[:, t, part], psum[2 + k % 4][:, :],
                               ALU.add).then_inc(S_("out_added"), 1)
            dve.wait_ge(S_("out_added"), out_done[l] + 16 * tiles + 8)
            for t in range(tiles):
                rows_done()

        def rows_done():
            memset(soft[:, 0, 3:4], 0.0).then_inc(S_("ys_ready"), 1)

        normalise_stream(0)
        dve.wait_ge(S_("ctx_landed"), 16)
        normalise_stream(1)
        for s in range(2):
            even_chunks(("pool_d", s), lambda c, s=s: diffT[:, c, s * S:(s + 1) * S],
                        lambda c, s=s: mod_gain[:, 0, 0, s, c:c + 1])
        dve.wait_ge(S_("pool_scale_landed"), 16)
        for t in range(2 * NT):
            for half in range(2):
                name = ("pool_y", t, half)
                ps = full(dve, name)
                part = slice(half * 512, (half + 1) * 512)
                free(tt(ys[:, t, part], ps[:, :], rows[:, 2, part], ALU.mult), name)
            freed(dve, ("pool_y", t, 0))
            freed(dve, ("pool_y", t, 1))
            rows_done()
        diagonals(0, 0, "g_mix_post", 2, "rows_mix0")
        add_branch("rows_mix0", 2)
        for s in range(2):
            normalise_stream(s)
        step(memset(soft[:, :, :], 0.0))
        memset(soft[:, 3, 3:4], 0.0).then_inc(S_("relu_ready"), 2)
        memset(ys[:, :, :], 0.0).then_inc(S_("out_added"), 8)
        for s in range(2):
            even_modulated("xm0", s, 0, 1)
        mlp(0, 2)
        diagonals(0, 1, "g_mlp_post", 2, "rows_mlp0")
        add_branch("rows_mlp0", 2)

        dve.wait_ge(S_("rope2_landed"), 16)
        dve.wait_ge(S_("gqk_landed"), 16)
        for i in range(2):
            g = gqk[:, i, :]
            g4 = g.rearrange("p (a b d) -> p a b d", a=2, b=2)
            tick(tt(rope_g[:, i, 0, :, :], rope_c[:, 0, :, :],
                    g.unsqueeze(1).broadcast_to([P, NT, P]), ALU.mult))
            for t in range(NT):
                sin4 = rope_c[:, 1, t, :].rearrange("p (a b d) -> p a b d", a=2, b=2)
                out4 = rope_g[:, i, 1, t, :].rearrange("p (a b d) -> p a b d", a=2, b=2)
                for b in range(2):
                    tick(tt(out4[:, :, b, :], sin4[:, :, b, :], g4[:, :, 1 - b, :], ALU.mult))
        for s in range(2):
            normalise_stream(s)
        for s in range(2):
            even_modulated("xa", s, 1, 0)

        def rotate(x, t, heads, i, tmp, out):
            quarters = x.rearrange("p (h b d) -> p h b d", h=2 * heads, b=2)
            tmp4 = tmp[1].rearrange("p (h b d) -> p h b d", h=2 * heads, b=2)
            sin4 = rope_g[:, i, 1, t, :].rearrange("p (a b d) -> p a b d", a=2, b=2)
            cos_ = rope_g[:, i, 0, t, :].unsqueeze(1).broadcast_to([P, heads, P])
            tick(tt(tmp[0].rearrange("p (h d) -> p h d", h=heads),
                    x.rearrange("p (h d) -> p h d", h=heads), cos_, ALU.mult))
            for b in range(2):
                for a in range(2):
                    tick(tt(tmp4[:, a::2, b, :], quarters[:, a::2, 1 - b, :],
                                sin4[:, a, b, :].unsqueeze(1).broadcast_to([P, heads, 32]),
                                ALU.mult))
            return tt(out, tmp[0], tmp[1], ALU.add)

        for t in range(NT):
            for n in range(2):
                freed(dve, ("q", n, t))
            ins = reduce(qst[:, 0, t * NQ:(t + 1) * NQ],
                                  q_tmp[:, t, :].rearrange("p (h d) -> p h d", h=NQ), AX.X,
                                  ALU.add)
            if t == 0:
                tick(ins)
        ins.then_inc(S_("q_sum_ready"), 1)
        for t in range(2 * NT):
            freed(dve, ("kv", t))
            ins = reduce(kst[:, 0, t * NKV:(t + 1) * NKV],
                                  xs2[:, t, 0:2 * P].rearrange("p (h d) -> p h d", h=NKV), AX.X,
                                  ALU.add)
            if t < 3:
                tick(ins)
        ins.then_inc(S_("k_sum2_ready"), 1)
        expect("q_std_ready")
        step(reciprocal(qst[:, 2, :], qst[:, 1, :]))
        for t in range(NT):
            rows_ = q_raw[:, t, :].rearrange("p (h d) -> p h d", h=NQ)
            step(tt(rows_, rows_, qst[:, 2, t * NQ:(t + 1) * NQ].unsqueeze(2)
                    .broadcast_to([P, NQ, P]), ALU.mult))
            rotate(q_raw[:, t, :], t, NQ, 0, (q_tmp[:, 0, :], q_tmp[:, 1, :]),
                   qr[:, t, :]).then_inc(S_("q_rot_ready"), 1)
        expect("k_std_ready")
        step(reciprocal(kst[:, 2, :], kst[:, 1, :]))
        for t in range(2 * NT):
            k_ = kv[:, t, 0, :]
            rows_ = k_.rearrange("p (h d) -> p h d", h=NKV)
            step(tt(rows_, rows_, kst[:, 2, t * NKV:(t + 1) * NKV].unsqueeze(2)
                    .broadcast_to([P, NKV, P]), ALU.mult))
            if t < NT:
                ins = rotate(k_, t, NKV, 1, (q_tmp[:, 0, 0:2 * P], q_tmp[:, 1, 0:2 * P]), k_)
            else:
                ins = tt(rows_, rows_, gqk[:, 1, :].unsqueeze(1).broadcast_to([P, NKV, P]),
                         ALU.mult)
            ins.then_inc(S_("k_rot_ready"), 1)
        for g in range(NKV):
            name = ("kT", g)
            ps = full(dve, name)
            free(copy(kT2[:, g, :], ps[:, :]), name)

        def score_max(u):
            name = ("s", u)
            ps = full(dve, name)
            step(reduce(soft[:, u % 4, 0:1], ps[:, :], AX.X, ALU.max))
            ts(soft[:, u % 4, 1:2], soft[:, u % 4, 0:1], -HEAD_SCALE, None,
               ALU.mult).then_inc(S_("score_max_ready"), 1)

        def take_values(head):
            name = ("o", head)
            ps = full(dve, name)
            free(copy(oT[:, head, :], ps[:, 0:S]), name)

        score_max(0)
        for u in range(NQ * NT):
            if u + 1 < NQ * NT:
                score_max(u + 1)
            freed(dve, ("s", u))
            step(reciprocal(soft[:, u % 4, 3:4], soft[:, u % 4, 2:3]))
            ts(pr[:, u % 2, :], pr[:, u % 2, :], soft[:, u % 4, 3:4], None,
               ALU.mult).then_inc(S_("prob_ready"), 1)
            if u >= 2 and u % 2 == 0:
                take_values(u // 2 - 1)
        take_values(NQ - 1)
        diagonals(1, 0, "g_mix_post", 1, "rows_mix1")
        add_branch("rows_mix1", 1)
        normalise_stream(0)
        step(memset(ys[:, 0:NT, :], 0.0))
        even_modulated("xm1", 0, 1, 1)
        mlp(1, 1)
        diagonals(1, 1, "g_mlp_post", 1, "rows_mlp1")
        add_branch("rows_mlp1", 1)

    @block.gpsimd
    def _(pool):
        g = nc.gpsimd
        g.memset(ones[:, :], 1.0)
        g.memset(zeros[:, :], 0.0).then_inc(S_("gate_T_full"), 1)
        g.memset(eps[:, :], EPS).then_inc(S_("scattered"), 1)
        g.memset(cT[:, :, :], 0.0).then_inc(S_("ones_ready"), 1)
        for l in range(DEPTH):
            freed(pool, ("ret_s", l, H4 - 1))
            g.memset(kdec[:, :, :, :], 0.0).then_inc(S_("kdec_ready"), 1)
            freed(pool, ("w_out", l, 0, 0))
            g.dma_start(wr[:, :, :], w_router[l].rearrange("(c p) e -> p c e", p=P)).then_inc(
                S_("router_landed"), 16)
        pool.wait_ge(S_("spread_ready"), 2 * DEPTH)
        g.dma_start(gfin[:, :], final_g.partition_broadcast(P)).then_inc(S_("final_g_landed"), 16)
        for b in range(4):
            freed(pool, ("moe", DEPTH - 1, b))
        g.dma_start(band[:, :, :, :].rearrange("p a b c -> p (a b c)"),
                    bands).then_inc(S_("bands_landed"), 16)
        g.dma_start(x4[:, NT:2 * NT, :],
                    ctx_x.rearrange("(t p) d -> p t d", p=P)).then_inc(S_("ctx_landed"), 16)
        g.dma_start(rows[:, 2, :], pool_scale.partition_broadcast(P)).then_inc(
            S_("pool_scale_landed"), 16)
        g.dma_start(rope_c[:, :, :, :].rearrange("p a b c -> p (a b c)"),
                    rope2).then_inc(S_("rope2_landed"), 16)
        g.dma_start(gqk[:, :, :].rearrange("p a b -> p (a b)"),
                    g_qk.partition_broadcast(P)).then_inc(S_("gqk_landed"), 16)

    @block.sync
    def _(sp):
        sp.dma_start(h[:, :, :], x.rearrange("(t p) d -> p t d", p=P)).then_inc(
            S_("x_landed"), 16)

        def load(name, depth, sources, view):
            slot, number, _ = items[name]
            if number >= depth:
                sp.wait_ge(weights_used, number - depth + 1)
            for out_, src in zip(view(ring[:, slot, :]), sources):
                sp.dma_start(out_, src).then_inc(landed[slot], 16)

        def chunked(w):
            return [w.rearrange("(c p) n -> p c n", p=P)]

        def eight(slot_):
            return [slot_.rearrange("p (c n) -> p c n", c=KC)]

        def four(slot_):
            return [slot_.rearrange("p (c n) -> p c n", c=4)]

        for l in range(DEPTH):
            ada_n = 0
            for n, kind in enumerate(mixer_items()):
                if kind == ADA:
                    src = w_ada[l, :, ada_n * 512:(ada_n + 1) * 512]
                    ada_n += 1
                else:
                    src = w_in[l, :, kind * 512:(kind + 1) * 512]
                load(("mix", l, n), RING1, chunked(src), eight)
            for n in range(2):
                load(("w_out", l, n), RING1, chunked(w_out[l, :, n * 512:(n + 1) * 512]), eight)
            with sp.Fori(0, NEXP) as e:
                for n in range(6):
                    slot, number, _ = items[("moe", l, 0, n)]
                    sp.wait_ge(weights_used, 6 * e + (number - RING1 + 1))
                    if n < 4:
                        dst = ring[:, slot, :].rearrange("p (k a f) -> p k a f", k=2, a=2)
                        for a, w in enumerate((w_gate, w_up)):
                            src = w[l, bass.ds(e, 1), 2 * n * P:2 * (n + 1) * P, :]
                            sp.dma_start(dst[:, :, a, :],
                                         src.rearrange("o (k p) f -> p (o k) f", p=P)).then_inc(
                                landed[slot], 16)
                    else:
                        src = w_down[l, bass.ds(e, 1), :, :].rearrange(
                            "o (g two p) d -> two p (o g) d", two=2, p=P)[n - 4]
                        sp.dma_start(ring[:, slot, :].rearrange("p (g d) -> p g d", g=4),
                                     src).then_inc(landed[slot], 16)
        for l in range(DEPTH):
            if l == 0:
                load(("mix2", 0, 0), RING2, [w_pool.rearrange("g (k p) e -> p (g k) e", p=P)],
                     lambda s_: [s_[:, 0:2048].rearrange("p (c e) -> p c e", c=8)])
            else:
                for n in range(3):
                    load(("mix2", 1, n), RING2, chunked(w_qkv[:, n * 512:(n + 1) * 512]), eight)
                for n in range(2):
                    load(("mix2", 1, 3 + n), RING2, chunked(w_o[:, n * 512:(n + 1) * 512]),
                         eight)
            with sp.Fori(0, 4) as i:
                for n in range(4):
                    slot, number, _ = items[("mlp", l, n)]
                    sp.wait_ge(weights_used, 4 * i + (number - RING2 + 1))
                    if n < 2:
                        src = w_mlp_in[l, :, bass.ds(i * 1024 + n * 512, 512)]
                        sp.dma_start(eight(ring[:, slot, :])[0],
                                     src.rearrange("(c p) n -> p c n", p=P)).then_inc(
                            landed[slot], 16)
                    else:
                        src = w_mlp_out[l, bass.ds(i * 1024 + (n - 2) * 512, 512), :]
                        sp.dma_start(four(ring[:, slot, :])[0],
                                     src.rearrange("(c p) n -> p c n", p=P)).then_inc(
                            landed[slot], 16)
        sp.wait_ge(S_("x4_ready"), X4_TOTAL)
        sp.dma_start(out.rearrange("(t p) d -> p t d", p=P), x4[:, 0:NT, :]).then_inc(
            S_("stored"), 16)
        sp.wait_ge(S_("stored"), 16)

    es.close()


X4_TOTAL = 2 + 4 + 4 + 2 + 2


def shape_constants():
    f = np.float32
    tok = np.arange(S)
    half = P // 2
    inv = f(10000.0) ** (-np.arange(half, dtype=f) / f(half))
    ang = tok.astype(f)[:, None] * inv[None, :]
    cos = np.concatenate([np.cos(ang)] * 2, 1)
    sin = np.concatenate([-np.sin(ang), np.sin(ang)], 1)

    def by_tile(a):
        return a.reshape(NT, P, -1).transpose(1, 0, 2).reshape(P, -1)

    gamma = np.log1p(-(2.0 ** (-5.0 - np.arange(H4, dtype=f)))).astype(f)
    dist = np.abs(np.arange(3 * P)[None, :] - P - np.arange(P)[:, None]).astype(f)
    decay = np.exp(gamma[None, :, None] * dist[:, None, :]) * HEAD_SCALE
    sel = np.zeros((P, 2), f)
    for g in range(4):
        for j in range(2):
            sel[32 * g + j, j] = 1
    token = np.stack([np.arange(P) + P * t for t in range(NT)], 1)
    delta = np.zeros((P, NEXP), f)
    delta[:NEXP] = np.eye(NEXP)
    consts = np.concatenate([np.eye(P), by_tile(cos), by_tile(sin), decay.reshape(P, -1), sel,
                             token, delta], 1).astype(f)

    masks = np.zeros((P, len(LEVELS), 2, P // 2), f)
    s = np.arange(P)[:, None]
    u = np.arange(P // 2)[None, :]
    for i, m in enumerate(LEVELS):
        same = s // (2 * m) == u // m
        masks[:, i, 0] = same & (s % (2 * m) < m)
        masks[:, i, 1] = same & (s % (2 * m) >= m)
    masks = masks.reshape(P, -1)

    bands = np.zeros((len(WINDOWS), S, S), f)
    for g, w in enumerate(WINDOWS):
        lo = np.clip(tok - w // 2, 0, S)
        hi = np.clip(tok + w - w // 2, 0, S)
        for t in range(S):
            bands[g, lo[t]:hi[t], t] = f(1) / f(hi[t] - lo[t])
            bands[g, t, t] -= f(1)
    bands = bands.reshape(len(WINDOWS), NT, P, S).transpose(2, 0, 1, 3).reshape(P, -1)

    inv2 = f(10000.0) ** (-np.arange(0, half, 2, dtype=f) / f(half))
    ar = (tok // GRID_W).astype(f)[:, None] * inv2
    ac = (tok % GRID_W).astype(f)[:, None] * inv2
    cos2 = np.concatenate([np.cos(ar)] * 2 + [np.cos(ac)] * 2, 1)
    sin2 = np.concatenate([-np.sin(ar), np.sin(ar), -np.sin(ac), np.sin(ac)], 1)
    rope2 = np.concatenate([by_tile(cos2), by_tile(sin2)], 1)
    return consts, masks, np.ascontiguousarray(bands, f), np.ascontiguousarray(rope2, f)


def kernel(**inputs):
    import concourse.bacc as bacc
    from concourse.bass_utils import run_bass_kernel_spmd

    a = {k: np.asarray(v) for k, v in inputs.items()}

    def columns(v):
        return np.asarray(v).reshape(-1, P).T

    cols = np.concatenate([columns(a[n]) for n in (
        "norm1_g", "norm2_g", "ret_norm_g", "hgrn_norm_g", "lower_bounds", "b_ada_2",
        "g_mix_pre_2", "g_mix_post_2", "g_mlp_pre_2", "g_mlp_post_2", "c_2", "c_ctx_2")], 1)
    assert cols.shape == (P, NCOLS)
    consts, masks, bands, rope2 = shape_constants()
    arrays = {
        "x": a["x"].reshape(S, D), "cols": cols, "w_in": a["w_in"], "w_out": a["w_out"],
        "w_router": a["w_router"], "w_gate": a["w_gate"], "w_up": a["w_up"],
        "w_down": a["w_down"], "final_g": a["final_norm_g"], "ctx_x": a["ctx_2"].reshape(S, D),
        "w_ada": a["w_ada_2"], "w_pool": a["w_pool_2"][0], "pool_scale": a["pool_scale_2"][0],
        "w_qkv": a["w_qkv_2"][0], "g_qk": np.concatenate([a["g_q_2"][0], a["g_k_2"][0]]),
        "w_o": a["w_o_2"][0], "w_mlp_in": a["w_mlp_in_2"], "w_mlp_out": a["w_mlp_out_2"],
        "consts": consts, "masks": masks, "bands": bands, "rope2": rope2,
    }
    arrays = {f"in_{k}": np.ascontiguousarray(v) for k, v in arrays.items()}
    nc = bacc.Bacc("TRN2", target_bir_lowering=False, num_devices=1)
    args = {k[3:]: nc.dram_tensor(k, v.shape, mybir.dt.from_np(v.dtype),
                                  kind="ExternalInput").ap() for k, v in arrays.items()}
    out = nc.dram_tensor("out", (S, D), F32, kind="ExternalOutput").ap()
    build_program(nc, out=out, **args)
    r = run_bass_kernel_spmd(nc, [arrays], core_ids=[0])
    return r.results[0]["out"].reshape(1, S, D)
```

```python
from contextlib import ExitStack

import numpy as np

import concourse.bass as bass
from concourse import mybir

ALU = mybir.AluOpType
ACT = mybir.ActivationFunctionType
F32 = mybir.dt.float32
F32R = mybir.dt.float32r
BF16 = mybir.dt.bfloat16
U8 = mybir.dt.uint8
U32 = mybir.dt.uint32
AX = mybir.AxisListType

P = 128
D = 1024
KC = D // P
S = 256
NT = S // P
DEPTH = 2
H4 = 4
W4 = H4 * P
IN_COLS = 9 * W4
NEXP = 16
CAP = 2 * S // NEXP
FF = 1024
DFF = 4096
NMOD = 6
NQ, NKV = 8, 2
EPS = 1e-6
HEAD_SCALE = float(P) ** -0.5
WINDOWS = (2, 4, 8, 16)
GRID_W = 64
SLOT = 4096
RING1 = 6
RING2 = (2, 4)
LEVELS = (1, 2, 4, 8, 16, 32, 64)

COLS = {}
_n = 0
for _name, _w in (("norm1_g", 16), ("norm2_g", 16), ("ret_g", 8), ("hgrn_g", 8), ("lower", 8),
                  ("b_ada", 96), ("g_mix_pre", 16), ("g_mix_post", 16), ("g_mlp_pre", 16),
                  ("g_mlp_post", 16), ("c", 8), ("c_ctx", 8)):
    COLS[_name] = (_n, _n + _w)
    _n += _w
NCOLS = _n
CONSTS = {}
_n = 0
for _name, _w in (("ident", P), ("cos", NT * P), ("sin", NT * P), ("decay", H4 * 3 * P),
                  ("sel", 2), ("token", NT), ("delta", NEXP)):
    CONSTS[_name] = (_n, _n + _w)
    _n += _w
NCONST = _n

RQ, RK, RV, RG, HQ, HFF, HFB, HI, HG = range(9)
ADA = "ada"


def mixer_items():
    return [RQ, RK, HFF, HFB, HQ, RV, ADA, HI, ADA, ADA, RG, ADA, ADA, HG, ADA, ADA,
            ADA, ADA, ADA, ADA, ADA]


def build_program(nc, x, cols, w_in, w_out, w_router, w_gate, w_up, w_down, final_g, ctx_x, w_ada,
                  w_pool, pool_scale, w_qkv, g_qk, w_o, w_mlp_in, w_mlp_out, consts, masks,
                  bands, rope2, out):
    es = ExitStack()
    at = [16512]
    here = {}

    def place(name, shape, dtype=F32, where=None):
        size = int(np.prod(shape[1:])) * (1 if dtype == U8 else 2 if dtype == BF16 else 4)
        offset = at[0] if where is None else here[where]
        here[name] = offset
        if where is None:
            at[0] += (size + 31) // 32 * 32
        return nc.alloc_sbuf_tensor_at(name, list(shape), dtype, offset=offset)

    ring = place("ring", [P, RING1, SLOT])
    ring_end = at[0]
    ident_all = place("consts_sb", [P, NCONST])
    col = place("cols_sb", [P, NCOLS])
    mods = place("mods", [P, DEPTH, NMOD * KC, 2])
    mod_gain = place("mod_gain", [P, DEPTH, 2, 2, KC])
    cT = place("silu_c", [P, KC, 32])
    ones = place("ones", [P, P])
    lb = place("lower_bound", [P, 3, DEPTH, H4])
    eps = place("eps", [P, 1])
    ssq = place("ssq", [P, 4])
    std = place("std", [P, 4])
    rinv = place("rinv", [P, 4])
    zeros = place("zeros", [P, P], BF16)
    mask = place("mask_sb", [P, len(LEVELS), 2, P // 2], U8)
    h = place("h", [P, NT, D])
    h_at = here["h"]

    first_at = at[0]
    xs = place("xs", [P, NT, D])
    xT = place("xT", [P, KC, S])
    r_at = at[0]
    rot = place("rot", [P, 2, NT, W4])
    RS_ = place("ret_scores", [P, NT, H4, S], where="rot")
    ret_v = place("ret_v", [P, NT, W4])
    ret_gate = place("ret_gate", [P, NT, W4])
    hg_v = place("hgrn_v", [P, NT, W4])
    hg_gate = place("hgrn_gate", [P, NT, W4])
    retT = place("retT", [P, 2, H4, S])
    kdec = place("kdec", [P, 2, H4, S], where="retT")
    hq = place("hgrn_q", [P, H4, S])
    hf = place("hgrn_f", [P, 2, H4, S])
    hk = place("hgrn_k", [P, 2, H4, S])
    hx = place("hgrn_x", [P, 2, H4, S])
    qdec = place("qdec", [P, 2, H4, P])
    rope_t = place("rope_tmp", [P, 2, W4], where="qdec")
    AD = place("hgrn_diag", [P, 2 * H4, P])
    AO = place("hgrn_off", [P, 2, H4, P])
    ada_s = place("ada_rows", [P, 512])
    rstat = place("ret_stat", [P, 3, NT, H4])
    sq = place("square", [P, NT, W4], where="qdec")
    save = at[0]
    at[0] = r_at
    wr = place("router_sb", [P, KC, NEXP])
    logit = place("logit", [P, NT, NEXP])
    aff = place("affinity", [P, NT, NEXP])
    rstats = place("router_stat", [P, NT, 4])
    affT = place("affinityT", [NEXP, 2, S])
    top = place("top_gate", [NEXP, CAP])
    topi = place("top_index", [NEXP, CAP], U32)
    topf = place("top_index_f", [NEXP, CAP])
    spread = place("spread", [NEXP, 2, NEXP, CAP])
    onehot = place("onehot", [P, NT, NEXP * CAP])
    gated = place("gated", [P, NT, NEXP * CAP])
    gsel = place("gate_sel", [P, NT, 4, CAP])
    GT = place("gate_T", [P, S])
    xeT = place("xeT", [P, KC, CAP])
    silu_g = place("silu_g", [P, 256])
    hidE = place("hid_e", [P, 256])
    hidT = place("hid_T", [P, 2, P])
    Y = place("y_e", [P, D])
    gfin = place("final_g_row", [P, D])
    assert at[0] <= save
    top_of_first = save

    at[0] = h_at
    x4 = place("x4", [P, 2 * NT, D])
    assert at[0] >= first_at
    ys = place("y2", [P, 2 * NT, D])
    xs2 = place("xs2", [P, 2 * NT, D])
    xT2 = place("xT2", [P, KC, 2 * S])
    x_full = place("x_full", [P, KC, 2 * S])
    rows = place("gate_rows", [P, 3, D])
    rope_g = place("rope_gained", [P, 2, 2, NT, P])
    gqk = place("gqk_sb", [P, 2, P])
    gate_col = place("gate_col", [P, KC])
    soft = place("softmax_stat", [P, 4, 4])
    qst = place("q_stat", [P, 3, NT * NQ])
    kst = place("k_stat", [P, 3, 2 * NT * NKV])
    assert at[0] <= 229344, at[0]
    x_high = place("x_high", [P, KC, 2 * S], F32R, where="xT2")
    x_low = place("x_low", [P, KC, 2 * S], F32R, where="x_full")
    w_low = place("w_low", [P, RING2[1], SLOT], F32R, where="ring")
    at[0] = here["ring"] + 2 * SLOT * 4
    h_high0 = place("hid_high0", [P, 2, 4, 2 * S], F32R)
    h_low0 = place("hid_low0", [P, 2, 4, 2 * S], F32R)
    w_high = place("w_high", [P, 2, SLOT], F32R)
    assert at[0] == ring_end
    at[0] = here["xs2"]
    h_high1 = place("hid_high1", [P, 2, 4, S], F32R)
    h_low1 = place("hid_low1", [P, 2, 4, S], F32R)
    dg = place("diag", [P, KC, P], where="rope_gained")
    h_raw = place("hid_raw", [P, 2, 2 * S], where="rope_gained")
    band = place("band_sb", [P, 4, NT, S], where="x_full")
    diffT = place("diffT", [P, KC, 2 * S], where="xT2")
    qr = place("q_rot", [P, NT, D], where="y2")
    at[0] = here["y2"] + NT * D * 4
    q_tmp = place("q_tmp", [P, 2, D])
    q_sq = place("q_square", [P, NT, D], where="xs2")
    at[0] = here["xs2"]
    qT2 = place("qT2", [P, NQ, S])
    pr = place("prob", [P, 2, 2 * S])
    prT = place("probT", [P, 4, S])
    q_raw = place("q_raw", [P, NT, D], where="x_full")
    oT = place("oT", [P, NQ, S], where="x_full")
    at[0] = here["x_full"] + NT * D * 4
    kv = place("kv", [P, 2 * NT, 2, 2 * P])
    at[0] = here["consts_sb"] + 4 * CONSTS["decay"][0]
    kT2 = place("kT2", [P, NKV, 2 * S])
    rope_c = place("rope2_sb", [P, 2, NT, P])
    assert at[0] <= here["consts_sb"] + 4 * CONSTS["decay"][1]
    mlp_parts = ((h_high0, h_low0), (h_high1, h_low1))

    psum = [es.enter_context(nc.psum_tensor(f"bank{i}", [P, 512], F32)) for i in range(8)]
    sems = {}

    def S_(name):
        if name not in sems:
            sems[name] = es.enter_context(nc.semaphore(name))
        return sems[name]

    landed = [S_(f"landed{i}") for i in range(RING1)]
    weights_used = S_("weights_used")
    bank_full = [S_(f"bank_full{i}") for i in range(8)]
    bank_free = [S_(f"bank_free{i}") for i in range(8)]

    def C(name, i=None, n=1):
        a, b = COLS[name]
        return col[:, a:b] if i is None else col[:, a + i:a + i + n]

    def K(name):
        a, b = CONSTS[name]
        return ident_all[:, a:b]

    ident = K("ident")

    items, count = {}, [0, [0] * RING1]

    def item(name, slot, dmas):
        count[1][slot] += 16 * dmas
        items[name] = (slot, count[0], count[1][slot])
        count[0] += 1

    slot = 0
    for layer in range(DEPTH):
        for n, kind in enumerate(mixer_items()):
            item(("mix", layer, n), slot, 1)
            slot = (slot + 1) % RING1
        for n in range(2):
            item(("w_out", layer, n), slot, 1)
            slot = (slot + 1) % RING1
        for e in range(NEXP):
            for n in range(6):
                item(("moe", layer, e, n), slot, 2 if n < 4 else 1)
                slot = (slot + 1) % RING1
    assert slot == 4
    for layer in range(DEPTH):
        order = ((0, 1), (1, 0, 2, 3))[layer]
        for n, name in enumerate(
                [("mix2", layer, n) for n in range(1 if layer == 0 else 5)]
                + [("mlp", layer, n) for n in range(16)]):
            item(name, order[n % RING2[layer]], 1)

    def wait_landed(pe, name):
        slot, _, value = items[name]
        pe.wait_ge(landed[slot], value)
        return ring[:, slot, :]

    filled, frees, where_is, read_by = [0] * 8, [0] * 8, {}, {}

    def take(pe, name, bank, readers=1):
        if frees[bank]:
            pe.wait_ge(bank_free[bank], frees[bank])
        frees[bank] += readers
        read_by[name] = (bank_free[bank], frees[bank])
        where_is[name] = (bank, None, None)
        return psum[bank]

    def fill(ins, name):
        bank = where_is[name][0]
        filled[bank] += 1
        where_is[name] = (bank, bank_full[bank], filled[bank])
        ins.then_inc(bank_full[bank], 1)

    def fill_and_release(ins, name, item_name):
        where_is[name] = (where_is[name][0], weights_used, items[item_name][1] + 1)
        ins.then_inc(weights_used, 1)

    def full(eng, name):
        bank, sem, value = where_is[name]
        eng.wait_ge(sem, value)
        return psum[bank]

    def freed(eng, name):
        eng.wait_ge(*read_by[name])

    def free(ins, name):
        ins.then_inc(bank_free[where_is[name][0]], 1)

    class InTurn:

        def __init__(self, eng, step_name):
            self.eng, self.step, self.mine, self.totals = eng, S_(step_name), None, {}

        def __call__(self, op):
            def run(*args, **kw):
                assert self.mine != "none", "the instruction before signals nothing"
                if self.mine:
                    self.eng.wait_ge(*self.mine)
                self.ins, self.mine = op(*args, **kw), "none"
                return self
            return run

        def then_inc(self, sem, n, value=None):
            self.ins.then_inc(sem, n)
            self.totals[id(sem)] = self.totals.get(id(sem), 0) + n
            self.mine = (sem, value or self.totals[id(sem)])

        def tick(self, _=None):
            self.then_inc(self.step, 1)

        def free(self, _, name):
            self.then_inc(read_by[name][0], 1, read_by[name][1])

    units = [(m, d) for m in LEVELS for d in range(2)] + [(P, 0), (P, 1)]
    moe_base = [items[("moe", l, 0, 0)][1] for l in range(DEPTH)]
    per_item = [16 * 4 // r for r in RING2]
    mlp_base = [items[("mlp", l, 0)][1] for l in range(DEPTH)]
    hid_done, out_done = [0, 4 * 8], [0, 8 * 8]

    block = es.enter_context(nc.Block())

    @block.tensor
    def _(pe):
        mm, turn = nc.tensor.matmul, nc.tensor.transpose
        turned = [None]

        def transposes(tag, src, ready, first=4):
            for t in range(NT):
                ready(t)
                for b in range(4):
                    bank = (first + b) % 8
                    ps = take(pe, (tag, b), bank) if t == 0 else psum[bank]
                    for c in (2 * b, 2 * b + 1):
                        at_ = (c % 2) * S + t * P
                        ins = turn(ps[:, at_:at_ + P], src(t)[:, c * P:(c + 1) * P], ident)
                    if t == NT - 1:
                        fill(ins, (tag, b))
            turned[0] = tag

        def wait_turned(c=KC - 1):
            freed(pe, (turned[0], c // 2))

        def rows_ready(name):
            seen = [0]

            def ready(t):
                seen[0] += 1
                pe.wait_ge(S_(name), seen[0])
            return ready

        xs_ready, xs2_ready = rows_ready("xs_ready"), rows_ready("xs2_ready")

        def ada_item(layer, l_item, n, tag):
            w = wait_landed(pe, l_item).rearrange("p (c n) -> p c n", c=KC)
            if n == 0 and layer == 0:
                pe.wait_ge(S_("silu_c_ready"), 2)
            ps = take(pe, tag, 6)
            for k in range(2):
                for g in range(4):
                    ins = mm(ps[32 * g:32 * g + 32, :], cT[:, 2 * g + k, :], w[:, 2 * g + k, :],
                             start=k == 0, stop=k == 1)
            fill_and_release(ins, tag, l_item)

        def ada_columns(layer, n, tag):
            freed(pe, ("ada", layer, n))
            ps = take(pe, tag, 7)
            for j in range(4):
                ins = mm(ps[:, 2 * j:2 * j + 2], ada_s[:, j * P:(j + 1) * P], K("sel"),
                         start=True, stop=True)
            fill(ins, tag)

        pe.wait_ge(S_("consts"), 16)
        pe.wait_ge(S_("ones_ready"), 1)

        for l in range(DEPTH):
            transposes(("x1", l), lambda t: xs[:, t, :], xs_ready)
            proj_bank = [0]

            def take_proj(name, readers=1):
                b = proj_bank[0]
                proj_bank[0] = (b + 1) % 4
                return take(pe, name, b, readers)

            def project_rows(n, kind, t):
                it = ("mix", l, n)
                w = wait_landed(pe, it).rearrange("p (c n) -> p c n", c=KC)
                name = ("proj", l, kind, t)
                ps = take_proj(name)
                for c in range(KC):
                    if n == 0 and t == 0:
                        wait_turned(c)
                    ins = mm(ps[:, :], xT[:, c, t * P:(t + 1) * P], w[:, c, :], start=c == 0,
                             stop=c == KC - 1)
                if t == NT - 1:
                    fill_and_release(ins, name, it)
                else:
                    fill(ins, name)

            def project_features(n, kind):
                it = ("mix", l, n)
                w = wait_landed(pe, it).rearrange("p (c n) -> p c n", c=KC)
                for pair in range(2):
                    name = ("proj", l, kind, pair)
                    ps = take_proj(name)
                    for head in (2 * pair, 2 * pair + 1):
                        for c in range(KC):
                            ins = mm(ps[:, (head % 2) * S:(head % 2 + 1) * S],
                                     w[:, c, head * P:(head + 1) * P], xT[:, c, :],
                                     start=c == 0, stop=c == KC - 1)
                    if pair == 1:
                        fill_and_release(ins, name, it)
                    else:
                        fill(ins, name)

            def turn_ret(i):
                pe.wait_ge(S_("rot_ready"), (2 * l + i) * NT + NT)
                for pair in range(2):
                    name = ("retT", l, i, pair)
                    ps = take(pe, name, 4 + 2 * i + pair)
                    for head in (2 * pair, 2 * pair + 1):
                        for t in range(NT):
                            at_ = (head % 2) * S + t * P
                            ins = turn(ps[:, at_:at_ + P], rot[:, i, t, head * P:(head + 1) * P],
                                       ident)
                    fill(ins, name)

            def ret_scores():
                for i in range(2):
                    for pair in range(2):
                        freed(pe, ("retT", l, i, pair))
                for head in range(H4):
                    name = ("ret_s", l, head)
                    ps = take(pe, name, 4 + head)
                    for t in range(NT):
                        ins = mm(ps[:, t * S:(t + 1) * S], retT[:, 1, head, t * P:(t + 1) * P],
                                 retT[:, 0, head, :], start=True, stop=True)
                    fill(ins, name)

            def hgrn_same():
                pe.wait_ge(S_("k_sum_ready"), l + 1)
                for pair in range(2):
                    freed(pe, ("proj", l, HQ, pair))
                for t in range(2):
                    name = ("same", l, t)
                    ps = take(pe, name, 4 + t)
                    for j in range(H4):
                        head, tile = (4 * t + j) // 2, j % 2
                        part = slice(tile * P, (tile + 1) * P)
                        ins = mm(ps[:, j * P:(j + 1) * P], hx[:, 0, head, part], hq[:, head, part],
                                 start=True, stop=True)
                    fill(ins, name)

            def hgrn_unit(u):
                m, d = units[u]
                name = ("unit", l, u)
                pe.wait_ge(S_("level_ready"), len(units) * l + u + 1)
                ps = take(pe, name, 4 + u % 2)
                for head in range(H4):
                    if m == P:
                        ins = mm(ps[:, head * P:(head + 1) * P],
                                 kdec[:, d, head, d * P:(d + 1) * P], qdec[:, d, head, :],
                                 start=True, stop=True)
                        continue
                    for t in range(NT):
                        j = 2 * head + t
                        key = (hk if m == 1 else kdec)[:, d, head, t * P:(t + 1) * P]
                        ins = mm(ps[:, j * 64:(j + 1) * 64], key,
                                 qdec[:, d, head, t * 64:(t + 1) * 64], start=True, stop=True)
                fill(ins, name)

            def ret_out():
                for head in range(H4):
                    freed(pe, ("ret_s", l, head))
                for t in range(NT):
                    freed(pe, ("proj", l, RV, t))
                for t in range(NT):
                    name = ("ret_o", l, t)
                    ps = take_proj(name)
                    for head in range(H4):
                        part = slice(head * P, (head + 1) * P)
                        for j in range(NT):
                            ins = mm(ps[:, part], RS_[:, j, head, t * P:(t + 1) * P],
                                     ret_v[:, j, part], start=j == 0, stop=j == NT - 1)
                    fill(ins, name)

            def hgrn_out():
                for u in range(len(units) - 4, len(units)):
                    freed(pe, ("unit", l, u))
                for t in range(NT):
                    freed(pe, ("proj", l, HI, t))
                for t in range(NT):
                    name = ("hgrn_o", l, t)
                    ps = take_proj(name)
                    for head in range(H4):
                        part = slice(head * P, (head + 1) * P)
                        mm(ps[:, part], AD[:, 2 * head + t, :], hg_v[:, t, part],
                           start=True, stop=False)
                        ins = mm(ps[:, part], AO[:, 1 - t, head, :], hg_v[:, 1 - t, part],
                                 start=False, stop=True)
                    fill(ins, name)

            fill_u, ada_n, pending = [0], [0], []

            def some_units(n):
                for _ in range(n):
                    if fill_u[0] < len(units):
                        hgrn_unit(fill_u[0])
                        fill_u[0] += 1

            for n, kind in enumerate(mixer_items()):
                if kind == ADA:
                    if pending:
                        ada_columns(l, pending[0], ("ada_c", l, pending.pop()))
                    ada_item(l, ("mix", l, n), ada_n[0], ("ada", l, ada_n[0]))
                    pending.append(ada_n[0])
                    ada_n[0] += 1
                elif kind in (HQ, HFF, HFB):
                    project_features(n, kind)
                    if kind == HFF:
                        turn_ret(0)
                    elif kind == HFB:
                        turn_ret(1)
                    else:
                        ret_scores()
                        hgrn_same()
                else:
                    for t in range(NT):
                        project_rows(n, kind, t)
                        if n > 4:
                            some_units(2)
                if kind == HG:
                    some_units(len(units))
                    ret_out()
                    hgrn_out()
            ada_columns(l, pending[0], ("ada_c", l, pending.pop()))

            def mix_ready(t):
                freed(pe, ("ret_o", l, t))
                freed(pe, ("hgrn_o", l, t))

            transposes(("mix", l), lambda t: xs[:, t, :], mix_ready)
            for n in range(2):
                it = ("w_out", l, n)
                w = wait_landed(pe, it).rearrange("p (c n) -> p c n", c=KC)
                for t in range(NT):
                    name = ("w_out", l, n, t)
                    ps = take(pe, name, 2 * n + t)
                    for c in range(KC):
                        if n == 0 and t == 0:
                            wait_turned(c)
                        ins = mm(ps[:, :], xT[:, c, t * P:(t + 1) * P], w[:, c, :],
                                 start=c == 0, stop=c == KC - 1)
                    if t == NT - 1:
                        fill_and_release(ins, name, it)
                    else:
                        fill(ins, name)

            transposes(("x2", l), lambda t: xs[:, t, :], xs_ready)
            for c in range(0, KC, 2):
                wait_turned(c)
            name = ("logit", l)
            ps = take(pe, name, 4)
            pe.wait_ge(S_("router_landed"), 16 * (l + 1))
            for t in range(NT):
                for c in range(KC):
                    ins = mm(ps[:, t * NEXP:(t + 1) * NEXP], xT[:, c, t * P:(t + 1) * P],
                             wr[:, c, :], start=c == 0, stop=c == KC - 1)
            fill(ins, name)
            pe.wait_ge(S_("affinity_ready"), NT * (l + 1))
            name = ("affT", l)
            ps = take(pe, name, 5)
            for t in range(NT):
                ins = turn(ps[0:NEXP, t * P:(t + 1) * P], aff[:, t, :], ident)
            fill(ins, name)
            for b in range(4):
                ps = take(pe, ("moe", l, b), b)
                mm(ps[:, :], zeros[:, :], zeros[:, :].unsqueeze(1).broadcast_to([P, 4, P]),
                   start=True, stop=False,
                   skip_group_check=True)
            for i in range(2):
                pe.wait_ge(S_("spread_ready"), 2 * l + i + 1)
                name = ("spread", l, i)
                ps = take(pe, name, 6 + i, 1)
                ins = mm(ps[:, :], ones[0:NEXP, :], spread[:, i, :, :].rearrange("e a b -> e (a b)"),
                         start=True, stop=True)
                fill(ins, name)
            for b in range(4, 8):
                pe.wait_ge(bank_free[b], frees[b])
            start_slot = items[("moe", l, 0, 0)][0]
            land = [items[("moe", l, 0, n)] for n in range(6)]
            with pe.Fori(0, NEXP) as e:
                done = l * NEXP + e
                pe.wait_ge(S_("gate_sel_ready"), done + 1)
                for t in range(NT):
                    ins = turn(psum[5][:, t * P:(t + 1) * P],
                               gsel[:, t, :, :].rearrange("p a b -> p (a b)"), ident)
                ins.then_inc(S_("gate_T_full"), 1)
                for c in range(KC):
                    for t in range(NT):
                        ins = mm(psum[7][:, c * CAP:(c + 1) * CAP],
                                 xs[:, t, c * P:(c + 1) * P],
                                 onehot[:, t, bass.ds(e * CAP, CAP)], start=t == 0,
                                 stop=t == NT - 1, skip_group_check=True)
                ins.then_inc(S_("gathered"), 1)
                pe.wait_ge(S_("xeT_ready"), done + 1)
                for n in range(4):
                    sl, _, value = land[n]
                    pe.wait_ge(landed[sl], value + 32 * e)
                    w = ring[:, sl, :].rearrange("p (k a f) -> p k a f", k=2, a=2)
                    for k in range(2):
                        for g in range(4):
                            ins = mm(psum[4][32 * g:32 * g + 32, :], xeT[:, 2 * n + k, :],
                                     w[:, k, :, 256 * g:256 * (g + 1)],
                                     start=n == 0 and k == 0, stop=n == 3 and k == 1,
                                     skip_group_check=True)
                    ins.then_inc(weights_used, 1)
                pe.wait_ge(S_("gate_T_ready"), done + 1)
                pe.wait_ge(S_("hid_e_ready"), done + 1)
                for j in range(2):
                    ins = turn(psum[6][:, j * P:(j + 1) * P], hidE[:, j * P:(j + 1) * P], ident)
                ins.then_inc(S_("hid_T_full"), 1)
                pe.wait_ge(S_("hid_T_ready"), done + 1)
                for n in range(2):
                    sl, _, value = land[4 + n]
                    pe.wait_ge(landed[sl], value + 16 * e)
                    w = ring[:, sl, :].rearrange("p (g d) -> p g d", g=4)
                    for half in range(2):
                        for g in range(4):
                            ins = mm(psum[5 + half][32 * g:32 * g + 32, :],
                                     hidT[:, n, 32 * g:32 * g + 32],
                                     w[:, g, half * 512:(half + 1) * 512],
                                     start=n == 0, stop=n == 1, skip_group_check=True)
                    ins.then_inc(weights_used, 1)
                pe.wait_ge(S_("y_left_ready"), done + 1)
                pe.wait_ge(S_("y_right_ready"), done + 1)
                for half in range(2):
                    for t in range(NT):
                        ins = mm(psum[2 * half + t][:, :], GT[:, t * P:(t + 1) * P],
                                 Y[:, half * 512:(half + 1) * 512], start=False, stop=False,
                                 skip_group_check=True)
                ins.then_inc(S_("scattered"), 1)

        def post_rows(tag, n):
            for i in range(n):
                pe.wait_ge(S_("diag_ready"), rows_done[0] + 1)
                for half in range(2):
                    name = (tag, i, half)
                    ps = take(pe, name, 2 * (rows_done[0] % 2) + half)
                    ins = mm(ps[:, :], ones[:, :],
                             dg[:, 4 * half:4 * half + 4, :].rearrange("p a b -> p (a b)"),
                             start=True, stop=True)
                    fill(ins, name)
                rows_done[0] += 1

        rows_done = [0]

        def product(ps, left, right, first, last):
            (lh, ll), (rh, rl) = left, right
            mm(ps, lh, rh, start=first, stop=False, skip_group_check=True)
            mm(ps, lh, rl, start=False, stop=False, skip_group_check=True)
            return mm(ps, ll, rh, start=False, stop=last, skip_group_check=True)

        def mlp(l, streams):
            T = streams * S
            tiles = streams * NT
            first = [items[("mlp", l, n)][0] for n in range(4)]
            base_h, base_o = hid_done[l], out_done[l]
            h_high, h_low = mlp_parts[l]

            def parts(n, c):
                return [w.rearrange("p (c n) -> p c n", c=c)
                        for w in (w_high[:, n % 2, :], w_low[:, first[n], :])]

            pe.wait_ge(S_("x_split"), base_h // 32 * 2 + streams)
            with pe.Fori(0, 4) as i:
                for b in range(2):
                    pe.wait_ge(S_("w_split"), 4 * i + (16 * l + b + 1))
                    wh, wl = parts(b, KC)
                    for j in range(4):
                        k = 4 * b + j
                        pe.wait_ge(S_("relu_ready"), i * 8 + (base_h + k + 1))
                        for c in range(KC):
                            part = slice(j * P, (j + 1) * P)
                            ins = product(psum[k % 2][:, 0:T], (wh[:, c, part], wl[:, c, part]),
                                          (x_high[:, c, 0:T], x_low[:, c, 0:T]), c == 0,
                                          c == KC - 1)
                        if j < 3:
                            ins.then_inc(S_("hidden_full"), 1)
                        else:
                            ins.then_inc(weights_used, 1)
                for b in range(2):
                    pe.wait_ge(S_("w_split"), 4 * i + (16 * l + b + 3))
                    wh, wl = parts(2 + b, 4)
                    pe.wait_ge(S_("hidden_ready"), i * 8 + (base_h + 2 + 4 * (b + 1)))
                    for t in range(tiles):
                        for half in range(2):
                            k = (b * tiles + t) * 2 + half
                            pe.wait_ge(S_("out_added"), i * (4 * tiles) + (base_o + k + 5))
                            for c in range(4):
                                row = slice(t * P, (t + 1) * P)
                                part = slice(half * 512, (half + 1) * 512)
                                ins = product(psum[2 + k % 4][:, :],
                                              (h_high[:, b, c, row], h_low[:, b, c, row]),
                                              (wh[:, c, part], wl[:, c, part]), c == 0, c == 3)
                            if (t, half) == (tiles - 1, 1):
                                ins.then_inc(weights_used, 1)
                            else:
                                ins.then_inc(S_("out_full"), 1)

        post_rows("rows_mix0", 2)
        pe.wait_ge(S_("bands_landed"), 16)
        for s in range(2):
            for t in range(NT):
                xs2_ready(t)
            for c in range(KC):
                name = (("pool_d", s), c // 2)
                ps = take(pe, name, 4 + c // 2) if c % 2 == 0 else ps
                for t in range(NT):
                    ins = mm(ps[:, (c % 2) * S:(c % 2 + 1) * S],
                             xs2[:, 2 * s + t, c * P:(c + 1) * P], band[:, c // 2, t, :],
                             start=t == 0, stop=t == NT - 1)
                if c % 2:
                    fill(ins, name)
        pe.wait_ge(S_("pool_w_ready"), 1)
        w = ring[:, items[("mix2", 0, 0)][0], 0:2048].rearrange("p (g k e) -> p g k e", g=4, k=2)
        for t in range(2 * NT):
            for b in range(4):
                freed(pe, (("pool_d", t // 2), b))
            for half in range(2):
                name = ("pool_y", t, half)
                ps = take(pe, name, 2 * (t % 2) + half)
                for g in (2 * half, 2 * half + 1):
                    for k in range(2):
                        ins = mm(ps[:, (g % 2) * S:(g % 2 + 1) * S],
                                 diffT[:, 2 * g + k, t * P:(t + 1) * P], w[:, g, k, :],
                                 start=k == 0, stop=k == 1)
                if (t, half) == (2 * NT - 1, 1):
                    fill_and_release(ins, name, ("mix2", 0, 0))
                else:
                    fill(ins, name)
        post_rows("rows_mlp0", 2)
        for s in range(2):
            transposes(("xm0", s), lambda t, s=s: xs2[:, 2 * s + t, :], xs2_ready,
                       first=(4, 0)[s])
        for b in range(8):
            pe.wait_ge(bank_free[b], frees[b])
        mlp(0, 2)

        def project(t, n, name, bank, it, last):
            w = wait_landed(pe, it).rearrange("p (c n) -> p c n", c=KC)
            ps = take(pe, name, bank)
            for c in range(KC):
                ins = mm(ps[:, :], xT2[:, c, t * P:(t + 1) * P], w[:, c, :], start=c == 0,
                         stop=c == KC - 1)
            if last:
                fill_and_release(ins, name, it)
            else:
                fill(ins, name)

        pe.wait_ge(S_("relu_ready"), hid_done[1] + 2)
        transposes(("xa", 0), lambda t: xs2[:, t, :], xs2_ready, first=6)
        pe.wait_ge(S_("out_added"), out_done[1] + 8)
        for b in range(4):
            wait_turned(2 * b)
        for t in range(NT):
            for n in range(2):
                project(t, n, ("q", n, t), 2 + 2 * n + t, ("mix2", 1, n), t == NT - 1)
            if t == 0:
                transposes(("xa", 1), lambda t: xs2[:, NT + t, :], xs2_ready, first=6)
        for b in range(4):
            wait_turned(2 * b)
        for t in range(2 * NT):
            project(t, 2, ("kv", t), 2 + t, ("mix2", 1, 2), t == 2 * NT - 1)
        pe.wait_ge(S_("q_rot_ready"), NT)
        for pair in range(4):
            name = ("qT", pair)
            ps = take(pe, name, pair)
            for head in (2 * pair, 2 * pair + 1):
                for t in range(NT):
                    at_ = (head % 2) * S + t * P
                    ins = turn(ps[:, at_:at_ + P], qr[:, t, head * P:(head + 1) * P], ident)
            fill(ins, name)
        pe.wait_ge(S_("k_rot_ready"), 2 * NT)
        for g in range(NKV):
            name = ("kT", g)
            ps = take(pe, name, 4 + g)
            for t in range(2 * NT):
                ins = turn(ps[:, t * P:(t + 1) * P], kv[:, t, 0, g * P:(g + 1) * P], ident)
            fill(ins, name)
        for pair in range(4):
            freed(pe, ("qT", pair))
        for g in range(NKV):
            freed(pe, ("kT", g))

        def scores(u):
            head, t = divmod(u, NT)
            name = ("s", u)
            ps = take(pe, name, (0, 1, 6, 7)[u % 4])
            ins = mm(ps[:, :], qT2[:, head, t * P:(t + 1) * P], kT2[:, head // 4, :],
                     start=True, stop=True)
            fill(ins, name)

        def turn_probs(u):
            name = ("pT", u)
            pe.wait_ge(S_("prob_ready"), u + 1)
            ps = take(pe, name, 2 + u % 2)
            for j in range(4):
                ins = turn(ps[:, j * P:(j + 1) * P], pr[:, u % 2, j * P:(j + 1) * P], ident)
            fill(ins, name)

        def values(head):
            name = ("o", head)
            freed(pe, ("pT", 2 * head))
            freed(pe, ("pT", 2 * head + 1))
            ps = take(pe, name, 4 + head % 2)
            g = head // 4
            for j in range(4):
                ins = mm(ps[:, 0:S], kv[:, j, 1, g * P:(g + 1) * P], prT[:, j, :],
                         start=j == 0, stop=j == 3)
            fill(ins, name)

        scores(0)
        scores(1)
        for u in range(NQ * NT):
            if u + 2 < NQ * NT:
                scores(u + 2)
            turn_probs(u)
            if u % 2:
                values(u // 2)
        post_rows("rows_mix1", 1)
        post_rows("rows_mlp1", 1)
        freed(pe, ("o", NQ - 2))
        freed(pe, ("o", NQ - 1))
        for t in range(NT):
            for n in range(2):
                it = ("mix2", 1, 3 + n)
                w = wait_landed(pe, it).rearrange("p (c n) -> p c n", c=KC)
                name = ("wo", n, t)
                ps = take(pe, name, 4 + 2 * n + t)
                for c in range(KC):
                    ins = mm(ps[:, :], oT[:, c, t * P:(t + 1) * P], w[:, c, :], start=c == 0,
                             stop=c == KC - 1)
                if t == NT - 1:
                    fill_and_release(ins, name, it)
                else:
                    fill(ins, name)
        transposes(("xm1", 0), lambda t: xs2[:, t, :], xs2_ready, first=0)
        for b in range(8):
            pe.wait_ge(bank_free[b], frees[b])
        mlp(1, 1)

    @block.scalar
    def _(act):
        turn = InTurn(act, "act_step")
        raw = nc.scalar.activation
        f, step, free = turn(raw), turn.tick, turn.free
        seen = {}

        def expect(name, k=1):
            seen[name] = seen.get(name, 0) + k
            act.wait_ge(S_(name), seen[name])

        def norm_stats(tiles, ready, src, junk, width=D, first=0):
            for t in range(tiles):
                ready(t)
                step(f(junk(t), src(t), ACT.Square, accum_out=ssq[:, first + t:first + t + 1]))
            cols_ = slice(first, first + tiles)
            f(std[:, cols_], ssq[:, cols_], ACT.Sqrt, bias=eps[:, :],
              scale=1.0 / width).then_inc(S_("std_ready"), 1)

        def odd_chunks(tag, out, gain, shift=None):
            for b in (1, 3):
                ps = full(act, (tag, b))
                for c in (2 * b, 2 * b + 1):
                    kw = {} if shift is None else {"bias": shift(c)}
                    at_ = (c % 2) * S
                    ins = f(out(c), ps[:, at_:at_ + S], ACT.Identity, scale=gain(c), **kw)
                    if c % 2 == 0:
                        step(ins)
                free(ins, (tag, b))

        act.dma_start(ident_all[:, :], consts).then_inc(S_("consts"), 16)
        act.dma_start(col[:, :], cols).then_inc(S_("cols"), 16)
        act.dma_start(AD[:, :, :].rearrange("p a b -> p (a b)")[:, 0:len(LEVELS) * P],
                      masks).then_inc(S_("masks"), 16)
        act.wait_ge(S_("ones_ready"), 1)
        act.wait_ge(S_("cols"), 16)
        expect("lower_shifted")
        f(lb[:, 2, :, :], lb[:, 2, :, :], ACT.Exp).then_inc(S_("lower_exp"), 1)
        for i, name in enumerate(("c", "c_ctx")):
            f(cT[:, :, i], C(name), ACT.Silu).then_inc(S_("silu_c_ready"), 1)

        def x_tile_ready(l):
            def ready(t):
                if l == 0:
                    act.wait_ge(S_("x_landed"), 16)
                else:
                    for half in range(2):
                        freed(act, ("moe", l - 1, 2 * half + t))
            return ready

        for l in range(DEPTH):
            norm_stats(NT, x_tile_ready(l), lambda t: h[:, t, :], lambda t: xs[:, t, :])
            odd_chunks(("x1", l), lambda c: xT[:, c, :], lambda c: C("norm1_g", KC * l + c))
            for d, kind in enumerate((HFF, HFB)):
                for pair in range(2):
                    name = ("proj", l, kind, pair)
                    ps = full(act, name)
                    part = slice(2 * pair, 2 * pair + 2)
                    z = ps[:, :].rearrange("p (a t) -> p a t", a=2)
                    step(f(hf[:, d, part, :], z, ACT.Sigmoid))
                    free(f(hk[:, d, part, :], z, ACT.Sigmoid, scale=-1.0), name)
                if l == 0 and d == 0:
                    expect("lower_ready")
                for head in range(H4):
                    step(f(hf[:, d, head, :], hf[:, d, head, :], ACT.Identity,
                           scale=lb[:, 1, l, head:head + 1], bias=lb[:, 0, l, head:head + 1]))
                    ins = f(hk[:, d, head, :], hk[:, d, head, :], ACT.Identity,
                            scale=lb[:, 2, l, head:head + 1])
                    if head < H4 - 1:
                        step(ins)
                ins.then_inc(S_("forget_ready"), 1)
                for pair in range(2):
                    name = ("retT", l, d, pair)
                    ps = full(act, name)
                    free(f(retT[:, d, 2 * pair:2 * pair + 2, :],
                           ps[:, :].rearrange("p (a t) -> p a t", a=2), ACT.Copy), name)
            for pair in range(2):
                name = ("proj", l, HQ, pair)
                ps = full(act, name)
                free(f(hq[:, 2 * pair:2 * pair + 2, :],
                       ps[:, :].rearrange("p (a t) -> p a t", a=2), ACT.Silu), name)
            act.wait_ge(S_("masks_ready"), 1)
            for t in range(2):
                name = ("same", l, t)
                ps = full(act, name)
                free(f(AD[:, 4 * t:4 * t + 4, :], ps[:, :].rearrange("p (a t) -> p a t", a=4),
                       ACT.Copy), name)
            where = {RV: ret_v, HI: hg_v, RG: ret_gate, HG: hg_gate}
            u, ada_n = 0, 0
            for n, kind in enumerate(mixer_items()):
                if kind == ADA:
                    name = ("ada", l, ada_n)
                    ps = full(act, name)
                    free(f(ada_s[:, :], ps[:, :], ACT.Copy), name)
                    ada_n += 1
                elif kind in where:
                    for t in range(NT):
                        name = ("proj", l, kind, t)
                        ps = full(act, name)
                        func = ACT.Silu if kind in (RG, HG) else ACT.Copy
                        free(f(where[kind][:, t, :], ps[:, :], func), name)
                        for _ in range(2):
                            if units[u][0] == P:
                                name = ("unit", l, u)
                                ps = full(act, name)
                                free(f(AO[:, units[u][1], :, :],
                                       ps[:, :].rearrange("p (a t) -> p a t", a=H4),
                                       ACT.Copy), name)
                            u += 1
                if kind == HG:
                    for t in range(NT):
                        name = ("ret_o", l, t)
                        ps = full(act, name)
                        f(sq[:, t, :], ps[:, :], ACT.Square).then_inc(S_("ret_sq_ready"), 1)
                    for t in range(NT):
                        name = ("hgrn_o", l, t)
                        ps = full(act, name)
                        step(f(xs[:, t, W4:D], ps[:, :], ACT.Square,
                               accum_out=ssq[:, t:t + 1]))
                    f(std[:, 0:NT], ssq[:, 0:NT], ACT.Sqrt, bias=eps[:, :],
                      scale=1.0 / W4).then_inc(S_("std_ready"), 1)
                    expect("ret_sum_ready")
                    f(rstat[:, 1, :, :], rstat[:, 0, :, :], ACT.Sqrt, bias=eps[:, :],
                      scale=1.0 / P).then_inc(S_("ret_std_ready"), 1)

            def mix_gain(c):
                return C("ret_g", H4 * l + c) if c < H4 else C("hgrn_g", H4 * l + c - H4)

            odd_chunks(("mix", l), lambda c: xT[:, c, :], mix_gain)

            def out_ready(t):
                for n in range(2):
                    freed(act, ("w_out", l, n, t))

            norm_stats(NT, out_ready, lambda t: h[:, t, :], lambda t: xs[:, t, :])
            odd_chunks(("x2", l), lambda c: xT[:, c, :], lambda c: C("norm2_g", KC * l + c))
            expect("router_max_ready")
            name = ("logit", l)
            ps = full(act, name)
            for t in range(NT):
                ins = f(logit[:, t, :], ps[:, t * NEXP:(t + 1) * NEXP], ACT.Exp,
                        bias=rstats[:, t, 1:2], accum_out=rstats[:, t, 2:3])
                if t == 0:
                    step(ins)
            free(ins, name)
            with act.Fori(0, NEXP) as e:
                done = l * NEXP + e
                act.wait_ge(S_("gate_T_full"), done + 2)
                act.wait_ge(S_("scattered"), done + 1)
                raw(GT[:, :], psum[5][:, 0:S], ACT.Copy).then_inc(S_("gate_T_ready"), 1)
                act.wait_ge(weights_used, 6 * e + (moe_base[l] + 4))
                raw(silu_g[:, :], psum[4][:, 0:256], ACT.Silu).then_inc(S_("silu_g_ready"), 1)
                act.wait_ge(S_("hid_T_full"), done + 1)
                raw(hidT[:, :, :], psum[6][:, 0:S].rearrange("p (a b) -> p a b", a=2),
                  ACT.Copy).then_inc(S_("hid_T_ready"), 1)
                act.wait_ge(weights_used, 6 * e + (moe_base[l] + 6))
                raw(Y[:, 0:512], psum[5][:, :], ACT.Copy).then_inc(S_("y_left_ready"), 1)

        norm_stats(NT, x_tile_ready(DEPTH), lambda t: h[:, t, :], lambda t: xs2[:, t, :])

        def row_of(tag, i, row):
            for half in range(2):
                name = (tag, i, half)
                ps = full(act, name)
                free(f(rows[:, row, half * 512:(half + 1) * 512], ps[:, :], ACT.Copy), name)

        def next_rows(t):
            expect("x4_ready")

        def pre_norm(first, tiles=NT):
            norm_stats(tiles, next_rows, lambda t: x4[:, first + t, :],
                       lambda t: xs2[:, first + t, :], first=first)

        def post_norm(first, tiles=NT, ready=lambda t: expect("ys_ready")):
            norm_stats(tiles, ready, lambda t: ys[:, first + t, :],
                       lambda t: xs2[:, first + t, :], first=first)

        def odd_modulated(tag, s, l, which):
            odd_chunks((tag, s), lambda c: xT2[:, c, s * S:(s + 1) * S],
                       lambda c: mod_gain[:, l, which, s, c:c + 1],
                       lambda c: mods[:, l, 3 * which * KC + c, s:s + 1])

        def mlp(l, T):
            base_h, base_i = hid_done[l], mlp_base[l]

            def high(i, n):
                slot, number, value = items[("mlp", l, n % 4)]
                shift = n // 4
                act.wait_ge(landed[slot], per_item[l] * (i + shift) + value)
                act.wait_ge(weights_used, 4 * (i + shift) + (number - 1))
                raw(w_high[:, n % 2, :], ring[:, slot, :],
                    ACT.Copy).then_inc(S_("w_high_ready"), 1)

            def relus(i, b, units):
                for j in units:
                    if j < 3:
                        act.wait_ge(S_("hidden_full"), 6 * i + (24 * l + 3 * b + j + 1))
                    else:
                        act.wait_ge(weights_used, 4 * i + (base_i + b + 1))
                    act.wait_ge(S_("hidden_ready"), 8 * i + (base_h + 4 * b + j + 1))
                    raw(h_raw[:, j % 2, 0:T], psum[(4 * b + j) % 2][:, 0:T],
                        ACT.Relu).then_inc(S_("relu_ready"), 1)

            def blocks(i, last):
                for n in range(4):
                    if n < 2:
                        relus(i, n, (0,))
                    if not (last and n == 3):
                        high(i, n + 1)
                    if n < 2:
                        relus(i, n, (1, 2, 3))

            high(0, 0)
            with act.Fori(0, 3) as i:
                blocks(i, False)
            blocks(3, True)
            turn.mine = None

        def high_modulated(tag, s, l):
            for b in (1, 3):
                ps = full(act, ((tag, s), b))
                for out_ in (x_full, x_high):
                    for c in (2 * b, 2 * b + 1):
                        at_ = (c % 2) * S
                        ins = f(out_[:, c, s * S:(s + 1) * S], ps[:, at_:at_ + S], ACT.Identity,
                                scale=mod_gain[:, l, 1, s, c:c + 1],
                                bias=mods[:, l, 3 * KC + c, s:s + 1])
                        if out_ is x_full or c % 2 == 0:
                            step(ins)
                free(ins, ((tag, s), b))

        pre_norm(0)
        act.wait_ge(S_("ctx_landed"), 16)
        norm_stats(NT, lambda t: None, lambda t: x4[:, 2 + t, :], lambda t: xs2[:, 2 + t, :],
                   first=2)
        for s in range(2):
            row_of("rows_mix0", s, s)
        for s in range(2):
            odd_chunks(("pool_d", s), lambda c, s=s: diffT[:, c, s * S:(s + 1) * S],
                       lambda c, s=s: mod_gain[:, 0, 0, s, c:c + 1])
        for t in range(2 * NT):
            for half in range(2):
                name = ("pool_y", t, half)
                ps = full(act, name)
                free(f(ys[:, t, half * 512:(half + 1) * 512], ps[:, :], ACT.Copy), name)
            if t % NT:
                post_norm(t - 1, ready=lambda t: None)
        act.wait_ge(S_("pool_w_ready"), 1)
        row_of("rows_mlp0", 0, 2)
        pre_norm(0)
        row_of("rows_mlp0", 1, 0)
        pre_norm(2)
        for s in range(2):
            high_modulated("xm0", s, 0)
        mlp(0, 2 * S)
        post_norm(0)
        pre_norm(0)
        post_norm(2)
        odd_modulated("xa", 0, 1, 0)
        pre_norm(2)
        for t in range(NT):
            for n in range(2):
                name = ("q", n, t)
                ps = full(act, name)
                part = slice(n * 512, (n + 1) * 512)
                step(f(q_raw[:, t, part], ps[:, :], ACT.Copy))
                free(f(q_sq[:, t, part], ps[:, :], ACT.Square), name)
            if t == 0:
                odd_modulated("xa", 1, 1, 0)
            expect("q_sum_ready")
            heads = slice(t * NQ, (t + 1) * NQ)
            f(qst[:, 1, heads], qst[:, 0, heads], ACT.Sqrt, bias=eps[:, :],
              scale=1.0 / P).then_inc(S_("q_std_ready"), 1)
        for t in range(2 * NT):
            name = ("kv", t)
            ps = full(act, name)
            step(f(kv[:, t, :, :], ps[:, :].rearrange("p (a b) -> p a b", a=2), ACT.Copy))
            free(f(xs2[:, t, 0:2 * P], ps[:, 0:2 * P], ACT.Square), name)
            expect("k_sum2_ready")
            heads = slice(t * NKV, (t + 1) * NKV)
            f(kst[:, 1, heads], kst[:, 0, heads], ACT.Sqrt, bias=eps[:, :],
              scale=1.0 / P).then_inc(S_("k_std_ready"), 1)
        for pair in range(4):
            name = ("qT", pair)
            ps = full(act, name)
            free(f(qT2[:, 2 * pair:2 * pair + 2, :], ps[:, :].rearrange("p (a t) -> p a t", a=2),
                   ACT.Copy), name)

        def exponentials(u):
            expect("score_max_ready")
            name = ("s", u)
            ps = full(act, name)
            free(f(pr[:, u % 2, :], ps[:, :], ACT.Exp, bias=soft[:, u % 4, 1:2],
                   scale=HEAD_SCALE, accum_out=soft[:, u % 4, 2:3]), name)

        exponentials(0)
        for u in range(NQ * NT):
            if u + 1 < NQ * NT:
                exponentials(u + 1)
            name = ("pT", u)
            ps = full(act, name)
            t = u % NT
            free(f(prT[:, :, t * P:(t + 1) * P], ps[:, :].rearrange("p (a t) -> p a t", a=4),
                   ACT.Copy), name)
        row_of("rows_mix1", 0, 0)
        row_of("rows_mlp1", 0, 1)
        for t in range(NT):
            for n in range(2):
                name = ("wo", n, t)
                ps = full(act, name)
                free(f(ys[:, t, n * 512:(n + 1) * 512], ps[:, :], ACT.Copy), name)
            post_norm(t, 1, ready=lambda t: None)
            pre_norm(t, 1)
        high_modulated("xm1", 0, 1)
        mlp(1, S)
        for t in range(NT):
            post_norm(t, 1)

    @block.vector
    def _(dve):
        turn = InTurn(dve, "dve_step")
        tick, step, free = turn.tick, turn.tick, turn.free
        v = nc.vector
        tt, ts, stt = turn(v.tensor_tensor), turn(v.tensor_scalar), turn(v.scalar_tensor_tensor)
        copy, reciprocal, reduce = turn(v.tensor_copy), turn(v.reciprocal), turn(v.tensor_reduce)
        memset, top8, top8_at = turn(v.memset), turn(v.max), turn(v.max_index)
        replace, copy_where = turn(v.match_replace), turn(v.copy_predicated)
        seen = {}

        def expect(name, k=1):
            seen[name] = seen.get(name, 0) + k
            dve.wait_ge(S_(name), seen[name])

        def normalise(tiles, src, out, signal, first=0):
            expect("std_ready")
            step(reciprocal(rinv[:, first:first + tiles], std[:, first:first + tiles]))
            for t in range(tiles):
                ts(out(t), src(t), rinv[:, first + t:first + t + 1], None,
                   ALU.mult).then_inc(S_(signal), 1)

        def even_chunks(tag, out, gain, shift=None):
            for b in (0, 2):
                ps = full(dve, (tag, b))
                for c in (2 * b, 2 * b + 1):
                    at_ = (c % 2) * S
                    if shift is None:
                        ins = ts(out(c), ps[:, at_:at_ + S], gain(c), None, ALU.mult)
                    else:
                        ins = ts(out(c), ps[:, at_:at_ + S], gain(c), shift(c), ALU.mult,
                                 ALU.add)
                    if c % 2 == 0:
                        tick(ins)
                free(ins, (tag, b))

        dve.wait_ge(S_("cols"), 16)
        low = C("lower").rearrange("p (l h) -> p l h", l=DEPTH)
        step(tt(lb[:, 0, 0, :], low[:, 0, :], low[:, 1, :], ALU.max))
        tt(lb[:, 2, :, :], low, lb[:, 0, 0:1, :].broadcast_to([P, DEPTH, H4]),
           ALU.subtract).then_inc(S_("lower_shifted"), 1)
        expect("lower_exp")
        step(tt(lb[:, 0, 0, :], lb[:, 2, 0, :], lb[:, 2, 1, :], ALU.add))
        step(reciprocal(lb[:, 0, 1, :], lb[:, 0, 0, :]))
        step(tt(lb[:, 1, :, :], lb[:, 2, :, :], lb[:, 0, 1:2, :].broadcast_to([P, DEPTH, H4]),
                ALU.mult))
        step(tt(lb[:, 0, 1, :], lb[:, 1, 0, :], lb[:, 1, 1, :], ALU.add))
        tick(tt(lb[:, 0, 0, :], lb[:, 1, 0, :], lb[:, 1, 0, :], ALU.subtract))
        step(tt(lb[:, 0, 1, :], lb[:, 0, 1, :], lb[:, 1, 0, :], ALU.subtract))
        step(ts(lb[:, 1, :, :], lb[:, 0, :, :], -1.0, 1.0, ALU.mult, ALU.add))
        ts(lb[:, 2, :, :], lb[:, 1, :, :], HEAD_SCALE, None,
           ALU.mult).then_inc(S_("lower_ready"), 1)
        dve.wait_ge(S_("masks"), 16)
        copy(mask[:, :, :, :].rearrange("p a b c -> p (a b c)"),
             AD[:, :, :].rearrange("p a b -> p (a b)")[:, 0:len(LEVELS) * P]).then_inc(
            S_("masks_ready"), 1)
        dve.wait_ge(S_("x_landed"), 16)

        for l in range(DEPTH):
            normalise(NT, lambda t: h[:, t, :], lambda t: xs[:, t, :], "xs_ready")
            even_chunks(("x1", l), lambda c: xT[:, c, :], lambda c: C("norm1_g", KC * l + c))
            dve.wait_ge(S_("consts"), 16)
            cos = K("cos").rearrange("p (t d) -> p t d", t=NT)
            sin = K("sin").rearrange("p (t b d) -> p t b d", t=NT, b=2)
            for i, kind in enumerate((RQ, RK)):
                for t in range(NT):
                    name = ("proj", l, kind, t)
                    ps = full(dve, name)
                    rows_ = ps[:, :].rearrange("p (h d) -> p h d", h=H4)
                    halves = ps[:, :].rearrange("p (h b d) -> p h b d", h=H4, b=2)
                    tick(tt(rope_t[:, 0, :].rearrange("p (h d) -> p h d", h=H4), rows_,
                            cos[:, t, :].unsqueeze(1).broadcast_to([P, H4, P]), ALU.mult))
                    for b in range(2):
                        ins = tt(rope_t[:, 1, :].rearrange("p (h b d) -> p h b d", h=H4, b=2)
                                 [:, :, b, :], halves[:, :, 1 - b, :],
                                 sin[:, t, b, :].unsqueeze(1).broadcast_to([P, H4, 64]), ALU.mult)
                        if b == 0:
                            tick(ins)
                    free(ins, name)
                    tt(rot[:, i, t, :], rope_t[:, 0, :], rope_t[:, 1, :],
                       ALU.add).then_inc(S_("rot_ready"), 1)
            expect("forget_ready", 2)
            tt(hx[:, 0, :, :], hk[:, 0, :, :], hk[:, 1, :, :],
               ALU.add).then_inc(S_("k_sum_ready"), 1)
            decay = K("decay").rearrange("p (h c) -> p h c", h=H4)
            for head in range(H4):
                name = ("ret_s", l, head)
                ps = full(dve, name)
                tick(tt(RS_[:, 0, head, :], ps[:, 0:S], decay[:, head, P:3 * P], ALU.mult))
                free(tt(RS_[:, 1, head, :], ps[:, S:2 * S], decay[:, head, 0:2 * P], ALU.mult),
                     name)

            def split(x, m):
                return x.rearrange("p h (n b m) -> p (h n) b m", b=2, m=m)

            def prepare(u):
                m, d = units[u]
                q_half, k_half = (1, 0) if d == 0 else (0, 1)
                if m > 1:
                    if u == 2:
                        expect("kdec_ready")
                    if m == P:
                        part = slice(k_half * P, (k_half + 1) * P)
                        tick(tt(kdec[:, d, :, part], hk[:, d, :, part], hx[:, d, :, part],
                                ALU.mult))
                    else:
                        tick(tt(split(kdec[:, d, :, :], m)[:, :, k_half, :],
                                split(hk[:, d, :, :], m)[:, :, k_half, :],
                                split(hx[:, d, :, :], m)[:, :, k_half, :], ALU.mult))
                if m == P:
                    part = slice(q_half * P, (q_half + 1) * P)
                    ins = tt(qdec[:, d, :, :], hq[:, :, part], hf[:, d, :, part], ALU.mult)
                else:
                    ins = tt(qdec[:, d, :, :].rearrange("p h (n m) -> p (h n) m", m=m),
                             split(hq[:, :, :], m)[:, :, q_half, :],
                             split(hf[:, d, :, :], m)[:, :, q_half, :], ALU.mult)
                ins.then_inc(S_("level_ready"), 1)

            def widen(u):
                m, d = units[u]
                q_half, k_half = (1, 0) if d == 0 else (0, 1)
                prod, excl = split(hf[:, d, :, :], m), split(hx[:, d, :, :], m)
                shape = [P, H4 * S // (2 * m), m]
                end = m - 1 if d == 0 else 0
                whole_q = prod[:, :, q_half, end:end + 1]
                whole_k = prod[:, :, k_half, end:end + 1]
                if m == 1:
                    tick(memset(excl[:, :, q_half, :], 1.0))
                    tick(copy(excl[:, :, k_half, :], whole_q))
                else:
                    tick(tt(excl[:, :, k_half, :], excl[:, :, k_half, :],
                            whole_q.broadcast_to(shape), ALU.mult))
                tick(tt(prod[:, :, q_half, :], prod[:, :, q_half, :],
                                  whole_k.broadcast_to(shape), ALU.mult))

            def merge(u):
                m, d = units[u]
                name = ("unit", l, u)
                ps = full(dve, name)
                q_half = 1 if d == 0 else 0
                blocks = P // (2 * m)
                outs = AD[:, :, :].rearrange("p a (n b m) -> p a n b m", b=2, m=m)
                wide = [P, 2 * H4, blocks, m]
                where = mask[:, LEVELS.index(m), d, :].rearrange("p (n m) -> p n m", m=m)
                free(copy_where(outs[:, :, :, q_half, :],
                                       where.unsqueeze(1).broadcast_to(wide),
                                       ps[:, :].rearrange("p (a n m) -> p a n m", a=2 * H4, m=m)),
                     name)

            def ada_bias(n):
                name = ("ada_c", l, n)
                ps = full(dve, name)
                bias = C("b_ada", NMOD * KC * l + 4 * n, 4)
                free(tt(mods[:, l, 4 * n:4 * n + 4, :],
                        ps[:, 0:8].rearrange("p (a b) -> p a b", b=2),
                        bias.unsqueeze(2).broadcast_to([P, 4, 2]), ALU.add), name)

            for pair in range(2):
                freed(dve, ("proj", l, HQ, pair))
                freed(dve, ("same", l, pair))
            u, ada_n = 0, 0

            def one_unit(u):
                prepare(u)
                if units[u][0] < P:
                    widen(u)
                if 1 <= u <= 2 * len(LEVELS):
                    merge(u - 1)

            for kind in mixer_items()[5:]:
                if kind == ADA:
                    if ada_n:
                        ada_bias(ada_n - 1)
                    ada_n += 1
                else:
                    for _ in range(4):
                        one_unit(u)
                        u += 1
                if kind == HG:
                    for t in range(NT):
                        expect("ret_sq_ready")
                        ins = reduce(rstat[:, 0, t, :],
                                              sq[:, t, :].rearrange("p (h d) -> p h d", h=H4),
                                              AX.X, ALU.add)
                        if t == 0:
                            tick(ins)
                    ins.then_inc(S_("ret_sum_ready"), 1)
                    expect("std_ready")
                    step(reciprocal(rinv[:, 0:NT], std[:, 0:NT]))
                    for t in range(NT):
                        name = ("hgrn_o", l, t)
                        ps = full(dve, name)
                        freed(dve, ("proj", l, HG, t))
                        free(stt(xs[:, t, W4:D], ps[:, :], rinv[:, t:t + 1], hg_gate[:, t, :],
                                 ALU.mult, ALU.mult), name)
                    expect("ret_std_ready")
                    step(reciprocal(rstat[:, 2, :, :], rstat[:, 1, :, :]))
                    for t in range(NT):
                        freed(dve, ("proj", l, RG, t))
                        gate = ret_gate[:, t, :].rearrange("p (h d) -> p h d", h=H4)
                        step(tt(gate, gate, rstat[:, 2, t, :].unsqueeze(2)
                                .broadcast_to([P, H4, P]), ALU.mult))
                        name = ("ret_o", l, t)
                        free(tt(xs[:, t, 0:W4], psum[where_is[name][0]][:, :],
                                ret_gate[:, t, :], ALU.mult), name)
            ada_bias(ada_n - 1)
            if l == DEPTH - 1:
                for l2 in range(DEPTH):
                    for which, pre in enumerate(("g_mix_pre", "g_mlp_pre")):
                        for s in range(2):
                            at_ = (3 * which + 1) * KC
                            tick(stt(mod_gain[:, l2, which, s, :],
                                     mods[:, l2, at_:at_ + KC, s], 1.0, C(pre, KC * l2, KC),
                                     ALU.add, ALU.mult))

            def mix_gain(c):
                return C("ret_g", H4 * l + c) if c < H4 else C("hgrn_g", H4 * l + c - H4)

            even_chunks(("mix", l), lambda c: xT[:, c, :], mix_gain)
            for n in range(2):
                for t in range(NT):
                    name = ("w_out", l, n, t)
                    ps = full(dve, name)
                    part = slice(n * 512, (n + 1) * 512)
                    free(tt(h[:, t, part], h[:, t, part], ps[:, :], ALU.add), name)

            normalise(NT, lambda t: h[:, t, :], lambda t: xs[:, t, :], "xs_ready")
            even_chunks(("x2", l), lambda c: xT[:, c, :], lambda c: C("norm2_g", KC * l + c))
            name = ("logit", l)
            ps = full(dve, name)
            step(reduce(rstats[:, :, 0], ps[:, 0:NT * NEXP]
                                 .rearrange("p (t e) -> p t e", t=NT), AX.X, ALU.max))
            ts(rstats[:, :, 1], rstats[:, :, 0], -1.0, None,
               ALU.mult).then_inc(S_("router_max_ready"), 1)
            freed(dve, name)
            step(reciprocal(rstats[:, :, 3], rstats[:, :, 2]))
            for t in range(NT):
                ts(aff[:, t, :], logit[:, t, :], rstats[:, t, 3:4], None,
                   ALU.mult).then_inc(S_("affinity_ready"), 1)
            name = ("affT", l)
            ps = full(dve, name)
            free(copy(affT[:, 0, :], ps[0:NEXP, 0:S]), name)
            freed(dve, name)
            for r in range(CAP // 8):
                part = slice(8 * r, 8 * r + 8)
                a, b = affT[:, r % 2, :], affT[:, 1 - r % 2, :]
                step(top8(top[:, part], a))
                tick(top8_at(topi[:, part], top[:, part], a))
                if r < CAP // 8 - 1:
                    tick(replace(b, top[:, part], a, -1.0))
            step(copy(topf[:, :], topi[:, :]))
            delta = K("delta")[0:NEXP, :].unsqueeze(2).broadcast_to([NEXP, NEXP, CAP])
            for i, what in enumerate((topf, top)):
                tt(spread[:, i, :, :], what[:, :].unsqueeze(1).broadcast_to([NEXP, NEXP, CAP]),
                   delta, ALU.mult).then_inc(S_("spread_ready"), 1)
            name = ("spread", l, 0)
            ps = full(dve, name)
            for t in range(NT):
                ins = ts(onehot[:, t, :], ps[:, :], K("token")[:, t:t + 1], None, ALU.is_equal)
                if t == 0:
                    tick(ins)
            free(ins, name)
            freed(dve, name)
            name = ("spread", l, 1)
            ps = full(dve, name)
            for t in range(NT):
                ins = tt(gated[:, t, :], onehot[:, t, :], ps[:, :], ALU.mult)
                if t == 0:
                    tick(ins)
            free(ins, name)
            freed(dve, name)
            gain2 = C("norm2_g", KC * l, KC).unsqueeze(2).broadcast_to([P, KC, CAP])
            with dve.Fori(0, NEXP) as e:
                done = l * NEXP + e
                dve.wait_ge(S_("gate_T_full"), done + 1)
                nc.vector.tensor_copy(gsel[:, :, :, :], gated[:, :, bass.ds(e * CAP, CAP)].unsqueeze(2)
                              .broadcast_to([P, NT, 4, CAP])).then_inc(S_("gate_sel_ready"), 1)
                dve.wait_ge(S_("gathered"), done + 1)
                nc.vector.tensor_tensor(xeT[:, :, :], psum[7][:, 0:S].rearrange("p (c s) -> p c s", c=KC), gain2,
                   ALU.mult).then_inc(S_("xeT_ready"), 1)
                dve.wait_ge(S_("silu_g_ready"), done + 1)
                dve.wait_ge(weights_used, 6 * e + (moe_base[l] + 4))
                nc.vector.tensor_tensor(hidE[:, :], silu_g[:, :], psum[4][:, 256:512],
                   ALU.mult).then_inc(S_("hid_e_ready"), 1)
                dve.wait_ge(weights_used, 6 * e + (moe_base[l] + 6))
                nc.vector.tensor_copy(Y[:, 512:D], psum[6][:, :]).then_inc(S_("y_right_ready"), 1)
            dve.wait_ge(S_("scattered"), (l + 1) * NEXP + 1)
            for t in range(NT):
                for half in range(2):
                    b = 2 * half + t
                    part = slice(half * 512, (half + 1) * 512)
                    free(tt(h[:, t, part], h[:, t, part], psum[b][:, :], ALU.add), ("moe", l, b))

        expect("std_ready")
        step(reciprocal(rinv[:, 0:NT], std[:, 0:NT]))
        dve.wait_ge(S_("final_g_landed"), 16)
        for t in range(NT):
            stt(x4[:, t, :], h[:, t, :], rinv[:, t:t + 1], gfin[:, :], ALU.mult,
                ALU.mult).then_inc(S_("x4_ready"), 1)

        def normalise_x4(first, tiles=NT):
            normalise(tiles, lambda t: x4[:, first + t, :], lambda t: xs2[:, first + t, :],
                      "xs2_ready", first=first)

        def even_modulated(tag, s, l, which):
            even_chunks((tag, s), lambda c: xT2[:, c, s * S:(s + 1) * S],
                        lambda c: mod_gain[:, l, which, s, c:c + 1],
                        lambda c: mods[:, l, 3 * which * KC + c, s:s + 1])

        def add_branch(tag, i, row, first, tiles=NT):
            freed(dve, (tag, i, 0))
            freed(dve, (tag, i, 1))
            expect("std_ready")
            step(reciprocal(rinv[:, first:first + tiles], std[:, first:first + tiles]))
            for t in range(first, first + tiles):
                tick(stt(ys[:, t, :], ys[:, t, :], rinv[:, t:t + 1], rows[:, row, :],
                         ALU.mult, ALU.mult))
                tt(x4[:, t, :], x4[:, t, :], ys[:, t, :], ALU.add).then_inc(S_("x4_ready"), 1)

        def split_modulated(tag, s, l):
            cols_ = slice(s * S, (s + 1) * S)
            for b in (0, 2):
                ps = full(dve, ((tag, s), b))
                for out_ in (x_full, x_high):
                    for c in (2 * b, 2 * b + 1):
                        at_ = (c % 2) * S
                        ins = ts(out_[:, c, cols_], ps[:, at_:at_ + S],
                                 mod_gain[:, l, 1, s, c:c + 1], mods[:, l, 3 * KC + c, s:s + 1],
                                 ALU.mult, ALU.add)
                        if out_ is x_full or c % 2 == 0:
                            tick(ins)
                free(ins, ((tag, s), b))
            for b in (0, 2, 1, 3):
                if b % 2:
                    freed(dve, ((tag, s), b))
                part = slice(2 * b, 2 * b + 2)
                ins = tt(x_low[:, part, cols_], x_full[:, part, cols_],
                         x_high[:, part, cols_].bitcast(F32), ALU.subtract)
                if b != 3:
                    tick(ins)
            ins.then_inc(S_("x_split"), 1)

        def mlp(l, streams, after):
            T, tiles = streams * S, streams * NT
            base_h, base_o, base_i = hid_done[l], out_done[l], mlp_base[l]
            h_high, h_low = mlp_parts[l]
            vector = nc.vector

            def low(i, n):
                slot = items[("mlp", l, n % 4)][0]
                dve.wait_ge(S_("w_high_ready"), 4 * i + (16 * l + n + 1))
                vector.tensor_tensor(w_low[:, slot, :], ring[:, slot, :],
                                     w_high[:, n % 2, :].bitcast(F32),
                                     ALU.subtract).then_inc(S_("w_split"), 1)

            def squares(i, b, units):
                if 0 in units:
                    dve.wait_ge(weights_used, 4 * i + (base_i - 1 + b))
                for j in units:
                    k = base_h + 4 * b + j
                    dve.wait_ge(S_("relu_ready"), 8 * i + (k + 3))
                    q = h_raw[:, j % 2, 0:T]
                    vector.tensor_tensor(q, q, q, ALU.mult).then_inc(S_("squared"), 1)
                    dve.wait_ge(S_("squared"), 8 * i + (k + 1))
                    vector.tensor_copy(h_high[:, b, j, 0:T], q).then_inc(S_("squared_high"), 1)
                    dve.wait_ge(S_("squared_high"), 8 * i + (k + 1))
                    vector.tensor_tensor(h_low[:, b, j, 0:T], q,
                                         h_high[:, b, j, 0:T].bitcast(F32),
                                         ALU.subtract).then_inc(S_("hidden_ready"), 1)

            def sums(i, b, some):
                for t in some:
                    for half in range(2):
                        k = (b * tiles + t) * 2 + half
                        if (t, half) == (tiles - 1, 1):
                            dve.wait_ge(weights_used, 4 * i + (base_i + 3 + b))
                        else:
                            dve.wait_ge(S_("out_full"), (4 * tiles - 2) * i
                                        + (8 * 7 * l + k - b + 1))
                        dve.wait_ge(S_("out_added"), 4 * tiles * i + (base_o + 9 + k - 2 * tiles))
                        part = slice(half * 512, (half + 1) * 512)
                        vector.tensor_tensor(ys[:, t, part], ys[:, t, part],
                                             psum[2 + k % 4][:, :],
                                             ALU.add).then_inc(S_("out_added"), 1)

            def blocks(i, last):
                for n in range(4):
                    if n < 2:
                        squares(i, n, (0, 1))
                    elif not (last and n == 3):
                        sums(i, n - 2, range(tiles // 2))
                    if not (last and n == 3):
                        low(i, n + 1)
                    if n < 2:
                        squares(i, n, (2, 3))
                    elif not (last and n == 3):
                        sums(i, n - 2, range(tiles // 2, tiles))

            low(0, 0)
            with dve.Fori(0, 3) as i:
                blocks(i, False)
            blocks(3, True)
            turn.mine = None
            for t in range(tiles):
                sums(3, 1, (t,))
                dve.wait_ge(S_("out_added"), base_o + 8 + 16 * tiles - 2 * (tiles - 1 - t))
                memset(soft[:, 0, 3:4], 0.0).then_inc(S_("ys_ready"), 1)
                after(t)

        normalise_x4(0)
        normalise_x4(2)
        for s in range(2):
            even_chunks(("pool_d", s), lambda c, s=s: diffT[:, c, s * S:(s + 1) * S],
                        lambda c, s=s: mod_gain[:, 0, 0, s, c:c + 1])
        add_branch("rows_mix0", 0, 0, 0)
        add_branch("rows_mix0", 1, 1, 2)
        normalise_x4(0)
        normalise_x4(2)
        step(memset(soft[:, :, :], 0.0))
        memset(soft[:, 3, 3:4], 0.0).then_inc(S_("relu_ready"), 2)
        memset(soft[:, 3, 3:4], 0.0).then_inc(S_("hidden_ready"), 2)
        memset(soft[:, 3, 3:4], 0.0).then_inc(S_("out_added"), 8)
        for s in range(2):
            split_modulated("xm0", s, 0)
        dve.wait_ge(S_("ys_cleared"), 1)

        def latents_first(t):
            if t == NT:
                add_branch("rows_mlp0", 0, 2, 0)
            elif t == 2 * NT - 1:
                normalise_x4(0)
                even_modulated("xa", 0, 1, 0)
                add_branch("rows_mlp0", 1, 0, 2)
                normalise_x4(2)
                even_modulated("xa", 1, 1, 0)

        mlp(0, 2, latents_first)

        dve.wait_ge(S_("rope2_landed"), 16)
        dve.wait_ge(S_("gqk_landed"), 16)
        full(dve, ("rows_mlp0", 1, 1))
        for i in range(2):
            g = gqk[:, i, :]
            g4 = g.rearrange("p (a b d) -> p a b d", a=2, b=2)
            tick(tt(rope_g[:, i, 0, :, :], rope_c[:, 0, :, :],
                    g.unsqueeze(1).broadcast_to([P, NT, P]), ALU.mult))
            for t in range(NT):
                sin4 = rope_c[:, 1, t, :].rearrange("p (a b d) -> p a b d", a=2, b=2)
                out4 = rope_g[:, i, 1, t, :].rearrange("p (a b d) -> p a b d", a=2, b=2)
                for b in range(2):
                    tick(tt(out4[:, :, b, :], sin4[:, :, b, :], g4[:, :, 1 - b, :], ALU.mult))
        def rotate(x, t, heads, i, tmp, out):
            quarters = x.rearrange("p (h b d) -> p h b d", h=2 * heads, b=2)
            tmp4 = tmp[1].rearrange("p (h b d) -> p h b d", h=2 * heads, b=2)
            sin4 = rope_g[:, i, 1, t, :].rearrange("p (a b d) -> p a b d", a=2, b=2)
            cos_ = rope_g[:, i, 0, t, :].unsqueeze(1).broadcast_to([P, heads, P])
            tick(tt(tmp[0].rearrange("p (h d) -> p h d", h=heads),
                    x.rearrange("p (h d) -> p h d", h=heads), cos_, ALU.mult))
            for b in range(2):
                for a in range(2):
                    tick(tt(tmp4[:, a::2, b, :], quarters[:, a::2, 1 - b, :],
                                sin4[:, a, b, :].unsqueeze(1).broadcast_to([P, heads, 32]),
                                ALU.mult))
            return tt(out, tmp[0], tmp[1], ALU.add)

        for t in range(NT):
            for n in range(2):
                freed(dve, ("q", n, t))
            heads = slice(t * NQ, (t + 1) * NQ)
            reduce(qst[:, 0, heads], q_sq[:, t, :].rearrange("p (h d) -> p h d", h=NQ), AX.X,
                   ALU.add).then_inc(S_("q_sum_ready"), 1)
            expect("q_std_ready")
            step(reciprocal(qst[:, 2, heads], qst[:, 1, heads]))
            rows_ = q_raw[:, t, :].rearrange("p (h d) -> p h d", h=NQ)
            step(tt(rows_, rows_, qst[:, 2, heads].unsqueeze(2).broadcast_to([P, NQ, P]),
                    ALU.mult))
            rotate(q_raw[:, t, :], t, NQ, 0, (q_tmp[:, 0, :], q_tmp[:, 1, :]),
                   qr[:, t, :]).then_inc(S_("q_rot_ready"), 1)
        for t in range(2 * NT):
            freed(dve, ("kv", t))
            heads = slice(t * NKV, (t + 1) * NKV)
            reduce(kst[:, 0, heads], xs2[:, t, 0:2 * P].rearrange("p (h d) -> p h d", h=NKV),
                   AX.X, ALU.add).then_inc(S_("k_sum2_ready"), 1)
            expect("k_std_ready")
            step(reciprocal(kst[:, 2, heads], kst[:, 1, heads]))
            k_ = kv[:, t, 0, :]
            rows_ = k_.rearrange("p (h d) -> p h d", h=NKV)
            step(tt(rows_, rows_, kst[:, 2, heads].unsqueeze(2).broadcast_to([P, NKV, P]),
                    ALU.mult))
            if t < NT:
                ins = rotate(k_, t, NKV, 1, (q_tmp[:, 0, 0:2 * P], q_tmp[:, 1, 0:2 * P]), k_)
            else:
                ins = tt(rows_, rows_, gqk[:, 1, :].unsqueeze(1).broadcast_to([P, NKV, P]),
                         ALU.mult)
            ins.then_inc(S_("k_rot_ready"), 1)
        for g in range(NKV):
            name = ("kT", g)
            ps = full(dve, name)
            free(copy(kT2[:, g, :], ps[:, :]), name)

        def score_max(u):
            name = ("s", u)
            ps = full(dve, name)
            step(reduce(soft[:, u % 4, 0:1], ps[:, :], AX.X, ALU.max))
            ts(soft[:, u % 4, 1:2], soft[:, u % 4, 0:1], -HEAD_SCALE, None,
               ALU.mult).then_inc(S_("score_max_ready"), 1)

        def take_values(head):
            name = ("o", head)
            ps = full(dve, name)
            free(copy(oT[:, head, :], ps[:, 0:S]), name)

        score_max(0)
        score_max(1)
        for u in range(NQ * NT):
            freed(dve, ("s", u))
            step(reciprocal(soft[:, u % 4, 3:4], soft[:, u % 4, 2:3]))
            ts(pr[:, u % 2, :], pr[:, u % 2, :], soft[:, u % 4, 3:4], None,
               ALU.mult).then_inc(S_("prob_ready"), 1)
            if u + 2 < NQ * NT:
                score_max(u + 2)
            if u >= 2 and u % 2 == 0:
                take_values(u // 2 - 1)
        take_values(NQ - 1)
        for t in range(NT):
            add_branch("rows_mix1", 0, 0, t, 1)
            normalise_x4(t, 1)
        split_modulated("xm1", 0, 1)
        dve.wait_ge(S_("ys_cleared"), 2)

        def tile_by_tile(t):
            if t:
                add_branch("rows_mlp1", 0, 1, t - 1, 1)
            if t == NT - 1:
                add_branch("rows_mlp1", 0, 1, t, 1)

        mlp(1, 1, tile_by_tile)

    @block.gpsimd
    def _(pool):
        g = nc.gpsimd
        turn = InTurn(pool, "pool_step")
        g.memset(ones[:, :], 1.0)
        g.memset(zeros[:, :], 0.0).then_inc(S_("gate_T_full"), 1)
        g.memset(eps[:, :], EPS).then_inc(S_("scattered"), 1)
        g.memset(cT[:, :, :], 0.0).then_inc(S_("ones_ready"), 1)
        for l in range(DEPTH):
            freed(pool, ("ret_s", l, H4 - 1))
            g.memset(kdec[:, :, :, :], 0.0).then_inc(S_("kdec_ready"), 1)
            freed(pool, ("w_out", l, 0, 0))
            g.dma_start(wr[:, :, :], w_router[l].rearrange("(c p) e -> p c e", p=P)).then_inc(
                S_("router_landed"), 16)
        pool.wait_ge(S_("spread_ready"), 2 * DEPTH)
        g.dma_start(gfin[:, :], final_g.partition_broadcast(P)).then_inc(S_("final_g_landed"), 16)
        for b in range(4):
            freed(pool, ("moe", DEPTH - 1, b))
        g.dma_start(band[:, :, :, :].rearrange("p a b c -> p (a b c)"),
                    bands).then_inc(S_("bands_landed"), 16)
        g.dma_start(x4[:, NT:2 * NT, :],
                    ctx_x.rearrange("(t p) d -> p t d", p=P)).then_inc(S_("ctx_landed"), 16)
        g.dma_start(rows[:, 2, :], pool_scale.partition_broadcast(P)).then_inc(
            S_("pool_scale_landed"), 16)
        g.dma_start(rope_c[:, :, :, :].rearrange("p a b c -> p (a b c)"),
                    rope2).then_inc(S_("rope2_landed"), 16)
        g.dma_start(gqk[:, :, :].rearrange("p a b -> p (a b)"),
                    g_qk.partition_broadcast(P)).then_inc(S_("gqk_landed"), 16)

        tt = turn(g.tensor_tensor)

        def diagonal(l, which, s, post):
            at_ = (3 * which + 2) * KC
            tt(gate_col[:, :], mods[:, l, at_:at_ + KC, s], C(post, KC * l, KC), ALU.mult)
            turn.tick()
            tt(dg[:, :, :], ident.unsqueeze(1).broadcast_to([P, KC, P]),
               gate_col[:, :].unsqueeze(2).broadcast_to([P, KC, P]),
               ALU.mult).then_inc(S_("diag_ready"), 1)

        def clear_sums(tiles, added):
            pool.wait_ge(S_("x4_ready"), added)
            turn(g.memset)(ys[:, 0:tiles, :], 0.0).then_inc(S_("ys_cleared"), 1)

        diagonal(0, 0, 0, "g_mix_post")
        full(pool, ("rows_mix0", 0, 1))
        diagonal(0, 0, 1, "g_mix_post")
        pool.wait_ge(S_("pool_scale_landed"), 16)
        slot, _, value = items[("mix2", 0, 0)]
        pool.wait_ge(landed[slot], value)
        w = ring[:, slot, 0:2048].rearrange("p (g k e) -> p g k e", g=4, k=2)
        scale = rows[:, 2, :].rearrange("p (g e) -> p g e", g=4)
        for k in range(2):
            ins = tt(w[:, :, k, :], w[:, :, k, :], scale, ALU.mult)
            if k == 0:
                turn.tick()
        ins.then_inc(S_("pool_w_ready"), 1)
        full(pool, ("rows_mix0", 1, 1))
        diagonal(0, 1, 0, "g_mlp_post")
        full(pool, ("rows_mlp0", 0, 1))
        diagonal(0, 1, 1, "g_mlp_post")
        clear_sums(2 * NT, X4_BEFORE["mlp0"])
        pool.wait_ge(S_("q_rot_ready"), NT)
        pool.wait_ge(S_("k_rot_ready"), 2 * NT)
        diagonal(1, 0, 0, "g_mix_post")
        full(pool, ("rows_mix1", 0, 1))
        diagonal(1, 1, 0, "g_mlp_post")
        clear_sums(NT, X4_BEFORE["mlp1"])

    @block.sync
    def _(sp):
        sp.dma_start(h[:, :, :], x.rearrange("(t p) d -> p t d", p=P)).then_inc(
            S_("x_landed"), 16)

        def load(name, depth, sources, view):
            slot, number, _ = items[name]
            if number >= depth:
                sp.wait_ge(weights_used, number - depth + 1)
            for out_, src in zip(view(ring[:, slot, :]), sources):
                sp.dma_start(out_, src).then_inc(landed[slot], 16)

        def chunked(w):
            return [w.rearrange("(c p) n -> p c n", p=P)]

        def eight(slot_):
            return [slot_.rearrange("p (c n) -> p c n", c=KC)]

        def four(slot_):
            return [slot_.rearrange("p (c n) -> p c n", c=4)]

        for l in range(DEPTH):
            ada_n = 0
            for n, kind in enumerate(mixer_items()):
                if kind == ADA:
                    src = w_ada[l, :, ada_n * 512:(ada_n + 1) * 512]
                    ada_n += 1
                else:
                    src = w_in[l, :, kind * 512:(kind + 1) * 512]
                load(("mix", l, n), RING1, chunked(src), eight)
            for n in range(2):
                load(("w_out", l, n), RING1, chunked(w_out[l, :, n * 512:(n + 1) * 512]), eight)
            with sp.Fori(0, NEXP) as e:
                for n in range(6):
                    slot, number, _ = items[("moe", l, 0, n)]
                    sp.wait_ge(weights_used, 6 * e + (number - RING1 + 1))
                    if n < 4:
                        dst = ring[:, slot, :].rearrange("p (k a f) -> p k a f", k=2, a=2)
                        for a, w in enumerate((w_gate, w_up)):
                            src = w[l, bass.ds(e, 1), 2 * n * P:2 * (n + 1) * P, :]
                            sp.dma_start(dst[:, :, a, :],
                                         src.rearrange("o (k p) f -> p (o k) f", p=P)).then_inc(
                                landed[slot], 16)
                    else:
                        src = w_down[l, bass.ds(e, 1), :, :].rearrange(
                            "o (g two p) d -> two p (o g) d", two=2, p=P)[n - 4]
                        sp.dma_start(ring[:, slot, :].rearrange("p (g d) -> p g d", g=4),
                                     src).then_inc(landed[slot], 16)
        for l in range(DEPTH):
            if l == 0:
                load(("mix2", 0, 0), RING2[l], [w_pool.rearrange("g (k p) e -> p (g k) e", p=P)],
                     lambda s_: [s_[:, 0:2048].rearrange("p (c e) -> p c e", c=8)])
            else:
                for n in range(3):
                    load(("mix2", 1, n), (2, 2, 3)[n],
                         chunked(w_qkv[:, n * 512:(n + 1) * 512]), eight)
                for n in range(2):
                    load(("mix2", 1, 3 + n), RING2[l], chunked(w_o[:, n * 512:(n + 1) * 512]),
                         eight)
            with sp.Fori(0, 4) as i:
                for n in range(4):
                    slot, number, _ = items[("mlp", l, n)]
                    sp.wait_ge(weights_used, 4 * i + (number - RING2[l] + 1))
                    if n < 2:
                        src = w_mlp_in[l, :, bass.ds(i * 1024 + n * 512, 512)]
                        sp.dma_start(eight(ring[:, slot, :])[0],
                                     src.rearrange("(c p) n -> p c n", p=P)).then_inc(
                            landed[slot], 16)
                    else:
                        src = w_mlp_out[l, bass.ds(i * 1024 + (n - 2) * 512, 512), :]
                        sp.dma_start(four(ring[:, slot, :])[0],
                                     src.rearrange("(c p) n -> p c n", p=P)).then_inc(
                            landed[slot], 16)
        for t in range(NT):
            sp.wait_ge(S_("x4_ready"), X4_TOTAL - NT + t + 1)
            sp.dma_start(out[t * P:(t + 1) * P, :], x4[:, t, :]).then_inc(S_("stored"), 16)
        sp.wait_ge(S_("stored"), 16 * NT)

    es.close()


X4_BEFORE = {"mlp0": 2 + 4, "mlp1": 2 + 4 + 4 + 2}
X4_TOTAL = 2 + 4 + 4 + 2 + 2


def shape_constants():
    f = np.float32
    tok = np.arange(S)
    half = P // 2
    inv = f(10000.0) ** (-np.arange(half, dtype=f) / f(half))
    ang = tok.astype(f)[:, None] * inv[None, :]
    cos = np.concatenate([np.cos(ang)] * 2, 1)
    sin = np.concatenate([-np.sin(ang), np.sin(ang)], 1)

    def by_tile(a):
        return a.reshape(NT, P, -1).transpose(1, 0, 2).reshape(P, -1)

    gamma = np.log1p(-(2.0 ** (-5.0 - np.arange(H4, dtype=f)))).astype(f)
    dist = np.abs(np.arange(3 * P)[None, :] - P - np.arange(P)[:, None]).astype(f)
    decay = np.exp(gamma[None, :, None] * dist[:, None, :]) * HEAD_SCALE
    sel = np.zeros((P, 2), f)
    for g in range(4):
        for j in range(2):
            sel[32 * g + j, j] = 1
    token = np.stack([np.arange(P) + P * t for t in range(NT)], 1)
    delta = np.zeros((P, NEXP), f)
    delta[:NEXP] = np.eye(NEXP)
    consts = np.concatenate([np.eye(P), by_tile(cos), by_tile(sin), decay.reshape(P, -1), sel,
                             token, delta], 1).astype(f)

    masks = np.zeros((P, len(LEVELS), 2, P // 2), f)
    s = np.arange(P)[:, None]
    u = np.arange(P // 2)[None, :]
    for i, m in enumerate(LEVELS):
        same = s // (2 * m) == u // m
        masks[:, i, 0] = same & (s % (2 * m) < m)
        masks[:, i, 1] = same & (s % (2 * m) >= m)
    masks = masks.reshape(P, -1)

    bands = np.zeros((len(WINDOWS), S, S), f)
    for g, w in enumerate(WINDOWS):
        lo = np.clip(tok - w // 2, 0, S)
        hi = np.clip(tok + w - w // 2, 0, S)
        for t in range(S):
            bands[g, lo[t]:hi[t], t] = f(1) / f(hi[t] - lo[t])
            bands[g, t, t] -= f(1)
    bands = bands.reshape(len(WINDOWS), NT, P, S).transpose(2, 0, 1, 3).reshape(P, -1)

    inv2 = f(10000.0) ** (-np.arange(0, half, 2, dtype=f) / f(half))
    ar = (tok // GRID_W).astype(f)[:, None] * inv2
    ac = (tok % GRID_W).astype(f)[:, None] * inv2
    cos2 = np.concatenate([np.cos(ar)] * 2 + [np.cos(ac)] * 2, 1)
    sin2 = np.concatenate([-np.sin(ar), np.sin(ar), -np.sin(ac), np.sin(ac)], 1)
    rope2 = np.concatenate([by_tile(cos2), by_tile(sin2)], 1)
    return consts, masks, np.ascontiguousarray(bands, f), np.ascontiguousarray(rope2, f)


def kernel(**inputs):
    import concourse.bacc as bacc
    from concourse.bass_utils import run_bass_kernel_spmd

    a = {k: np.asarray(v) for k, v in inputs.items()}

    def columns(v):
        return np.asarray(v).reshape(-1, P).T

    cols = np.concatenate([columns(a[n]) for n in (
        "norm1_g", "norm2_g", "ret_norm_g", "hgrn_norm_g", "lower_bounds", "b_ada_2",
        "g_mix_pre_2", "g_mix_post_2", "g_mlp_pre_2", "g_mlp_post_2", "c_2", "c_ctx_2")], 1)
    assert cols.shape == (P, NCOLS)
    consts, masks, bands, rope2 = shape_constants()
    arrays = {
        "x": a["x"].reshape(S, D), "cols": cols, "w_in": a["w_in"], "w_out": a["w_out"],
        "w_router": a["w_router"], "w_gate": a["w_gate"], "w_up": a["w_up"],
        "w_down": a["w_down"], "final_g": a["final_norm_g"], "ctx_x": a["ctx_2"].reshape(S, D),
        "w_ada": a["w_ada_2"], "w_pool": a["w_pool_2"][0], "pool_scale": a["pool_scale_2"][0],
        "w_qkv": a["w_qkv_2"][0], "g_qk": np.concatenate([a["g_q_2"][0], a["g_k_2"][0]]),
        "w_o": a["w_o_2"][0], "w_mlp_in": a["w_mlp_in_2"], "w_mlp_out": a["w_mlp_out_2"],
        "consts": consts, "masks": masks, "bands": bands, "rope2": rope2,
    }
    arrays = {f"in_{k}": np.ascontiguousarray(v) for k, v in arrays.items()}
    nc = bacc.Bacc("TRN2", target_bir_lowering=False, num_devices=1)
    args = {k[3:]: nc.dram_tensor(k, v.shape, mybir.dt.from_np(v.dtype),
                                  kind="ExternalInput").ap() for k, v in arrays.items()}
    out = nc.dram_tensor("out", (S, D), F32, kind="ExternalOutput").ap()
    build_program(nc, out=out, **args)
    r = run_bass_kernel_spmd(nc, [arrays], core_ids=[0])
    return r.results[0]["out"].reshape(1, S, D)
```

```python
from contextlib import ExitStack

import numpy as np

import concourse.bass as bass
from concourse import mybir

ALU = mybir.AluOpType
ACT = mybir.ActivationFunctionType
F32 = mybir.dt.float32
F32R = mybir.dt.float32r
BF16 = mybir.dt.bfloat16
U8 = mybir.dt.uint8
U32 = mybir.dt.uint32
AX = mybir.AxisListType

P = 128
D = 1024
KC = D // P
S = 256
NT = S // P
DEPTH = 2
H4 = 4
W4 = H4 * P
IN_COLS = 9 * W4
NEXP = 16
CAP = 2 * S // NEXP
FF = 1024
DFF = 4096
NMOD = 6
NQ, NKV = 8, 2
EPS = 1e-6
HEAD_SCALE = float(P) ** -0.5
WINDOWS = (2, 4, 8, 16)
GRID_W = 64
SLOT = 4096
RING1 = 6
RING2 = (2, 4)
LEVELS = (1, 2, 4, 8, 16, 32, 64)

COLS = {}
_n = 0
for _name, _w in (("norm1_g", 16), ("norm2_g", 16), ("ret_g", 8), ("hgrn_g", 8), ("lower", 8),
                  ("b_ada", 96), ("g_mix_pre", 16), ("g_mix_post", 16), ("g_mlp_pre", 16),
                  ("g_mlp_post", 16), ("c", 8), ("c_ctx", 8)):
    COLS[_name] = (_n, _n + _w)
    _n += _w
NCOLS = _n
CONSTS = {}
_n = 0
for _name, _w in (("ident", P), ("cos", NT * P), ("sin", NT * P), ("decay", H4 * 3 * P),
                  ("sel", 2), ("token", NT), ("delta", NEXP)):
    CONSTS[_name] = (_n, _n + _w)
    _n += _w
NCONST = _n

RQ, RK, RV, RG, HQ, HFF, HFB, HI, HG = range(9)
ADA = "ada"


def mixer_items():
    return [RQ, RK, HFF, HFB, HQ, RV, ADA, HI, ADA, ADA, RG, ADA, ADA, HG, ADA]


ADA_EARLY, ADA_ALL = mixer_items().count(ADA), 12
ADA_LATE = range(ADA_EARLY, ADA_ALL)

SPLIT = [n for n, kind in enumerate(mixer_items()) if kind != ADA]
SPLITS, BY_VECTOR = len(SPLIT) + 2, 5

HALVES = [(j, half) for j in range(SPLITS) for half in range(2)]
VECTOR_HALVES = [(j, half) for j, half in HALVES if j < BY_VECTOR and (j, half) != (0, 1)]
POOL_HALVES = [x for x in HALVES if x not in VECTOR_HALVES]


def build_program(nc, x, cols, w_in, w_out, w_router, w_gate, w_up, w_down, final_g, ctx_x, w_ada,
                  w_pool, pool_scale, w_qkv, g_qk, w_o, w_mlp_in, w_mlp_out, consts, masks,
                  bands, rope2, out):
    es = ExitStack()
    at = [16512]
    here = {}

    def place(name, shape, dtype=F32, where=None):
        size = int(np.prod(shape[1:])) * (1 if dtype == U8 else 2 if dtype == BF16 else 4)
        offset = at[0] if where is None else here[where]
        here[name] = offset
        if where is None:
            at[0] += (size + 31) // 32 * 32
        return nc.alloc_sbuf_tensor_at(name, list(shape), dtype, offset=offset)

    ring = place("ring", [P, RING1, SLOT])
    ring_end = at[0]
    ident_all = place("consts_sb", [P, NCONST])
    col = place("cols_sb", [P, NCOLS])
    mods = place("mods", [P, DEPTH, NMOD * KC, 2])
    mod_gain = place("mod_gain", [P, DEPTH, 2, 2, KC])
    cT = place("silu_c", [P, KC, 32])
    ones = place("ones", [P, P])
    lb = place("lower_bound", [P, 3, DEPTH, H4])
    eps = place("eps", [P, 1])
    ssq = place("ssq", [P, 4])
    std = place("std", [P, 4])
    rinv = place("rinv", [P, 4])
    zeros = place("zeros", [P, P], BF16)
    mask = place("mask_sb", [P, len(LEVELS), 2, P // 2], U8)
    h = place("h", [P, NT, D])
    h_at = here["h"]

    first_at = at[0]
    xs = place("xs", [P, NT, D])
    xT = place("xT", [P, KC, S])
    r_at = at[0]
    rot = place("rot", [P, 2, NT, W4])
    RS_ = place("ret_scores", [P, NT, H4, S], where="rot")
    ret_v = place("ret_v", [P, NT, W4])
    ret_gate = place("ret_gate", [P, NT, W4])
    hg_v = place("hgrn_v", [P, NT, W4])
    hg_gate = place("hgrn_gate", [P, NT, W4])
    retT = place("retT", [P, 2, H4, S])
    kdec = place("kdec", [P, 2, H4, S], where="retT")
    hq = place("hgrn_q", [P, H4, S])
    hf = place("hgrn_f", [P, 2, H4, S])
    hk = place("hgrn_k", [P, 2, H4, S])
    hx = place("hgrn_x", [P, 2, H4, S])
    qdec = place("qdec", [P, 2, H4, P])
    rope_t = place("rope_tmp", [P, 2, W4], where="qdec")
    AD = place("hgrn_diag", [P, 2 * H4, P])
    AO = place("hgrn_off", [P, 2, H4, P])
    ada_s = place("ada_rows", [P, 512])
    rstat = place("ret_stat", [P, 3, NT, H4])
    sq = place("square", [P, NT, W4], where="qdec")
    save = at[0]
    at[0] = r_at
    wr = place("router_sb", [P, KC, NEXP])
    logit = place("logit", [P, NT, NEXP])
    aff = place("affinity", [P, NT, NEXP])
    rstats = place("router_stat", [P, NT, 4])
    affT = place("affinityT", [NEXP, 2, S])
    top = place("top_gate", [NEXP, CAP])
    topi = place("top_index", [NEXP, CAP], U32)
    topf = place("top_index_f", [NEXP, CAP])
    spread = place("spread", [NEXP, 2, NEXP, CAP])
    onehot = place("onehot", [P, NT, NEXP * CAP])
    gated = place("gated", [P, NT, NEXP * CAP])
    gsel = place("gate_sel", [P, NT, 4, CAP])
    GT = place("gate_T", [P, S])
    xeT = place("xeT", [P, KC, CAP])
    silu_g = place("silu_g", [P, 256])
    hidE = place("hid_e", [P, 256])
    hidT = place("hid_T", [P, 2, P])
    Y = place("y_e", [P, D])
    gfin = place("final_g_row", [P, D])
    assert at[0] <= save
    top_of_first = save

    at[0] = h_at
    x4 = place("x4", [P, 2 * NT, D])
    assert at[0] >= first_at
    ys = place("y2", [P, 2 * NT, D])
    xs2 = place("xs2", [P, 2 * NT, D])
    xT2 = place("xT2", [P, KC, 2 * S])
    x_full = place("x_full", [P, KC, 2 * S])
    rows = place("gate_rows", [P, 3, D])
    rope_g = place("rope_gained", [P, 2, 2, NT, P])
    gqk = place("gqk_sb", [P, 2, P])
    gate_col = place("gate_col", [P, KC])
    soft = place("softmax_stat", [P, 4, 4])
    qst = place("q_stat", [P, 3, NT * NQ])
    kst = place("k_stat", [P, 3, 2 * NT * NKV])
    assert at[0] <= 229344, at[0]
    x_high = place("x_high", [P, KC, 2 * S], F32R, where="xT2")
    x_low = place("x_low", [P, KC, 2 * S], F32R, where="x_full")
    w_low = place("w_low", [P, RING2[1], SLOT], F32R, where="ring")
    at[0] = here["ring"] + 2 * SLOT * 4
    h_high0 = place("hid_high0", [P, 2, 4, 2 * S], F32R)
    h_low0 = place("hid_low0", [P, 2, 4, 2 * S], F32R)
    w_high = place("w_high", [P, 2, SLOT], F32R)
    assert at[0] == ring_end
    at[0] = here["xs2"]
    h_high1 = place("hid_high1", [P, 2, 4, S], F32R)
    h_low1 = place("hid_low1", [P, 2, 4, S], F32R)
    dg = place("diag", [P, KC, P], where="rope_gained")
    h_raw = place("hid_raw", [P, 2, 2 * S], where="rope_gained")
    band = place("band_sb", [P, 4, NT, S], where="x_full")
    diffT = place("diffT", [P, KC, 2 * S], where="xT2")
    qr = place("q_rot", [P, NT, D], where="y2")
    at[0] = here["y2"] + NT * D * 4
    q_tmp = place("q_tmp", [P, 2, D])
    q_sq = place("q_square", [P, NT, D], where="xs2")
    at[0] = here["xs2"]
    qT2 = place("qT2", [P, NQ, S])
    pr = place("prob", [P, 2, 2 * S])
    prT = place("probT", [P, 4, S])
    q_raw = place("q_raw", [P, NT, D], where="x_full")
    oT = place("oT", [P, NQ, S], where="x_full")
    at[0] = here["x_full"] + NT * D * 4
    kv = place("kv", [P, 2 * NT, 2, 2 * P])
    at[0] = here["consts_sb"] + 4 * CONSTS["decay"][0]
    kT2 = place("kT2", [P, NKV, 2 * S])
    rope_c = place("rope2_sb", [P, 2, NT, P])
    assert at[0] <= here["consts_sb"] + 4 * CONSTS["decay"][1]
    xs_high = place("xs_high", [P, NT, KC, P], F32R, where="xs")
    xT_low = place("xT_low", [P, KC, S], F32R, where="xT")
    hidden_plan = ({1: (0, 1), 2: (2, 3)}, {0: (0,), 1: (1,), 2: (2, 3)})
    output_plan = ({1: (0, 1), 2: (2, 3)}, {0: (0, 1), 1: (2, 3)})

    def quarter(q):
        return slice(q * SLOT // 4, (q + 1) * SLOT // 4)

    mlp_parts = ((h_high0, h_low0), (h_high1, h_low1))

    psum = [es.enter_context(nc.psum_tensor(f"bank{i}", [P, 512], F32)) for i in range(8)]
    sems = {}

    def S_(name):
        if name not in sems:
            sems[name] = es.enter_context(nc.semaphore(name))
        return sems[name]

    landed = [S_(f"landed{i}") for i in range(RING1)]
    weights_used = S_("weights_used")
    bank_full = [S_(f"bank_full{i}") for i in range(8)]
    bank_free = [S_(f"bank_free{i}") for i in range(8)]

    def C(name, i=None, n=1):
        a, b = COLS[name]
        return col[:, a:b] if i is None else col[:, a + i:a + i + n]

    def K(name):
        a, b = CONSTS[name]
        return ident_all[:, a:b]

    ident = K("ident")

    items, free_at, count = {}, {}, [0, [0] * RING1, [0] * RING1]

    def item(name, slot, dmas):
        count[1][slot] += 16 * dmas
        items[name] = (slot, count[0], count[1][slot])
        free_at[name] = count[2][slot]
        count[0] += 1
        count[2][slot] = count[0]

    for layer in range(DEPTH):
        order = sorted(range(4), key=lambda slot: count[2][slot])
        slots = [order[n % 4] for n in range(len(mixer_items()) + 2)]
        order = [order[(len(slots) + n) % 4] for n in range(4)] + [4, 5]
        slots += [order[n % 6] for n in range(len(ADA_LATE) + 6 * NEXP)]
        names = ([("mix", layer, n) for n in range(len(mixer_items()))]
                 + [("w_out", layer, n) for n in range(2)]
                 + [("late", layer, n) for n in ADA_LATE]
                 + [("moe", layer, e, n) for e in range(NEXP) for n in range(6)])
        for name, slot in zip(names, slots):
            if name == ("late", layer, ADA_EARLY):
                count[2][4:6] = [count[0]] * 2
            item(name, slot, 2 if name[0] == "moe" and name[3] < 4 else 1)
    for layer in range(DEPTH):
        order = ((0, 1), (1, 0, 2, 3))[layer]
        if layer == 1:
            count[2][2:4] = [count[0]] * 2
        for n, name in enumerate(
                [("mix2", layer, n) for n in range(1 if layer == 0 else 5)]
                + [("mlp", layer, n) for n in range(16)]):
            item(name, order[n % RING2[layer]], 1)

    def wait_landed(pe, name):
        slot, _, value = items[name]
        pe.wait_ge(landed[slot], value)
        return ring[:, slot, :]

    filled, frees, where_is, read_by = [0] * 8, [0] * 8, {}, {}

    def take(pe, name, bank, readers=1):
        if frees[bank]:
            pe.wait_ge(bank_free[bank], frees[bank])
        frees[bank] += readers
        read_by[name] = (bank_free[bank], frees[bank])
        where_is[name] = (bank, None, None)
        return psum[bank]

    def fill(ins, name):
        bank = where_is[name][0]
        filled[bank] += 1
        where_is[name] = (bank, bank_full[bank], filled[bank])
        ins.then_inc(bank_full[bank], 1)

    def fill_and_release(ins, name, item_name):
        where_is[name] = (where_is[name][0], weights_used, items[item_name][1] + 1)
        ins.then_inc(weights_used, 1)

    def full(eng, name):
        bank, sem, value = where_is[name]
        eng.wait_ge(sem, value)
        return psum[bank]

    def freed(eng, name):
        eng.wait_ge(*read_by[name])

    def free(ins, name):
        ins.then_inc(bank_free[where_is[name][0]], 1)

    def split_item(l, j):
        return items[("mix", l, SPLIT[j]) if j < len(SPLIT) else ("w_out", l, j - len(SPLIT))]

    def split_half(l, j, half):
        slot, part = split_item(l, j)[0], slice(half * SLOT // 2, (half + 1) * SLOT // 2)
        return (ring[:, slot, part], w_high[:, (SPLITS * l + j) % 2, part],
                w_low[:, slot, part])

    class InTurn:

        def __init__(self, eng, step_name):
            self.eng, self.step, self.mine, self.totals = eng, S_(step_name), None, {}

        def __call__(self, op):
            def run(*args, **kw):
                assert self.mine != "none", "the instruction before signals nothing"
                if self.mine:
                    self.eng.wait_ge(*self.mine)
                self.ins, self.mine = op(*args, **kw), "none"
                return self
            return run

        def then_inc(self, sem, n, value=None):
            self.ins.then_inc(sem, n)
            self.totals[id(sem)] = self.totals.get(id(sem), 0) + n
            self.mine = (sem, value or self.totals[id(sem)])

        def tick(self, _=None):
            self.then_inc(self.step, 1)

        def free(self, _, name):
            self.then_inc(read_by[name][0], 1, read_by[name][1])

    def low_item(subtract, eng, l, j):
        by, halves = (("split_by_pool", POOL_HALVES) if eng is nc.gpsimd
                      else ("split_by_vector", VECTOR_HALVES))
        for half in range(2):
            if (j, half) not in halves:
                continue
            eng.wait_ge(S_("mix_high_ready"), 2 * (SPLITS * l + j) + half + 1)
            whole, high, low = split_half(l, j, half)
            subtract(low, whole, high.bitcast(F32), ALU.subtract).then_inc(S_(by), 1)

    def low_chunks(subtract, b):
        part = slice(2 * b, 2 * b + 2)
        high = xs_high[:, :, part, :].bitcast(F32).rearrange("p t c n -> p c t n")
        return subtract(xT_low[:, part, :].rearrange("p c (t n) -> p c t n", t=NT),
                        xT[:, part, :].rearrange("p c (t n) -> p c t n", t=NT), high,
                        ALU.subtract)

    units = [(m, d) for m in LEVELS for d in range(2)] + [(P, 0), (P, 1)]
    moe_base = [items[("moe", l, 0, 0)][1] for l in range(DEPTH)]
    per_item = [16 * 4 // r for r in RING2]
    mlp_base = [items[("mlp", l, 0)][1] for l in range(DEPTH)]
    hid_done, out_done = [0, 4 * 8], [0, 8 * 8]

    block = es.enter_context(nc.Block())

    @block.tensor
    def _(pe):
        mm, turn = nc.tensor.matmul, nc.tensor.transpose
        turned = [None]

        def transposes(tag, src, ready, first=4):
            for t in range(NT):
                ready(t)
                for b in range(4):
                    bank = (first + b) % 8
                    ps = take(pe, (tag, b), bank) if t == 0 else psum[bank]
                    for c in (2 * b, 2 * b + 1):
                        at_ = (c % 2) * S + t * P
                        ins = turn(ps[:, at_:at_ + P], src(t)[:, c * P:(c + 1) * P], ident)
                    if t == NT - 1:
                        fill(ins, (tag, b))
            turned[0] = tag

        def wait_turned(c=KC - 1):
            freed(pe, (turned[0], c // 2))

        def rows_ready(name):
            seen = [0]

            def ready(t):
                seen[0] += 1
                pe.wait_ge(S_(name), seen[0])
            return ready

        xs_ready, xs2_ready = rows_ready("xs_ready"), rows_ready("xs2_ready")

        def product(ps, left, right, first, last):
            (lh, ll), (rh, rl) = left, right
            mm(ps, lh, rh, start=first, stop=False, skip_group_check=True)
            mm(ps, lh, rl, start=False, stop=False, skip_group_check=True)
            return mm(ps, ll, rh, start=False, stop=last, skip_group_check=True)

        def ada_item(layer, l_item, n, tag):
            w = wait_landed(pe, l_item).rearrange("p (c n) -> p c n", c=KC)
            if n == 0 and layer == 0:
                pe.wait_ge(S_("silu_c_ready"), 2)
            ps = take(pe, tag, 6)
            for k in range(2):
                for g in range(4):
                    ins = mm(ps[32 * g:32 * g + 32, :], cT[:, 2 * g + k, :], w[:, 2 * g + k, :],
                             start=k == 0, stop=k == 1)
            fill_and_release(ins, tag, l_item)

        def ada_columns(layer, n, tag):
            freed(pe, ("ada", layer, n))
            ps = take(pe, tag, 7)
            for j in range(4):
                ins = mm(ps[:, 2 * j:2 * j + 2], ada_s[:, j * P:(j + 1) * P], K("sel"),
                         start=True, stop=True)
            fill(ins, tag)

        pe.wait_ge(S_("consts"), 16)
        pe.wait_ge(S_("ones_ready"), 1)

        for l in range(DEPTH):
            transposes(("x1", l), lambda t: xs[:, t, :], xs_ready)
            proj_bank = [0]

            def take_proj(name, readers=1):
                b = proj_bank[0]
                proj_bank[0] = (b + 1) % 4
                return take(pe, name, b, readers)

            def wait_split(j, c, conversion=None):
                if conversion is not None and c % 2 == 0:
                    b = c // 2
                    if conversion:
                        pe.wait_ge(S_("mix_x_split"), 6 * l + 2 + b + 1)
                    elif b % 2 == 0:
                        pe.wait_ge(S_("mix_x_split"), 6 * l + b // 2 + 1)
                    else:
                        pe.wait_ge(S_("mix_x_split_by_pool"), 2 * l + b // 2 + 1)
                if c % 4:
                    return
                for by, halves in (("vector", VECTOR_HALVES), ("pool", POOL_HALVES)):
                    if (j, c // 4) in halves:
                        pe.wait_ge(S_("split_by_" + by),
                                   len(halves) * l + halves.index((j, c // 4)) + 1)

            def split_parts(j):
                slot = split_item(l, j)[0]
                return [w.rearrange("p (c n) -> p c n", c=KC)
                        for w in (w_high[:, (SPLITS * l + j) % 2, :], w_low[:, slot, :])]

            def rows_times(ps, t, j, conversion):
                wh, wl = split_parts(j)
                for c in range(KC):
                    wait_split(j, c, conversion)
                    ins = product(ps[:, :], (xs_high[:, t, c, :], xT_low[:, c, t * P:(t + 1) * P]),
                                  (wh[:, c, :], wl[:, c, :]), c == 0, c == KC - 1)
                return ins

            def project_rows(n, kind, t):
                it = ("mix", l, n)
                name = ("proj", l, kind, t)
                ins = rows_times(take_proj(name), t, SPLIT.index(n),
                                 0 if (n, t) == (0, 0) else None)
                if t == NT - 1:
                    fill_and_release(ins, name, it)
                else:
                    fill(ins, name)

            def project_features(n, kind):
                it = ("mix", l, n)
                wh, wl = split_parts(SPLIT.index(n))
                for pair in range(2):
                    name = ("proj", l, kind, pair)
                    ps = take_proj(name)
                    for head in (2 * pair, 2 * pair + 1):
                        part = slice(head * P, (head + 1) * P)
                        for c in range(KC):
                            wait_split(SPLIT.index(n), c)
                            ins = product(ps[:, (head % 2) * S:(head % 2 + 1) * S],
                                          (wh[:, c, part], wl[:, c, part]),
                                          (xs_high[:, :, c, :], xT_low[:, c, :]),
                                          c == 0, c == KC - 1)
                    if pair == 1:
                        fill_and_release(ins, name, it)
                    else:
                        fill(ins, name)

            def turn_ret(i):
                pe.wait_ge(S_("rot_ready"), (2 * l + i) * NT + NT)
                for pair in range(2):
                    name = ("retT", l, i, pair)
                    ps = take(pe, name, 4 + 2 * i + pair)
                    for head in (2 * pair, 2 * pair + 1):
                        for t in range(NT):
                            at_ = (head % 2) * S + t * P
                            ins = turn(ps[:, at_:at_ + P], rot[:, i, t, head * P:(head + 1) * P],
                                       ident)
                    fill(ins, name)

            def ret_scores():
                for i in range(2):
                    for pair in range(2):
                        freed(pe, ("retT", l, i, pair))
                for head in range(H4):
                    name = ("ret_s", l, head)
                    ps = take(pe, name, 4 + head)
                    for t in range(NT):
                        ins = mm(ps[:, t * S:(t + 1) * S], retT[:, 1, head, t * P:(t + 1) * P],
                                 retT[:, 0, head, :], start=True, stop=True)
                    fill(ins, name)

            def hgrn_same():
                pe.wait_ge(S_("k_sum_ready"), l + 1)
                for pair in range(2):
                    freed(pe, ("proj", l, HQ, pair))
                for t in range(2):
                    name = ("same", l, t)
                    ps = take(pe, name, 4 + t)
                    for j in range(H4):
                        head, tile = (4 * t + j) // 2, j % 2
                        part = slice(tile * P, (tile + 1) * P)
                        ins = mm(ps[:, j * P:(j + 1) * P], hx[:, 0, head, part], hq[:, head, part],
                                 start=True, stop=True)
                    fill(ins, name)

            def hgrn_unit(u):
                m, d = units[u]
                name = ("unit", l, u)
                pe.wait_ge(S_("level_ready"), len(units) * l + u + 1)
                ps = take(pe, name, 4 + u % 2)
                for head in range(H4):
                    if m == P:
                        ins = mm(ps[:, head * P:(head + 1) * P],
                                 kdec[:, d, head, d * P:(d + 1) * P], qdec[:, d, head, :],
                                 start=True, stop=True)
                        continue
                    for t in range(NT):
                        j = 2 * head + t
                        key = (hk if m == 1 else kdec)[:, d, head, t * P:(t + 1) * P]
                        ins = mm(ps[:, j * 64:(j + 1) * 64], key,
                                 qdec[:, d, head, t * 64:(t + 1) * 64], start=True, stop=True)
                fill(ins, name)

            def ret_out():
                for head in range(H4):
                    freed(pe, ("ret_s", l, head))
                for t in range(NT):
                    freed(pe, ("proj", l, RV, t))
                for t in range(NT):
                    name = ("ret_o", l, t)
                    ps = take_proj(name)
                    for head in range(H4):
                        part = slice(head * P, (head + 1) * P)
                        for j in range(NT):
                            ins = mm(ps[:, part], RS_[:, j, head, t * P:(t + 1) * P],
                                     ret_v[:, j, part], start=j == 0, stop=j == NT - 1)
                    fill(ins, name)

            def hgrn_out():
                for u in range(len(units) - 4, len(units)):
                    freed(pe, ("unit", l, u))
                for t in range(NT):
                    freed(pe, ("proj", l, HI, t))
                for t in range(NT):
                    name = ("hgrn_o", l, t)
                    ps = take_proj(name)
                    for head in range(H4):
                        part = slice(head * P, (head + 1) * P)
                        mm(ps[:, part], AD[:, 2 * head + t, :], hg_v[:, t, part],
                           start=True, stop=False)
                        ins = mm(ps[:, part], AO[:, 1 - t, head, :], hg_v[:, 1 - t, part],
                                 start=False, stop=True)
                    fill(ins, name)

            fill_u, ada_n, pending = [0], [0], []

            def some_units(n):
                for _ in range(n):
                    if fill_u[0] < len(units):
                        hgrn_unit(fill_u[0])
                        fill_u[0] += 1

            for n, kind in enumerate(mixer_items()):
                if kind == ADA:
                    if pending:
                        ada_columns(l, pending[0], ("ada_c", l, pending.pop()))
                    ada_item(l, ("mix", l, n), ada_n[0], ("ada", l, ada_n[0]))
                    pending.append(ada_n[0])
                    ada_n[0] += 1
                elif kind in (HQ, HFF, HFB):
                    project_features(n, kind)
                    if kind == HFF:
                        turn_ret(0)
                    elif kind == HFB:
                        turn_ret(1)
                    else:
                        ret_scores()
                        hgrn_same()
                else:
                    for t in range(NT):
                        project_rows(n, kind, t)
                        if n > 4:
                            some_units(2)
                if kind == HG:
                    some_units(len(units))
                    ret_out()
                    hgrn_out()

            late_bank = [None]

            def late_ada(n):
                if n == ADA_LATE[0]:
                    ada_columns(l, n - 1, ("ada_c", l, n - 1))
                else:
                    late_columns(n - 1)
                ada_item(l, ("late", l, n), n, ("ada", l, n))

            def late_columns(n):
                name = ("ada_c", l, "late")
                freed(pe, ("ada", l, n))
                if n == ADA_LATE[0]:
                    late_bank[0] = take(pe, name, 7)
                for j in range(4):
                    at_ = 8 * (n - ADA_EARLY) + 2 * j
                    ins = mm(late_bank[0][:, at_:at_ + 2], ada_s[:, j * P:(j + 1) * P], K("sel"),
                             start=True, stop=True)
                if n == ADA_LATE[-1]:
                    fill(ins, name)

            def mix_ready(t):
                freed(pe, ("ret_o", l, t))
                freed(pe, ("hgrn_o", l, t))

            transposes(("mix", l), lambda t: xs[:, t, :], mix_ready)
            for t in range(NT):
                for n in range(2):
                    it = ("w_out", l, n)
                    name = ("w_out", l, n, t)
                    ins = rows_times(take(pe, name, 2 * n + t), t, len(SPLIT) + n,
                                     1 if (n, t) == (0, 0) else None)
                    if t == NT - 1:
                        fill_and_release(ins, name, it)
                    else:
                        fill(ins, name)

            late_ada(ADA_LATE[0])
            transposes(("x2", l), lambda t: xs[:, t, :], xs_ready)
            for c in range(0, KC, 2):
                wait_turned(c)
            name = ("logit", l)
            ps = take(pe, name, 4)
            pe.wait_ge(S_("router_landed"), 16 * (l + 1))
            for t in range(NT):
                for c in range(KC):
                    ins = mm(ps[:, t * NEXP:(t + 1) * NEXP], xT[:, c, t * P:(t + 1) * P],
                             wr[:, c, :], start=c == 0, stop=c == KC - 1)
            fill(ins, name)
            late_ada(ADA_LATE[1])
            pe.wait_ge(S_("affinity_ready"), NT * (l + 1))
            name = ("affT", l)
            ps = take(pe, name, 5)
            for t in range(NT):
                ins = turn(ps[0:NEXP, t * P:(t + 1) * P], aff[:, t, :], ident)
            fill(ins, name)
            for n in ADA_LATE[2:]:
                late_ada(n)
            late_columns(ADA_LATE[-1])
            for b in range(4):
                ps = take(pe, ("moe", l, b), b)
                mm(ps[:, :], zeros[:, :], zeros[:, :].unsqueeze(1).broadcast_to([P, 4, P]),
                   start=True, stop=False,
                   skip_group_check=True)
            for i in range(2):
                pe.wait_ge(S_("spread_ready"), 2 * l + i + 1)
                name = ("spread", l, i)
                ps = take(pe, name, 4 + i)
                ins = mm(ps[:, :], ones[0:NEXP, :], spread[:, i, :, :].rearrange("e a b -> e (a b)"),
                         start=True, stop=True)
                fill(ins, name)
            for b in range(4, 8):
                pe.wait_ge(bank_free[b], frees[b])
            land = [items[("moe", l, 0, n)] for n in range(6)]
            with pe.Fori(0, NEXP) as e:
                done = l * NEXP + e
                pe.wait_ge(S_("gate_sel_ready"), done + 1)
                for t in range(NT):
                    ins = turn(psum[5][:, t * P:(t + 1) * P],
                               gsel[:, t, :, :].rearrange("p a b -> p (a b)"), ident)
                ins.then_inc(S_("gate_T_full"), 1)
                for c in range(KC):
                    for t in range(NT):
                        ins = mm(psum[7][:, c * CAP:(c + 1) * CAP],
                                 xs[:, t, c * P:(c + 1) * P],
                                 onehot[:, t, bass.ds(e * CAP, CAP)], start=t == 0,
                                 stop=t == NT - 1, skip_group_check=True)
                ins.then_inc(S_("gathered"), 1)
                pe.wait_ge(S_("xeT_ready"), done + 1)
                for n in range(4):
                    sl, _, value = land[n]
                    pe.wait_ge(landed[sl], value + 32 * e)
                    w = ring[:, sl, :].rearrange("p (k a f) -> p k a f", k=2, a=2)
                    for k in range(2):
                        for g in range(4):
                            ins = mm(psum[4][32 * g:32 * g + 32, :], xeT[:, 2 * n + k, :],
                                     w[:, k, :, 256 * g:256 * (g + 1)],
                                     start=n == 0 and k == 0, stop=n == 3 and k == 1,
                                     skip_group_check=True)
                    ins.then_inc(weights_used, 1)
                pe.wait_ge(S_("gate_T_ready"), done + 1)
                pe.wait_ge(S_("hid_e_ready"), done + 1)
                for j in range(2):
                    ins = turn(psum[6][:, j * P:(j + 1) * P], hidE[:, j * P:(j + 1) * P], ident)
                ins.then_inc(S_("hid_T_full"), 1)
                pe.wait_ge(S_("hid_T_ready"), done + 1)
                for n in range(2):
                    sl, _, value = land[4 + n]
                    pe.wait_ge(landed[sl], value + 16 * e)
                    w = ring[:, sl, :].rearrange("p (g d) -> p g d", g=4)
                    for half in range(2):
                        for g in range(4):
                            ins = mm(psum[5 + half][32 * g:32 * g + 32, :],
                                     hidT[:, n, 32 * g:32 * g + 32],
                                     w[:, g, half * 512:(half + 1) * 512],
                                     start=n == 0, stop=n == 1, skip_group_check=True)
                    ins.then_inc(weights_used, 1)
                pe.wait_ge(S_("y_left_ready"), done + 1)
                pe.wait_ge(S_("y_right_ready"), done + 1)
                for half in range(2):
                    for t in range(NT):
                        ins = mm(psum[2 * half + t][:, :], GT[:, t * P:(t + 1) * P],
                                 Y[:, half * 512:(half + 1) * 512], start=False, stop=False,
                                 skip_group_check=True)
                ins.then_inc(S_("scattered"), 1)

        def post_rows(tag, n):
            for i in range(n):
                pe.wait_ge(S_("diag_ready"), rows_done[0] + 1)
                for half in range(2):
                    name = (tag, i, half)
                    ps = take(pe, name, 2 * (rows_done[0] % 2) + half)
                    ins = mm(ps[:, :], ones[:, :],
                             dg[:, 4 * half:4 * half + 4, :].rearrange("p a b -> p (a b)"),
                             start=True, stop=True)
                    fill(ins, name)
                rows_done[0] += 1

        rows_done = [0]

        def mlp(l, streams):
            T = streams * S
            tiles = streams * NT
            first = [items[("mlp", l, n)][0] for n in range(4)]
            base_h, base_o = hid_done[l], out_done[l]
            h_high, h_low = mlp_parts[l]

            def parts(n, c):
                return [w.rearrange("p (c n) -> p c n", c=c)
                        for w in (w_high[:, n % 2, :], w_low[:, first[n], :])]

            pe.wait_ge(S_("x_split"), base_h // 32 * 2 + streams)
            pe.wait_ge(S_("x_split_by_pool"), base_h // 32 * 2 + streams)
            with pe.Fori(0, 4) as i:
                for b in range(2):
                    pe.wait_ge(S_("w_split"), 16 * i + (64 * l + 4 * b + 4))
                    wh, wl = parts(b, KC)
                    for j in range(4):
                        k = 4 * b + j
                        pe.wait_ge(S_("relu_ready"), i * 8 + (base_h + k + 1))
                        for c in range(KC):
                            part = slice(j * P, (j + 1) * P)
                            ins = product(psum[k % 2][:, 0:T], (wh[:, c, part], wl[:, c, part]),
                                          (x_high[:, c, 0:T], x_low[:, c, 0:T]), c == 0,
                                          c == KC - 1)
                        if j < 3:
                            ins.then_inc(S_("hidden_full"), 1)
                        else:
                            ins.then_inc(weights_used, 1)
                for b in range(2):
                    pe.wait_ge(S_("w_split"), 16 * i + (64 * l + 4 * b + 12))
                    wh, wl = parts(2 + b, 4)
                    pe.wait_ge(S_("hidden_ready"), i * 8 + (base_h + 2 + 4 * (b + 1)))
                    for t in range(tiles):
                        for half in range(2):
                            k = (b * tiles + t) * 2 + half
                            pe.wait_ge(S_("out_added"), i * (4 * tiles) + (base_o + k + 5))
                            for c in range(4):
                                row = slice(t * P, (t + 1) * P)
                                part = slice(half * 512, (half + 1) * 512)
                                ins = product(psum[2 + k % 4][:, :],
                                              (h_high[:, b, c, row], h_low[:, b, c, row]),
                                              (wh[:, c, part], wl[:, c, part]), c == 0, c == 3)
                            if (t, half) == (tiles - 1, 1):
                                ins.then_inc(weights_used, 1)
                            else:
                                ins.then_inc(S_("out_full"), 1)

        post_rows("rows_mix0", 2)
        pe.wait_ge(S_("bands_landed"), 16)
        for s in range(2):
            for t in range(NT):
                xs2_ready(t)
            for c in range(KC):
                name = (("pool_d", s), c // 2)
                ps = take(pe, name, 4 + c // 2) if c % 2 == 0 else ps
                for t in range(NT):
                    ins = mm(ps[:, (c % 2) * S:(c % 2 + 1) * S],
                             xs2[:, 2 * s + t, c * P:(c + 1) * P], band[:, c // 2, t, :],
                             start=t == 0, stop=t == NT - 1)
                if c % 2:
                    fill(ins, name)
        pe.wait_ge(S_("pool_w_ready"), 1)
        w = ring[:, items[("mix2", 0, 0)][0], 0:2048].rearrange("p (g k e) -> p g k e", g=4, k=2)
        for t in range(2 * NT):
            for b in range(4):
                freed(pe, (("pool_d", t // 2), b))
            for half in range(2):
                name = ("pool_y", t, half)
                ps = take(pe, name, 2 * (t % 2) + half)
                for g in (2 * half, 2 * half + 1):
                    for k in range(2):
                        ins = mm(ps[:, (g % 2) * S:(g % 2 + 1) * S],
                                 diffT[:, 2 * g + k, t * P:(t + 1) * P], w[:, g, k, :],
                                 start=k == 0, stop=k == 1)
                if (t, half) == (2 * NT - 1, 1):
                    fill_and_release(ins, name, ("mix2", 0, 0))
                else:
                    fill(ins, name)
        post_rows("rows_mlp0", 2)
        for s in range(2):
            transposes(("xm0", s), lambda t, s=s: xs2[:, 2 * s + t, :], xs2_ready,
                       first=(4, 0)[s])
        for b in range(8):
            pe.wait_ge(bank_free[b], frees[b])
        mlp(0, 2)

        def project(t, n, name, bank, it, last):
            w = wait_landed(pe, it).rearrange("p (c n) -> p c n", c=KC)
            ps = take(pe, name, bank)
            for c in range(KC):
                ins = mm(ps[:, :], xT2[:, c, t * P:(t + 1) * P], w[:, c, :], start=c == 0,
                         stop=c == KC - 1)
            if last:
                fill_and_release(ins, name, it)
            else:
                fill(ins, name)

        pe.wait_ge(S_("relu_ready"), hid_done[1] + 2)
        transposes(("xa", 0), lambda t: xs2[:, t, :], xs2_ready, first=6)
        pe.wait_ge(S_("out_added"), out_done[1] + 8)
        for b in range(4):
            wait_turned(2 * b)
        for t in range(NT):
            for n in range(2):
                project(t, n, ("q", n, t), 2 + 2 * n + t, ("mix2", 1, n), t == NT - 1)
            if t == 0:
                transposes(("xa", 1), lambda t: xs2[:, NT + t, :], xs2_ready, first=6)
        for b in range(4):
            wait_turned(2 * b)
        for t in range(2 * NT):
            project(t, 2, ("kv", t), 2 + t, ("mix2", 1, 2), t == 2 * NT - 1)
        pe.wait_ge(S_("q_rot_ready"), NT)
        for pair in range(4):
            name = ("qT", pair)
            ps = take(pe, name, pair)
            for head in (2 * pair, 2 * pair + 1):
                for t in range(NT):
                    at_ = (head % 2) * S + t * P
                    ins = turn(ps[:, at_:at_ + P], qr[:, t, head * P:(head + 1) * P], ident)
            fill(ins, name)
        pe.wait_ge(S_("k_rot_ready"), 2 * NT)
        for g in range(NKV):
            name = ("kT", g)
            ps = take(pe, name, 4 + g)
            for t in range(2 * NT):
                ins = turn(ps[:, t * P:(t + 1) * P], kv[:, t, 0, g * P:(g + 1) * P], ident)
            fill(ins, name)
        for pair in range(4):
            freed(pe, ("qT", pair))
        for g in range(NKV):
            freed(pe, ("kT", g))

        def scores(u):
            head, t = divmod(u, NT)
            name = ("s", u)
            ps = take(pe, name, (0, 1, 6, 7)[u % 4])
            ins = mm(ps[:, :], qT2[:, head, t * P:(t + 1) * P], kT2[:, head // 4, :],
                     start=True, stop=True)
            fill(ins, name)

        def turn_probs(u):
            name = ("pT", u)
            pe.wait_ge(S_("prob_ready"), u + 1)
            ps = take(pe, name, 2 + u % 2)
            for j in range(4):
                ins = turn(ps[:, j * P:(j + 1) * P], pr[:, u % 2, j * P:(j + 1) * P], ident)
            fill(ins, name)

        def values(head):
            name = ("o", head)
            freed(pe, ("pT", 2 * head))
            freed(pe, ("pT", 2 * head + 1))
            ps = take(pe, name, 4 + head % 2)
            g = head // 4
            for j in range(4):
                ins = mm(ps[:, 0:S], kv[:, j, 1, g * P:(g + 1) * P], prT[:, j, :],
                         start=j == 0, stop=j == 3)
            fill(ins, name)

        scores(0)
        scores(1)
        for u in range(NQ * NT):
            if u + 2 < NQ * NT:
                scores(u + 2)
            if u and u % 2 == 0:
                values(u // 2 - 1)
            turn_probs(u)
        values(NQ - 1)
        post_rows("rows_mix1", 1)
        post_rows("rows_mlp1", 1)
        freed(pe, ("o", NQ - 2))
        freed(pe, ("o", NQ - 1))
        for t in range(NT):
            for n in range(2):
                it = ("mix2", 1, 3 + n)
                w = wait_landed(pe, it).rearrange("p (c n) -> p c n", c=KC)
                name = ("wo", n, t)
                ps = take(pe, name, 4 + 2 * n + t)
                for c in range(KC):
                    ins = mm(ps[:, :], oT[:, c, t * P:(t + 1) * P], w[:, c, :], start=c == 0,
                             stop=c == KC - 1)
                if t == NT - 1:
                    fill_and_release(ins, name, it)
                else:
                    fill(ins, name)
        transposes(("xm1", 0), lambda t: xs2[:, t, :], xs2_ready, first=0)
        for b in range(8):
            pe.wait_ge(bank_free[b], frees[b])
        mlp(1, 1)

    @block.scalar
    def _(act):
        turn = InTurn(act, "act_step")
        raw = nc.scalar.activation
        f, step, free = turn(raw), turn.tick, turn.free
        seen = {}

        def expect(name, k=1):
            seen[name] = seen.get(name, 0) + k
            act.wait_ge(S_(name), seen[name])

        def norm_stats(tiles, ready, src, junk, width=D, first=0):
            for t in range(tiles):
                ready(t)
                step(f(junk(t), src(t), ACT.Square, accum_out=ssq[:, first + t:first + t + 1]))
            cols_ = slice(first, first + tiles)
            f(std[:, cols_], ssq[:, cols_], ACT.Sqrt, bias=eps[:, :],
              scale=1.0 / width).then_inc(S_("std_ready"), 1)

        def odd_chunks(tag, out, gain, shift=None):
            for b in (1, 3):
                ps = full(act, (tag, b))
                for c in (2 * b, 2 * b + 1):
                    kw = {} if shift is None else {"bias": shift(c)}
                    at_ = (c % 2) * S
                    ins = f(out(c), ps[:, at_:at_ + S], ACT.Identity, scale=gain(c), **kw)
                    if c % 2 == 0:
                        step(ins)
                free(ins, (tag, b))

        def high_chunks(tag, gain):
            for b in (1, 3):
                ps = full(act, (tag, b))
                for c in (2 * b, 2 * b + 1):
                    at_ = (c % 2) * S
                    step(f(xT[:, c, :], ps[:, at_:at_ + S], ACT.Identity, scale=gain(c)))
                    ins = f(xs_high[:, :, c, :],
                            ps[:, at_:at_ + S].rearrange("p (t n) -> p t n", t=NT),
                            ACT.Identity, scale=gain(c))
                    if c % 2 == 0:
                        step(ins)
                free(ins, (tag, b))

        def high_item(l, j):
            slot, _, value = split_item(l, j)
            before = split_item(l, j - 2)[1] + 1 if j >= 2 else items[("mix", l, 0)][1]
            if before:
                act.wait_ge(weights_used, before)
            act.wait_ge(landed[slot], value)
            for half in range(2):
                whole, high, _ = split_half(l, j, half)
                f(high, whole, ACT.Copy).then_inc(S_("mix_high_ready"), 1)

        act.dma_start(col[:, :], cols).then_inc(S_("cols"), 16)
        act.dma_start(ident_all[:, :], consts).then_inc(S_("consts"), 16)
        act.dma_start(AD[:, :, :].rearrange("p a b -> p (a b)")[:, 0:len(LEVELS) * P],
                      masks).then_inc(S_("masks"), 16)
        act.wait_ge(S_("ones_ready"), 1)
        act.wait_ge(S_("cols"), 16)

        def exp_and_silu():
            expect("lower_shifted")
            f(lb[:, 2, :, :], lb[:, 2, :, :], ACT.Exp).then_inc(S_("lower_exp"), 1)
            for i, name in enumerate(("c", "c_ctx")):
                f(cT[:, :, i], C(name), ACT.Silu).then_inc(S_("silu_c_ready"), 1)

        def x_tile_ready(l):
            def ready(t):
                if l == 0:
                    act.wait_ge(S_("x_landed"), 16)
                else:
                    for half in range(2):
                        freed(act, ("moe", l - 1, 2 * half + t))
            return ready

        for l in range(DEPTH):
            for t in range(NT):
                norm_stats(1, lambda _, t=t: x_tile_ready(l)(t), lambda _, t=t: h[:, t, :],
                           lambda _, t=t: xs[:, t, :], first=t)
            high_item(l, 0)
            high_chunks(("x1", l), lambda c: C("norm1_g", KC * l + c))
            high_item(l, 1)
            if l == 0:
                exp_and_silu()
            for j in (2, 3):
                high_item(l, j)
            for d, kind in enumerate((HFF, HFB)):
                for pair in range(2):
                    name = ("proj", l, kind, pair)
                    ps = full(act, name)
                    part = slice(2 * pair, 2 * pair + 2)
                    z = ps[:, :].rearrange("p (a t) -> p a t", a=2)
                    step(f(hf[:, d, part, :], z, ACT.Sigmoid))
                    free(f(hk[:, d, part, :], z, ACT.Sigmoid, scale=-1.0), name)
                high_item(l, 4 + d)
                if l == 0 and d == 0:
                    expect("lower_ready")
                for head in range(H4):
                    step(f(hf[:, d, head, :], hf[:, d, head, :], ACT.Identity,
                           scale=lb[:, 1, l, head:head + 1], bias=lb[:, 0, l, head:head + 1]))
                    ins = f(hk[:, d, head, :], hk[:, d, head, :], ACT.Identity,
                            scale=lb[:, 2, l, head:head + 1])
                    if head < H4 - 1:
                        step(ins)
                ins.then_inc(S_("forget_ready"), 1)
                for pair in range(2):
                    name = ("retT", l, d, pair)
                    ps = full(act, name)
                    free(f(retT[:, d, 2 * pair:2 * pair + 2, :],
                           ps[:, :].rearrange("p (a t) -> p a t", a=2), ACT.Copy), name)
            for pair in range(2):
                name = ("proj", l, HQ, pair)
                ps = full(act, name)
                free(f(hq[:, 2 * pair:2 * pair + 2, :],
                       ps[:, :].rearrange("p (a t) -> p a t", a=2), ACT.Silu), name)
            high_item(l, 6)
            act.wait_ge(S_("masks_ready"), 1)
            for t in range(2):
                name = ("same", l, t)
                ps = full(act, name)
                free(f(AD[:, 4 * t:4 * t + 4, :], ps[:, :].rearrange("p (a t) -> p a t", a=4),
                       ACT.Copy), name)
            where = {RV: ret_v, HI: hg_v, RG: ret_gate, HG: hg_gate}
            u, ada_n = 0, 0
            for n, kind in enumerate(mixer_items()):
                if kind == ADA:
                    name = ("ada", l, ada_n)
                    ps = full(act, name)
                    free(f(ada_s[:, :], ps[:, :], ACT.Copy), name)
                    ada_n += 1
                elif kind in where:
                    for t in range(NT):
                        name = ("proj", l, kind, t)
                        ps = full(act, name)
                        func = ACT.Silu if kind in (RG, HG) else ACT.Copy
                        free(f(where[kind][:, t, :], ps[:, :], func), name)
                        for _ in range(2):
                            if units[u][0] == P:
                                name = ("unit", l, u)
                                ps = full(act, name)
                                free(f(AO[:, units[u][1], :, :],
                                       ps[:, :].rearrange("p (a t) -> p a t", a=H4),
                                       ACT.Copy), name)
                            u += 1
                if n > 5 and n + 3 in SPLIT:
                    high_item(l, SPLIT.index(n + 3))
                if n == SPLIT[-1] - 1:
                    high_item(l, SPLITS - 2)
                if kind == HG:
                    for t in range(NT):
                        name = ("ret_o", l, t)
                        ps = full(act, name)
                        f(sq[:, t, :], ps[:, :], ACT.Square).then_inc(S_("ret_sq_ready"), 1)
                    for t in range(NT):
                        name = ("hgrn_o", l, t)
                        ps = full(act, name)
                        step(f(xs[:, t, W4:D], ps[:, :], ACT.Square,
                               accum_out=ssq[:, t:t + 1]))
                    f(std[:, 0:NT], ssq[:, 0:NT], ACT.Sqrt, bias=eps[:, :],
                      scale=1.0 / W4).then_inc(S_("std_ready"), 1)
                    expect("ret_sum_ready")
                    f(rstat[:, 1, :, :], rstat[:, 0, :, :], ACT.Sqrt, bias=eps[:, :],
                      scale=1.0 / P).then_inc(S_("ret_std_ready"), 1)

            def mix_gain(c):
                return C("ret_g", H4 * l + c) if c < H4 else C("hgrn_g", H4 * l + c - H4)

            high_item(l, SPLITS - 1)
            high_chunks(("mix", l), mix_gain)

            def out_ready(t):
                for n in range(2):
                    freed(act, ("w_out", l, n, t))

            def ada_row(n):
                name = ("ada", l, n)
                ps = full(act, name)
                free(f(ada_s[:, :], ps[:, :], ACT.Copy), name)

            for t in range(NT):
                norm_stats(1, lambda _, t=t: out_ready(t), lambda _, t=t: h[:, t, :],
                           lambda _, t=t: xs[:, t, :], first=t)
            ada_row(ADA_LATE[0])
            odd_chunks(("x2", l), lambda c: xT[:, c, :], lambda c: C("norm2_g", KC * l + c))
            expect("router_max_ready")
            name = ("logit", l)
            ps = full(act, name)
            for t in range(NT):
                ins = f(logit[:, t, :], ps[:, t * NEXP:(t + 1) * NEXP], ACT.Exp,
                        bias=rstats[:, t, 1:2], accum_out=rstats[:, t, 2:3])
                if t == 0:
                    step(ins)
            free(ins, name)
            for n in ADA_LATE[1:]:
                ada_row(n)
            with act.Fori(0, NEXP) as e:
                done = l * NEXP + e
                act.wait_ge(S_("gate_T_full"), done + 2)
                act.wait_ge(S_("scattered"), done + 1)
                raw(GT[:, :], psum[5][:, 0:S], ACT.Copy).then_inc(S_("gate_T_ready"), 1)
                act.wait_ge(weights_used, 6 * e + (moe_base[l] + 4))
                raw(silu_g[:, :], psum[4][:, 0:256], ACT.Silu).then_inc(S_("silu_g_ready"), 1)
                act.wait_ge(S_("hid_T_full"), done + 1)
                raw(hidT[:, :, :], psum[6][:, 0:S].rearrange("p (a b) -> p a b", a=2),
                  ACT.Copy).then_inc(S_("hid_T_ready"), 1)
                act.wait_ge(weights_used, 6 * e + (moe_base[l] + 6))
                raw(Y[:, 0:512], psum[5][:, :], ACT.Copy).then_inc(S_("y_left_ready"), 1)

        for t in range(NT):
            norm_stats(1, lambda _: x_tile_ready(DEPTH)(t), lambda _: h[:, t, :],
                       lambda _: xs2[:, t, :], first=t)

        def row_of(tag, i, row):
            for half in range(2):
                name = (tag, i, half)
                ps = full(act, name)
                free(f(rows[:, row, half * 512:(half + 1) * 512], ps[:, :], ACT.Copy), name)

        def next_rows(t):
            expect("x4_ready")

        def pre_norm(first, tiles=NT):
            norm_stats(tiles, next_rows, lambda t: x4[:, first + t, :],
                       lambda t: xs2[:, first + t, :], first=first)

        def post_norm(first, tiles=NT, ready=lambda t: expect("ys_ready")):
            norm_stats(tiles, ready, lambda t: ys[:, first + t, :],
                       lambda t: xs2[:, first + t, :], first=first)

        def odd_modulated(tag, s, l, which):
            odd_chunks((tag, s), lambda c: xT2[:, c, s * S:(s + 1) * S],
                       lambda c: mod_gain[:, l, which, s, c:c + 1],
                       lambda c: mods[:, l, 3 * which * KC + c, s:s + 1])

        def mlp_high(l, i, n, quarters, used=None):
            slot, number, value = items[("mlp", l, n % 4)]
            shift = n // 4
            if 0 in quarters:
                act.wait_ge(landed[slot], per_item[l] * (i + shift) + value)
                act.wait_ge(weights_used, used or 4 * (i + shift) + (number - 1))
            for q in quarters:
                raw(w_high[:, n % 2, quarter(q)], ring[:, slot, quarter(q)],
                    ACT.Copy).then_inc(S_("w_high_ready"), 1)

        def first_high(l):
            mlp_high(l, 0, 0, range(4), items[("mix2", l, 0)][1])

        def mlp(l, T):
            base_h, base_i = hid_done[l], mlp_base[l]

            def relus(i, b, units):
                for j in units:
                    if j < 3:
                        act.wait_ge(S_("hidden_full"), 6 * i + (24 * l + 3 * b + j + 1))
                    else:
                        act.wait_ge(weights_used, 4 * i + (base_i + b + 1))
                    act.wait_ge(S_("hidden_ready"), 8 * i + (base_h + 4 * b + j + 1))
                    raw(h_raw[:, j % 2, 0:T], psum[(4 * b + j) % 2][:, 0:T],
                        ACT.Relu).then_inc(S_("relu_ready"), 1)

            def blocks(i, last):
                for n in range(4):
                    plan = hidden_plan[l] if n < 2 else output_plan[l]
                    for unit in range(4):
                        if not (last and n == 3):
                            mlp_high(l, i, n + 1, plan.get(unit, ()))
                        if n < 2:
                            relus(i, n, (unit,))

            with act.Fori(0, 3) as i:
                blocks(i, False)
            blocks(3, True)
            turn.mine = None

        def high_modulated(tag, s, l):
            for b in (1, 3):
                ps = full(act, ((tag, s), b))
                for c in (2 * b, 2 * b + 1):
                    at_ = (c % 2) * S
                    step(f(x_full[:, c, s * S:(s + 1) * S], ps[:, at_:at_ + S], ACT.Identity,
                           scale=mod_gain[:, l, 1, s, c:c + 1],
                           bias=mods[:, l, 3 * KC + c, s:s + 1]))
                part = slice(2 * b, 2 * b + 2)
                free(f(x_high[:, part, s * S:(s + 1) * S], x_full[:, part, s * S:(s + 1) * S],
                       ACT.Copy), ((tag, s), b))

        for t in range(NT):
            pre_norm(t, 1)
        act.wait_ge(S_("ctx_landed"), 16)
        norm_stats(NT, lambda t: None, lambda t: x4[:, 2 + t, :], lambda t: xs2[:, 2 + t, :],
                   first=2)
        for s in range(2):
            row_of("rows_mix0", s, s)
        first_high(0)
        for s in range(2):
            odd_chunks(("pool_d", s), lambda c, s=s: diffT[:, c, s * S:(s + 1) * S],
                       lambda c, s=s: mod_gain[:, 0, 0, s, c:c + 1])
        for t in range(2 * NT):
            for half in range(2):
                name = ("pool_y", t, half)
                ps = full(act, name)
                free(f(ys[:, t, half * 512:(half + 1) * 512], ps[:, :], ACT.Copy), name)
            if t % NT:
                post_norm(t - 1, ready=lambda t: None)
        act.wait_ge(S_("pool_w_ready"), 1)
        row_of("rows_mlp0", 0, 2)
        pre_norm(0)
        row_of("rows_mlp0", 1, 0)
        pre_norm(2)
        for s in range(2):
            high_modulated("xm0", s, 0)
        mlp(0, 2 * S)
        post_norm(0)
        pre_norm(0)
        post_norm(2)
        odd_modulated("xa", 0, 1, 0)
        pre_norm(2)
        for t in range(NT):
            for n in range(2):
                name = ("q", n, t)
                ps = full(act, name)
                part = slice(n * 512, (n + 1) * 512)
                step(f(q_raw[:, t, part], ps[:, :], ACT.Copy))
                free(f(q_sq[:, t, part], ps[:, :], ACT.Square), name)
            if t == 0:
                odd_modulated("xa", 1, 1, 0)
            expect("q_sum_ready")
            heads = slice(t * NQ, (t + 1) * NQ)
            f(qst[:, 1, heads], qst[:, 0, heads], ACT.Sqrt, bias=eps[:, :],
              scale=1.0 / P).then_inc(S_("q_std_ready"), 1)
        for t in range(2 * NT):
            name = ("kv", t)
            ps = full(act, name)
            step(f(kv[:, t, :, :], ps[:, :].rearrange("p (a b) -> p a b", a=2), ACT.Copy))
            free(f(xs2[:, t, 0:2 * P], ps[:, 0:2 * P], ACT.Square), name)
            expect("k_sum2_ready")
            heads = slice(t * NKV, (t + 1) * NKV)
            f(kst[:, 1, heads], kst[:, 0, heads], ACT.Sqrt, bias=eps[:, :],
              scale=1.0 / P).then_inc(S_("k_std_ready"), 1)
        for pair in range(4):
            name = ("qT", pair)
            ps = full(act, name)
            free(f(qT2[:, 2 * pair:2 * pair + 2, :], ps[:, :].rearrange("p (a t) -> p a t", a=2),
                   ACT.Copy), name)

        def exponentials(u):
            expect("score_max_ready")
            name = ("s", u)
            ps = full(act, name)
            free(f(pr[:, u % 2, :], ps[:, :], ACT.Exp, bias=soft[:, u % 4, 1:2],
                   scale=HEAD_SCALE, accum_out=soft[:, u % 4, 2:3]), name)

        exponentials(0)
        for u in range(NQ * NT):
            if u + 1 < NQ * NT:
                exponentials(u + 1)
            name = ("pT", u)
            ps = full(act, name)
            t = u % NT
            free(f(prT[:, :, t * P:(t + 1) * P], ps[:, :].rearrange("p (a t) -> p a t", a=4),
                   ACT.Copy), name)
        first_high(1)
        row_of("rows_mix1", 0, 0)
        row_of("rows_mlp1", 0, 1)
        for t in range(NT):
            for n in range(2):
                name = ("wo", n, t)
                ps = full(act, name)
                free(f(ys[:, t, n * 512:(n + 1) * 512], ps[:, :], ACT.Copy), name)
            post_norm(t, 1, ready=lambda t: None)
            pre_norm(t, 1)
        high_modulated("xm1", 0, 1)
        mlp(1, S)
        for t in range(NT):
            post_norm(t, 1)

    @block.vector
    def _(dve):
        turn = InTurn(dve, "dve_step")
        tick, step, free = turn.tick, turn.tick, turn.free
        v = nc.vector
        tt, ts, stt = turn(v.tensor_tensor), turn(v.tensor_scalar), turn(v.scalar_tensor_tensor)
        copy, reciprocal, reduce = turn(v.tensor_copy), turn(v.reciprocal), turn(v.tensor_reduce)
        memset, top8, top8_at = turn(v.memset), turn(v.max), turn(v.max_index)
        replace, copy_where = turn(v.match_replace), turn(v.copy_predicated)
        seen = {}

        def expect(name, k=1):
            seen[name] = seen.get(name, 0) + k
            dve.wait_ge(S_(name), seen[name])

        def normalise(tiles, src, out, signal, first=0):
            expect("std_ready")
            step(reciprocal(rinv[:, first:first + tiles], std[:, first:first + tiles]))
            for t in range(tiles):
                ts(out(t), src(t), rinv[:, first + t:first + t + 1], None,
                   ALU.mult).then_inc(S_(signal), 1)

        def even_chunks(tag, out, gain, shift=None):
            for b in (0, 2):
                ps = full(dve, (tag, b))
                for c in (2 * b, 2 * b + 1):
                    at_ = (c % 2) * S
                    if shift is None:
                        ins = ts(out(c), ps[:, at_:at_ + S], gain(c), None, ALU.mult)
                    else:
                        ins = ts(out(c), ps[:, at_:at_ + S], gain(c), shift(c), ALU.mult,
                                 ALU.add)
                    if c % 2 == 0:
                        tick(ins)
                free(ins, (tag, b))

        def split_chunks(tag, gain):
            for b in (0, 1, 2, 3) if tag[0] == "mix" else (0, 2):
                if b % 2 == 0:
                    ps = full(dve, (tag, b))
                    for c in (2 * b, 2 * b + 1):
                        at_ = (c % 2) * S
                        tick(ts(xT[:, c, :], ps[:, at_:at_ + S], gain(c), None, ALU.mult))
                        ins = ts(xs_high[:, :, c, :],
                                 ps[:, at_:at_ + S].rearrange("p (t n) -> p t n", t=NT),
                                 gain(c), None, ALU.mult)
                        if c % 2 == 0:
                            tick(ins)
                    free(ins, (tag, b))
                else:
                    freed(dve, (tag, b))
                low_chunks(tt, b).then_inc(S_("mix_x_split"), 1)

        def lower_bounds():
            dve.wait_ge(S_("cols"), 16)
            low = C("lower").rearrange("p (l h) -> p l h", l=DEPTH)
            step(tt(lb[:, 0, 0, :], low[:, 0, :], low[:, 1, :], ALU.max))
            tt(lb[:, 2, :, :], low, lb[:, 0, 0:1, :].broadcast_to([P, DEPTH, H4]),
               ALU.subtract).then_inc(S_("lower_shifted"), 1)
            expect("lower_exp")
            step(tt(lb[:, 0, 0, :], lb[:, 2, 0, :], lb[:, 2, 1, :], ALU.add))
            step(reciprocal(lb[:, 0, 1, :], lb[:, 0, 0, :]))
            step(tt(lb[:, 1, :, :], lb[:, 2, :, :], lb[:, 0, 1:2, :].broadcast_to([P, DEPTH, H4]),
                    ALU.mult))
            step(tt(lb[:, 0, 1, :], lb[:, 1, 0, :], lb[:, 1, 1, :], ALU.add))
            tick(tt(lb[:, 0, 0, :], lb[:, 1, 0, :], lb[:, 1, 0, :], ALU.subtract))
            step(tt(lb[:, 0, 1, :], lb[:, 0, 1, :], lb[:, 1, 0, :], ALU.subtract))
            step(ts(lb[:, 1, :, :], lb[:, 0, :, :], -1.0, 1.0, ALU.mult, ALU.add))
            ts(lb[:, 2, :, :], lb[:, 1, :, :], HEAD_SCALE, None,
               ALU.mult).then_inc(S_("lower_ready"), 1)
            dve.wait_ge(S_("masks"), 16)
            copy(mask[:, :, :, :].rearrange("p a b c -> p (a b c)"),
                 AD[:, :, :].rearrange("p a b -> p (a b)")[:, 0:len(LEVELS) * P]).then_inc(
                S_("masks_ready"), 1)

        dve.wait_ge(S_("x_landed"), 16)

        for l in range(DEPTH):
            for t in range(NT):
                normalise(1, lambda _: h[:, t, :], lambda _: xs[:, t, :], "xs_ready", first=t)
            low_item(tt, dve, l, 0)
            if l == 0:
                dve.wait_ge(S_("cols"), 16)
            split_chunks(("x1", l), lambda c: C("norm1_g", KC * l + c))
            low_item(tt, dve, l, 1)
            if l == 0:
                lower_bounds()
            dve.wait_ge(S_("consts"), 16)
            cos = K("cos").rearrange("p (t d) -> p t d", t=NT)
            sin = K("sin").rearrange("p (t b d) -> p t b d", t=NT, b=2)
            for i, kind in enumerate((RQ, RK)):
                for t in range(NT):
                    name = ("proj", l, kind, t)
                    ps = full(dve, name)
                    rows_ = ps[:, :].rearrange("p (h d) -> p h d", h=H4)
                    halves = ps[:, :].rearrange("p (h b d) -> p h b d", h=H4, b=2)
                    tick(tt(rope_t[:, 0, :].rearrange("p (h d) -> p h d", h=H4), rows_,
                            cos[:, t, :].unsqueeze(1).broadcast_to([P, H4, P]), ALU.mult))
                    for b in range(2):
                        ins = tt(rope_t[:, 1, :].rearrange("p (h b d) -> p h b d", h=H4, b=2)
                                 [:, :, b, :], halves[:, :, 1 - b, :],
                                 sin[:, t, b, :].unsqueeze(1).broadcast_to([P, H4, 64]), ALU.mult)
                        if b == 0:
                            tick(ins)
                    free(ins, name)
                    tt(rot[:, i, t, :], rope_t[:, 0, :], rope_t[:, 1, :],
                       ALU.add).then_inc(S_("rot_ready"), 1)
                low_item(tt, dve, l, 2 + i)
            low_item(tt, dve, l, 4)
            expect("forget_ready", 2)
            tt(hx[:, 0, :, :], hk[:, 0, :, :], hk[:, 1, :, :],
               ALU.add).then_inc(S_("k_sum_ready"), 1)
            decay = K("decay").rearrange("p (h c) -> p h c", h=H4)
            for head in range(H4):
                name = ("ret_s", l, head)
                ps = full(dve, name)
                tick(tt(RS_[:, 0, head, :], ps[:, 0:S], decay[:, head, P:3 * P], ALU.mult))
                free(tt(RS_[:, 1, head, :], ps[:, S:2 * S], decay[:, head, 0:2 * P], ALU.mult),
                     name)

            def split(x, m):
                return x.rearrange("p h (n b m) -> p (h n) b m", b=2, m=m)

            def prepare(u):
                m, d = units[u]
                q_half, k_half = (1, 0) if d == 0 else (0, 1)
                if m > 1:
                    if u == 2:
                        expect("kdec_ready")
                    if m == P:
                        part = slice(k_half * P, (k_half + 1) * P)
                        tick(tt(kdec[:, d, :, part], hk[:, d, :, part], hx[:, d, :, part],
                                ALU.mult))
                    else:
                        tick(tt(split(kdec[:, d, :, :], m)[:, :, k_half, :],
                                split(hk[:, d, :, :], m)[:, :, k_half, :],
                                split(hx[:, d, :, :], m)[:, :, k_half, :], ALU.mult))
                if m == P:
                    part = slice(q_half * P, (q_half + 1) * P)
                    ins = tt(qdec[:, d, :, :], hq[:, :, part], hf[:, d, :, part], ALU.mult)
                else:
                    ins = tt(qdec[:, d, :, :].rearrange("p h (n m) -> p (h n) m", m=m),
                             split(hq[:, :, :], m)[:, :, q_half, :],
                             split(hf[:, d, :, :], m)[:, :, q_half, :], ALU.mult)
                ins.then_inc(S_("level_ready"), 1)

            def widen(u):
                m, d = units[u]
                q_half, k_half = (1, 0) if d == 0 else (0, 1)
                prod, excl = split(hf[:, d, :, :], m), split(hx[:, d, :, :], m)
                shape = [P, H4 * S // (2 * m), m]
                end = m - 1 if d == 0 else 0
                whole_q = prod[:, :, q_half, end:end + 1]
                whole_k = prod[:, :, k_half, end:end + 1]
                if m == 1:
                    tick(memset(excl[:, :, q_half, :], 1.0))
                    tick(copy(excl[:, :, k_half, :], whole_q))
                else:
                    tick(tt(excl[:, :, k_half, :], excl[:, :, k_half, :],
                            whole_q.broadcast_to(shape), ALU.mult))
                tick(tt(prod[:, :, q_half, :], prod[:, :, q_half, :],
                                  whole_k.broadcast_to(shape), ALU.mult))

            def merge(u):
                m, d = units[u]
                name = ("unit", l, u)
                ps = full(dve, name)
                q_half = 1 if d == 0 else 0
                blocks = P // (2 * m)
                outs = AD[:, :, :].rearrange("p a (n b m) -> p a n b m", b=2, m=m)
                wide = [P, 2 * H4, blocks, m]
                where = mask[:, LEVELS.index(m), d, :].rearrange("p (n m) -> p n m", m=m)
                free(copy_where(outs[:, :, :, q_half, :],
                                       where.unsqueeze(1).broadcast_to(wide),
                                       ps[:, :].rearrange("p (a n m) -> p a n m", a=2 * H4, m=m)),
                     name)

            def ada_bias(n):
                name = ("ada_c", l, n)
                ps = full(dve, name)
                bias = C("b_ada", NMOD * KC * l + 4 * n, 4)
                free(tt(mods[:, l, 4 * n:4 * n + 4, :],
                        ps[:, 0:8].rearrange("p (a b) -> p a b", b=2),
                        bias.unsqueeze(2).broadcast_to([P, 4, 2]), ALU.add), name)

            for pair in range(2):
                freed(dve, ("proj", l, HQ, pair))
                freed(dve, ("same", l, pair))
            u, ada_n = 0, 0

            def one_unit(u):
                prepare(u)
                if units[u][0] < P:
                    widen(u)
                if 1 <= u <= 2 * len(LEVELS):
                    merge(u - 1)

            for kind in mixer_items()[5:]:
                if kind == ADA:
                    if ada_n:
                        ada_bias(ada_n - 1)
                    ada_n += 1
                else:
                    for _ in range(4):
                        one_unit(u)
                        u += 1
                if kind == HG:
                    for t in range(NT):
                        expect("ret_sq_ready")
                        ins = reduce(rstat[:, 0, t, :],
                                              sq[:, t, :].rearrange("p (h d) -> p h d", h=H4),
                                              AX.X, ALU.add)
                        if t == 0:
                            tick(ins)
                    ins.then_inc(S_("ret_sum_ready"), 1)
                    expect("std_ready")
                    step(reciprocal(rinv[:, 0:NT], std[:, 0:NT]))
                    for t in range(NT):
                        name = ("hgrn_o", l, t)
                        ps = full(dve, name)
                        freed(dve, ("proj", l, HG, t))
                        free(stt(xs[:, t, W4:D], ps[:, :], rinv[:, t:t + 1], hg_gate[:, t, :],
                                 ALU.mult, ALU.mult), name)
                    expect("ret_std_ready")
                    step(reciprocal(rstat[:, 2, :, :], rstat[:, 1, :, :]))
                    for t in range(NT):
                        freed(dve, ("proj", l, RG, t))
                        gate = ret_gate[:, t, :].rearrange("p (h d) -> p h d", h=H4)
                        step(tt(gate, gate, rstat[:, 2, t, :].unsqueeze(2)
                                .broadcast_to([P, H4, P]), ALU.mult))
                        name = ("ret_o", l, t)
                        free(tt(xs[:, t, 0:W4], psum[where_is[name][0]][:, :],
                                ret_gate[:, t, :], ALU.mult), name)
            def mix_gain(c):
                return C("ret_g", H4 * l + c) if c < H4 else C("hgrn_g", H4 * l + c - H4)

            split_chunks(("mix", l), mix_gain)
            for t in range(NT):
                for n in range(2):
                    name = ("w_out", l, n, t)
                    ps = full(dve, name)
                    part = slice(n * 512, (n + 1) * 512)
                    free(tt(h[:, t, part], h[:, t, part], ps[:, :], ALU.add), name)
                if t:
                    normalise(1, lambda _: h[:, t - 1, :], lambda _: xs[:, t - 1, :],
                              "xs_ready", first=t - 1)
            normalise(1, lambda _: h[:, NT - 1, :], lambda _: xs[:, NT - 1, :], "xs_ready",
                      first=NT - 1)
            ada_bias(ADA_EARLY - 1)
            even_chunks(("x2", l), lambda c: xT[:, c, :], lambda c: C("norm2_g", KC * l + c))
            name = ("logit", l)
            ps = full(dve, name)
            step(reduce(rstats[:, :, 0], ps[:, 0:NT * NEXP]
                                 .rearrange("p (t e) -> p t e", t=NT), AX.X, ALU.max))
            ts(rstats[:, :, 1], rstats[:, :, 0], -1.0, None,
               ALU.mult).then_inc(S_("router_max_ready"), 1)
            freed(dve, name)
            step(reciprocal(rstats[:, :, 3], rstats[:, :, 2]))
            for t in range(NT):
                ts(aff[:, t, :], logit[:, t, :], rstats[:, t, 3:4], None,
                   ALU.mult).then_inc(S_("affinity_ready"), 1)
            name = ("affT", l)
            ps = full(dve, name)
            free(copy(affT[:, 0, :], ps[0:NEXP, 0:S]), name)
            freed(dve, name)
            for r in range(CAP // 8):
                part = slice(8 * r, 8 * r + 8)
                a, b = affT[:, r % 2, :], affT[:, 1 - r % 2, :]
                step(top8(top[:, part], a))
                tick(top8_at(topi[:, part], top[:, part], a))
                if r < CAP // 8 - 1:
                    tick(replace(b, top[:, part], a, -1.0))
            step(copy(topf[:, :], topi[:, :]))
            delta = K("delta")[0:NEXP, :].unsqueeze(2).broadcast_to([NEXP, NEXP, CAP])
            for i, what in enumerate((topf, top)):
                tt(spread[:, i, :, :], what[:, :].unsqueeze(1).broadcast_to([NEXP, NEXP, CAP]),
                   delta, ALU.mult).then_inc(S_("spread_ready"), 1)
            name = ("ada_c", l, "late")
            ps = full(dve, name)
            n = 4 * len(ADA_LATE)
            free(tt(mods[:, l, 4 * ADA_EARLY:4 * ADA_ALL, :],
                    ps[:, 0:2 * n].rearrange("p (a b) -> p a b", b=2),
                    C("b_ada", NMOD * KC * l + 4 * ADA_EARLY, n).unsqueeze(2)
                    .broadcast_to([P, n, 2]), ALU.add), name)
            if l == DEPTH - 1:
                for l2 in range(DEPTH):
                    for which, pre in enumerate(("g_mix_pre", "g_mlp_pre")):
                        for s in range(2):
                            at_ = (3 * which + 1) * KC
                            tick(stt(mod_gain[:, l2, which, s, :],
                                     mods[:, l2, at_:at_ + KC, s], 1.0, C(pre, KC * l2, KC),
                                     ALU.add, ALU.mult))

            name = ("spread", l, 0)
            ps = full(dve, name)
            for t in range(NT):
                ins = ts(onehot[:, t, :], ps[:, :], K("token")[:, t:t + 1], None, ALU.is_equal)
                if t == 0:
                    tick(ins)
            free(ins, name)
            freed(dve, name)
            name = ("spread", l, 1)
            ps = full(dve, name)
            for t in range(NT):
                ins = tt(gated[:, t, :], onehot[:, t, :], ps[:, :], ALU.mult)
                if t == 0:
                    tick(ins)
            free(ins, name)
            freed(dve, name)
            gain2 = C("norm2_g", KC * l, KC).unsqueeze(2).broadcast_to([P, KC, CAP])
            with dve.Fori(0, NEXP) as e:
                done = l * NEXP + e
                dve.wait_ge(S_("gate_T_full"), done + 1)
                nc.vector.tensor_copy(gsel[:, :, :, :], gated[:, :, bass.ds(e * CAP, CAP)].unsqueeze(2)
                              .broadcast_to([P, NT, 4, CAP])).then_inc(S_("gate_sel_ready"), 1)
                dve.wait_ge(S_("gathered"), done + 1)
                nc.vector.tensor_tensor(xeT[:, :, :], psum[7][:, 0:S].rearrange("p (c s) -> p c s", c=KC), gain2,
                   ALU.mult).then_inc(S_("xeT_ready"), 1)
                dve.wait_ge(S_("silu_g_ready"), done + 1)
                dve.wait_ge(weights_used, 6 * e + (moe_base[l] + 4))
                nc.vector.tensor_tensor(hidE[:, :], silu_g[:, :], psum[4][:, 256:512],
                   ALU.mult).then_inc(S_("hid_e_ready"), 1)
                dve.wait_ge(weights_used, 6 * e + (moe_base[l] + 6))
                nc.vector.tensor_copy(Y[:, 512:D], psum[6][:, :]).then_inc(S_("y_right_ready"), 1)
            dve.wait_ge(S_("scattered"), (l + 1) * NEXP + 1)
            for t in range(NT):
                for half in range(2):
                    b = 2 * half + t
                    part = slice(half * 512, (half + 1) * 512)
                    free(tt(h[:, t, part], h[:, t, part], psum[b][:, :], ALU.add), ("moe", l, b))

        dve.wait_ge(S_("final_g_landed"), 16)
        for t in range(NT):
            expect("std_ready")
            step(reciprocal(rinv[:, t:t + 1], std[:, t:t + 1]))
            stt(x4[:, t, :], h[:, t, :], rinv[:, t:t + 1], gfin[:, :], ALU.mult,
                ALU.mult).then_inc(S_("x4_ready"), 1)

        def normalise_x4(first, tiles=NT):
            normalise(tiles, lambda t: x4[:, first + t, :], lambda t: xs2[:, first + t, :],
                      "xs2_ready", first=first)

        def even_modulated(tag, s, l, which):
            even_chunks((tag, s), lambda c: xT2[:, c, s * S:(s + 1) * S],
                        lambda c: mod_gain[:, l, which, s, c:c + 1],
                        lambda c: mods[:, l, 3 * which * KC + c, s:s + 1])

        def add_branch(tag, i, row, first, tiles=NT):
            freed(dve, (tag, i, 0))
            freed(dve, (tag, i, 1))
            expect("std_ready")
            step(reciprocal(rinv[:, first:first + tiles], std[:, first:first + tiles]))
            for t in range(first, first + tiles):
                tick(stt(ys[:, t, :], ys[:, t, :], rinv[:, t:t + 1], rows[:, row, :],
                         ALU.mult, ALU.mult))
                tt(x4[:, t, :], x4[:, t, :], ys[:, t, :], ALU.add).then_inc(S_("x4_ready"), 1)

        def split_modulated(tag, s, l):
            cols_ = slice(s * S, (s + 1) * S)
            for b in (0, 2):
                ps = full(dve, ((tag, s), b))
                for c in (2 * b, 2 * b + 1):
                    at_ = (c % 2) * S
                    ins = ts(x_full[:, c, cols_], ps[:, at_:at_ + S],
                             mod_gain[:, l, 1, s, c:c + 1], mods[:, l, 3 * KC + c, s:s + 1],
                             ALU.mult, ALU.add)
                    if c % 2 == 0:
                        tick(ins)
                free(ins, ((tag, s), b))
                part = slice(2 * b, 2 * b + 2)
                tick(copy(x_high[:, part, cols_], x_full[:, part, cols_]))
                ins = tt(x_low[:, part, cols_], x_full[:, part, cols_],
                         x_high[:, part, cols_].bitcast(F32), ALU.subtract)
                if b == 0:
                    tick(ins)
            ins.then_inc(S_("x_split"), 1)

        def mlp_low(l, i, n, quarters):
            slot = items[("mlp", l, n % 4)][0]
            for q in quarters:
                dve.wait_ge(S_("w_high_ready"), 16 * i + (64 * l + 4 * n + q + 1))
                nc.vector.tensor_tensor(w_low[:, slot, quarter(q)], ring[:, slot, quarter(q)],
                                        w_high[:, n % 2, quarter(q)].bitcast(F32),
                                        ALU.subtract).then_inc(S_("w_split"), 1)

        def first_low(l):
            mlp_low(l, 0, 0, range(4))

        def mlp(l, streams, after):
            T, tiles = streams * S, streams * NT
            base_h, base_o, base_i = hid_done[l], out_done[l], mlp_base[l]
            h_high, h_low = mlp_parts[l]
            vector = nc.vector

            def squares(i, b, units):
                if 0 in units:
                    dve.wait_ge(weights_used, 4 * i + (base_i - 1 + b))
                for j in units:
                    k = base_h + 4 * b + j
                    dve.wait_ge(S_("relu_ready"), 8 * i + (k + 3))
                    q = h_raw[:, j % 2, 0:T]
                    vector.tensor_tensor(q, q, q, ALU.mult).then_inc(S_("squared"), 1)
                    dve.wait_ge(S_("squared"), 8 * i + (k + 1))
                    vector.tensor_copy(h_high[:, b, j, 0:T], q).then_inc(S_("squared_high"), 1)
                    dve.wait_ge(S_("squared_high"), 8 * i + (k + 1))
                    vector.tensor_tensor(h_low[:, b, j, 0:T], q,
                                         h_high[:, b, j, 0:T].bitcast(F32),
                                         ALU.subtract).then_inc(S_("hidden_ready"), 1)

            def sums(i, b, some):
                for t in some:
                    for half in range(2):
                        k = (b * tiles + t) * 2 + half
                        if (t, half) == (tiles - 1, 1):
                            dve.wait_ge(weights_used, 4 * i + (base_i + 3 + b))
                        else:
                            dve.wait_ge(S_("out_full"), (4 * tiles - 2) * i
                                        + (8 * 7 * l + k - b + 1))
                        dve.wait_ge(S_("out_added"), 4 * tiles * i + (base_o + 9 + k - 2 * tiles))
                        part = slice(half * 512, (half + 1) * 512)
                        vector.tensor_tensor(ys[:, t, part], ys[:, t, part],
                                             psum[2 + k % 4][:, :],
                                             ALU.add).then_inc(S_("out_added"), 1)

            def blocks(i, last):
                for n in range(4):
                    plan = hidden_plan[l] if n < 2 else output_plan[l]
                    for unit in range(4 if n < 2 else tiles):
                        if not (last and n == 3):
                            mlp_low(l, i, n + 1, plan.get(unit, ()))
                        if n < 2:
                            squares(i, n, (unit,))
                        elif not (last and n == 3):
                            sums(i, n - 2, (unit,))

            with dve.Fori(0, 3) as i:
                blocks(i, False)
            blocks(3, True)
            turn.mine = None
            for t in range(tiles):
                sums(3, 1, (t,))
                dve.wait_ge(S_("out_added"), base_o + 8 + 16 * tiles - 2 * (tiles - 1 - t))
                memset(soft[:, 0, 3:4], 0.0).then_inc(S_("ys_ready"), 1)
                after(t)

        for t in range(NT):
            normalise_x4(t, 1)
        normalise_x4(2)
        for s in range(2):
            even_chunks(("pool_d", s), lambda c, s=s: diffT[:, c, s * S:(s + 1) * S],
                        lambda c, s=s: mod_gain[:, 0, 0, s, c:c + 1])
        first_low(0)
        add_branch("rows_mix0", 0, 0, 0)
        add_branch("rows_mix0", 1, 1, 2)
        normalise_x4(0)
        normalise_x4(2)
        step(memset(soft[:, :, :], 0.0))
        memset(soft[:, 3, 3:4], 0.0).then_inc(S_("relu_ready"), 2)
        memset(soft[:, 3, 3:4], 0.0).then_inc(S_("hidden_ready"), 2)
        memset(soft[:, 3, 3:4], 0.0).then_inc(S_("out_added"), 8)
        for s in range(2):
            split_modulated("xm0", s, 0)
        dve.wait_ge(S_("ys_cleared"), 1)

        def latents_first(t):
            if t == NT:
                add_branch("rows_mlp0", 0, 2, 0)
            elif t == 2 * NT - 1:
                normalise_x4(0)
                even_modulated("xa", 0, 1, 0)
                add_branch("rows_mlp0", 1, 0, 2)
                normalise_x4(2)
                even_modulated("xa", 1, 1, 0)

        mlp(0, 2, latents_first)

        dve.wait_ge(S_("rope2_landed"), 16)
        dve.wait_ge(S_("gqk_landed"), 16)
        full(dve, ("rows_mlp0", 1, 1))
        for i in range(2):
            g = gqk[:, i, :]
            g4 = g.rearrange("p (a b d) -> p a b d", a=2, b=2)
            tick(tt(rope_g[:, i, 0, :, :], rope_c[:, 0, :, :],
                    g.unsqueeze(1).broadcast_to([P, NT, P]), ALU.mult))
            for t in range(NT):
                sin4 = rope_c[:, 1, t, :].rearrange("p (a b d) -> p a b d", a=2, b=2)
                out4 = rope_g[:, i, 1, t, :].rearrange("p (a b d) -> p a b d", a=2, b=2)
                for b in range(2):
                    tick(tt(out4[:, :, b, :], sin4[:, :, b, :], g4[:, :, 1 - b, :], ALU.mult))
        def rotate(x, t, heads, i, tmp, out):
            quarters = x.rearrange("p (h b d) -> p h b d", h=2 * heads, b=2)
            tmp4 = tmp[1].rearrange("p (h b d) -> p h b d", h=2 * heads, b=2)
            sin4 = rope_g[:, i, 1, t, :].rearrange("p (a b d) -> p a b d", a=2, b=2)
            cos_ = rope_g[:, i, 0, t, :].unsqueeze(1).broadcast_to([P, heads, P])
            tick(tt(tmp[0].rearrange("p (h d) -> p h d", h=heads),
                    x.rearrange("p (h d) -> p h d", h=heads), cos_, ALU.mult))
            for b in range(2):
                for a in range(2):
                    tick(tt(tmp4[:, a::2, b, :], quarters[:, a::2, 1 - b, :],
                                sin4[:, a, b, :].unsqueeze(1).broadcast_to([P, heads, 32]),
                                ALU.mult))
            return tt(out, tmp[0], tmp[1], ALU.add)

        for t in range(NT):
            for n in range(2):
                freed(dve, ("q", n, t))
            heads = slice(t * NQ, (t + 1) * NQ)
            reduce(qst[:, 0, heads], q_sq[:, t, :].rearrange("p (h d) -> p h d", h=NQ), AX.X,
                   ALU.add).then_inc(S_("q_sum_ready"), 1)
            expect("q_std_ready")
            step(reciprocal(qst[:, 2, heads], qst[:, 1, heads]))
            rows_ = q_raw[:, t, :].rearrange("p (h d) -> p h d", h=NQ)
            step(tt(rows_, rows_, qst[:, 2, heads].unsqueeze(2).broadcast_to([P, NQ, P]),
                    ALU.mult))
            rotate(q_raw[:, t, :], t, NQ, 0, (q_tmp[:, 0, :], q_tmp[:, 1, :]),
                   qr[:, t, :]).then_inc(S_("q_rot_ready"), 1)
        for t in range(2 * NT):
            freed(dve, ("kv", t))
            heads = slice(t * NKV, (t + 1) * NKV)
            reduce(kst[:, 0, heads], xs2[:, t, 0:2 * P].rearrange("p (h d) -> p h d", h=NKV),
                   AX.X, ALU.add).then_inc(S_("k_sum2_ready"), 1)
            expect("k_std_ready")
            step(reciprocal(kst[:, 2, heads], kst[:, 1, heads]))
            k_ = kv[:, t, 0, :]
            rows_ = k_.rearrange("p (h d) -> p h d", h=NKV)
            step(tt(rows_, rows_, kst[:, 2, heads].unsqueeze(2).broadcast_to([P, NKV, P]),
                    ALU.mult))
            if t < NT:
                ins = rotate(k_, t, NKV, 1, (q_tmp[:, 0, 0:2 * P], q_tmp[:, 1, 0:2 * P]), k_)
            else:
                ins = tt(rows_, rows_, gqk[:, 1, :].unsqueeze(1).broadcast_to([P, NKV, P]),
                         ALU.mult)
            ins.then_inc(S_("k_rot_ready"), 1)
        for g in range(NKV):
            name = ("kT", g)
            ps = full(dve, name)
            free(copy(kT2[:, g, :], ps[:, :]), name)

        def score_max(u):
            name = ("s", u)
            ps = full(dve, name)
            step(reduce(soft[:, u % 4, 0:1], ps[:, :], AX.X, ALU.max))
            ts(soft[:, u % 4, 1:2], soft[:, u % 4, 0:1], -HEAD_SCALE, None,
               ALU.mult).then_inc(S_("score_max_ready"), 1)

        def take_values(head):
            name = ("o", head)
            ps = full(dve, name)
            free(copy(oT[:, head, :], ps[:, 0:S]), name)

        score_max(0)
        score_max(1)
        for u in range(NQ * NT):
            freed(dve, ("s", u))
            step(reciprocal(soft[:, u % 4, 3:4], soft[:, u % 4, 2:3]))
            ts(pr[:, u % 2, :], pr[:, u % 2, :], soft[:, u % 4, 3:4], None,
               ALU.mult).then_inc(S_("prob_ready"), 1)
            if u + 2 < NQ * NT:
                score_max(u + 2)
            if u >= 2 and u % 2 == 0:
                take_values(u // 2 - 1)
        take_values(NQ - 1)
        first_low(1)
        for t in range(NT):
            add_branch("rows_mix1", 0, 0, t, 1)
            normalise_x4(t, 1)
        split_modulated("xm1", 0, 1)
        dve.wait_ge(S_("ys_cleared"), 2)

        def tile_by_tile(t):
            if t:
                add_branch("rows_mlp1", 0, 1, t - 1, 1)
            if t == NT - 1:
                add_branch("rows_mlp1", 0, 1, t, 1)

        mlp(1, 1, tile_by_tile)

    @block.gpsimd
    def _(pool):
        g = nc.gpsimd
        turn = InTurn(pool, "pool_step")
        g.memset(ones[:, :], 1.0)
        g.memset(zeros[:, :], 0.0).then_inc(S_("gate_T_full"), 1)
        g.memset(eps[:, :], EPS).then_inc(S_("scattered"), 1)
        g.memset(cT[:, :, :], 0.0).then_inc(S_("ones_ready"), 1)
        for l in range(DEPTH):
            low_item(turn(g.tensor_tensor), g, l, 0)
            for b in (1, 3):
                freed(pool, (("x1", l), b))
                low_chunks(turn(g.tensor_tensor), b).then_inc(S_("mix_x_split_by_pool"), 1)
            low_item(turn(g.tensor_tensor), g, l, BY_VECTOR)
            freed(pool, ("ret_s", l, H4 - 1))
            g.memset(kdec[:, :, :, :], 0.0).then_inc(S_("kdec_ready"), 1)
            for j in range(BY_VECTOR + 1, SPLITS):
                low_item(turn(g.tensor_tensor), g, l, j)
            freed(pool, ("w_out", l, 0, 0))
            g.dma_start(wr[:, :, :], w_router[l].rearrange("(c p) e -> p c e", p=P)).then_inc(
                S_("router_landed"), 16)
        pool.wait_ge(S_("spread_ready"), 2 * DEPTH)
        g.dma_start(gfin[:, :], final_g.partition_broadcast(P)).then_inc(S_("final_g_landed"), 16)
        for b in range(4):
            freed(pool, ("moe", DEPTH - 1, b))
        g.dma_start(band[:, :, :, :].rearrange("p a b c -> p (a b c)"),
                    bands).then_inc(S_("bands_landed"), 16)
        g.dma_start(x4[:, NT:2 * NT, :],
                    ctx_x.rearrange("(t p) d -> p t d", p=P)).then_inc(S_("ctx_landed"), 16)
        g.dma_start(rows[:, 2, :], pool_scale.partition_broadcast(P)).then_inc(
            S_("pool_scale_landed"), 16)
        g.dma_start(rope_c[:, :, :, :].rearrange("p a b c -> p (a b c)"),
                    rope2).then_inc(S_("rope2_landed"), 16)
        g.dma_start(gqk[:, :, :].rearrange("p a b -> p (a b)"),
                    g_qk.partition_broadcast(P)).then_inc(S_("gqk_landed"), 16)

        tt = turn(g.tensor_tensor)

        def diagonal(l, which, s, post):
            at_ = (3 * which + 2) * KC
            tt(gate_col[:, :], mods[:, l, at_:at_ + KC, s], C(post, KC * l, KC), ALU.mult)
            turn.tick()
            tt(dg[:, :, :], ident.unsqueeze(1).broadcast_to([P, KC, P]),
               gate_col[:, :].unsqueeze(2).broadcast_to([P, KC, P]),
               ALU.mult).then_inc(S_("diag_ready"), 1)

        def split_odd_banks(tag, s):
            cols_ = slice(s * S, (s + 1) * S)
            for b in (1, 3):
                freed(pool, ((tag, s), b))
                part = slice(2 * b, 2 * b + 2)
                ins = tt(x_low[:, part, cols_], x_full[:, part, cols_],
                         x_high[:, part, cols_].bitcast(F32), ALU.subtract)
                if b == 1:
                    turn.tick()
            ins.then_inc(S_("x_split_by_pool"), 1)

        def clear_sums(tiles, added):
            pool.wait_ge(S_("x4_ready"), added)
            turn(g.memset)(ys[:, 0:tiles, :], 0.0).then_inc(S_("ys_cleared"), 1)

        diagonal(0, 0, 0, "g_mix_post")
        full(pool, ("rows_mix0", 0, 1))
        diagonal(0, 0, 1, "g_mix_post")
        pool.wait_ge(S_("pool_scale_landed"), 16)
        slot, _, value = items[("mix2", 0, 0)]
        pool.wait_ge(landed[slot], value)
        w = ring[:, slot, 0:2048].rearrange("p (g k e) -> p g k e", g=4, k=2)
        scale = rows[:, 2, :].rearrange("p (g e) -> p g e", g=4)
        for k in range(2):
            ins = tt(w[:, :, k, :], w[:, :, k, :], scale, ALU.mult)
            if k == 0:
                turn.tick()
        ins.then_inc(S_("pool_w_ready"), 1)
        full(pool, ("rows_mix0", 1, 1))
        diagonal(0, 1, 0, "g_mlp_post")
        full(pool, ("rows_mlp0", 0, 1))
        diagonal(0, 1, 1, "g_mlp_post")
        for s in range(2):
            split_odd_banks("xm0", s)
        clear_sums(2 * NT, X4_BEFORE["mlp0"])
        pool.wait_ge(S_("q_rot_ready"), NT)
        pool.wait_ge(S_("k_rot_ready"), 2 * NT)
        diagonal(1, 0, 0, "g_mix_post")
        full(pool, ("rows_mix1", 0, 1))
        diagonal(1, 1, 0, "g_mlp_post")
        split_odd_banks("xm1", 0)
        clear_sums(NT, X4_BEFORE["mlp1"])

    @block.sync
    def _(sp):
        sp.dma_start(h[:, :, :], x.rearrange("(t p) d -> p t d", p=P)).then_inc(
            S_("x_landed"), 16)

        def load(name, sources, view):
            slot = items[name][0]
            if free_at[name]:
                sp.wait_ge(weights_used, free_at[name])
            for out_, src in zip(view(ring[:, slot, :]), sources):
                sp.dma_start(out_, src).then_inc(landed[slot], 16)

        def chunked(w):
            return [w.rearrange("(c p) n -> p c n", p=P)]

        def eight(slot_):
            return [slot_.rearrange("p (c n) -> p c n", c=KC)]

        def four(slot_):
            return [slot_.rearrange("p (c n) -> p c n", c=4)]

        for l in range(DEPTH):
            ada_n = 0
            for n, kind in enumerate(mixer_items()):
                if kind == ADA:
                    src = w_ada[l, :, ada_n * 512:(ada_n + 1) * 512]
                    ada_n += 1
                else:
                    src = w_in[l, :, kind * 512:(kind + 1) * 512]
                load(("mix", l, n), chunked(src), eight)
            for n in range(2):
                load(("w_out", l, n), chunked(w_out[l, :, n * 512:(n + 1) * 512]), eight)
            for n in ADA_LATE:
                load(("late", l, n), chunked(w_ada[l, :, n * 512:(n + 1) * 512]), eight)
            sp.wait_ge(weights_used, items[("w_out", l, 1)][1] + 1)
            with sp.Fori(0, NEXP) as e:
                for n in range(6):
                    slot, number, _ = items[("moe", l, 0, n)]
                    sp.wait_ge(weights_used, 6 * e + (number - RING1 + 1))
                    if n < 4:
                        dst = ring[:, slot, :].rearrange("p (k a f) -> p k a f", k=2, a=2)
                        for a, w in enumerate((w_gate, w_up)):
                            src = w[l, bass.ds(e, 1), 2 * n * P:2 * (n + 1) * P, :]
                            sp.dma_start(dst[:, :, a, :],
                                         src.rearrange("o (k p) f -> p (o k) f", p=P)).then_inc(
                                landed[slot], 16)
                    else:
                        src = w_down[l, bass.ds(e, 1), :, :].rearrange(
                            "o (g two p) d -> two p (o g) d", two=2, p=P)[n - 4]
                        sp.dma_start(ring[:, slot, :].rearrange("p (g d) -> p g d", g=4),
                                     src).then_inc(landed[slot], 16)
        for l in range(DEPTH):
            if l == 0:
                load(("mix2", 0, 0), [w_pool.rearrange("g (k p) e -> p (g k) e", p=P)],
                     lambda s_: [s_[:, 0:2048].rearrange("p (c e) -> p c e", c=8)])
            else:
                for n in range(3):
                    load(("mix2", 1, n), chunked(w_qkv[:, n * 512:(n + 1) * 512]), eight)
                for n in range(2):
                    load(("mix2", 1, 3 + n), chunked(w_o[:, n * 512:(n + 1) * 512]), eight)
            with sp.Fori(0, 4) as i:
                for n in range(4):
                    slot, number, _ = items[("mlp", l, n)]
                    sp.wait_ge(weights_used, 4 * i + (number - RING2[l] + 1))
                    if n < 2:
                        src = w_mlp_in[l, :, bass.ds(i * 1024 + n * 512, 512)]
                        sp.dma_start(eight(ring[:, slot, :])[0],
                                     src.rearrange("(c p) n -> p c n", p=P)).then_inc(
                            landed[slot], 16)
                    else:
                        src = w_mlp_out[l, bass.ds(i * 1024 + (n - 2) * 512, 512), :]
                        sp.dma_start(four(ring[:, slot, :])[0],
                                     src.rearrange("(c p) n -> p c n", p=P)).then_inc(
                            landed[slot], 16)
        for t in range(NT):
            sp.wait_ge(S_("x4_ready"), X4_TOTAL - NT + t + 1)
            sp.dma_start(out[t * P:(t + 1) * P, :], x4[:, t, :]).then_inc(S_("stored"), 16)
        sp.wait_ge(S_("stored"), 16 * NT)

    es.close()


X4_BEFORE = {"mlp0": 2 + 4, "mlp1": 2 + 4 + 4 + 2}
X4_TOTAL = 2 + 4 + 4 + 2 + 2


def shape_constants():
    f = np.float32
    tok = np.arange(S)
    half = P // 2
    inv = f(10000.0) ** (-np.arange(half, dtype=f) / f(half))
    ang = tok.astype(f)[:, None] * inv[None, :]
    cos = np.concatenate([np.cos(ang)] * 2, 1)
    sin = np.concatenate([-np.sin(ang), np.sin(ang)], 1)

    def by_tile(a):
        return a.reshape(NT, P, -1).transpose(1, 0, 2).reshape(P, -1)

    gamma = np.log1p(-(2.0 ** (-5.0 - np.arange(H4, dtype=f)))).astype(f)
    dist = np.abs(np.arange(3 * P)[None, :] - P - np.arange(P)[:, None]).astype(f)
    decay = np.exp(gamma[None, :, None] * dist[:, None, :]) * HEAD_SCALE
    sel = np.zeros((P, 2), f)
    for g in range(4):
        for j in range(2):
            sel[32 * g + j, j] = 1
    token = np.stack([np.arange(P) + P * t for t in range(NT)], 1)
    delta = np.zeros((P, NEXP), f)
    delta[:NEXP] = np.eye(NEXP)
    consts = np.concatenate([np.eye(P), by_tile(cos), by_tile(sin), decay.reshape(P, -1), sel,
                             token, delta], 1).astype(f)

    masks = np.zeros((P, len(LEVELS), 2, P // 2), f)
    s = np.arange(P)[:, None]
    u = np.arange(P // 2)[None, :]
    for i, m in enumerate(LEVELS):
        same = s // (2 * m) == u // m
        masks[:, i, 0] = same & (s % (2 * m) < m)
        masks[:, i, 1] = same & (s % (2 * m) >= m)
    masks = masks.reshape(P, -1)

    bands = np.zeros((len(WINDOWS), S, S), f)
    for g, w in enumerate(WINDOWS):
        lo = np.clip(tok - w // 2, 0, S)
        hi = np.clip(tok + w - w // 2, 0, S)
        for t in range(S):
            bands[g, lo[t]:hi[t], t] = f(1) / f(hi[t] - lo[t])
            bands[g, t, t] -= f(1)
    bands = bands.reshape(len(WINDOWS), NT, P, S).transpose(2, 0, 1, 3).reshape(P, -1)

    inv2 = f(10000.0) ** (-np.arange(0, half, 2, dtype=f) / f(half))
    ar = (tok // GRID_W).astype(f)[:, None] * inv2
    ac = (tok % GRID_W).astype(f)[:, None] * inv2
    cos2 = np.concatenate([np.cos(ar)] * 2 + [np.cos(ac)] * 2, 1)
    sin2 = np.concatenate([-np.sin(ar), np.sin(ar), -np.sin(ac), np.sin(ac)], 1)
    rope2 = np.concatenate([by_tile(cos2), by_tile(sin2)], 1)
    return consts, masks, np.ascontiguousarray(bands, f), np.ascontiguousarray(rope2, f)


def kernel(**inputs):
    import concourse.bacc as bacc
    from concourse.bass_utils import run_bass_kernel_spmd

    a = {k: np.asarray(v) for k, v in inputs.items()}

    def columns(v):
        return np.asarray(v).reshape(-1, P).T

    cols = np.concatenate([columns(a[n]) for n in (
        "norm1_g", "norm2_g", "ret_norm_g", "hgrn_norm_g", "lower_bounds", "b_ada_2",
        "g_mix_pre_2", "g_mix_post_2", "g_mlp_pre_2", "g_mlp_post_2", "c_2", "c_ctx_2")], 1)
    assert cols.shape == (P, NCOLS)
    consts, masks, bands, rope2 = shape_constants()
    arrays = {
        "x": a["x"].reshape(S, D), "cols": cols, "w_in": a["w_in"], "w_out": a["w_out"],
        "w_router": a["w_router"], "w_gate": a["w_gate"], "w_up": a["w_up"],
        "w_down": a["w_down"], "final_g": a["final_norm_g"], "ctx_x": a["ctx_2"].reshape(S, D),
        "w_ada": a["w_ada_2"], "w_pool": a["w_pool_2"][0], "pool_scale": a["pool_scale_2"][0],
        "w_qkv": a["w_qkv_2"][0], "g_qk": np.concatenate([a["g_q_2"][0], a["g_k_2"][0]]),
        "w_o": a["w_o_2"][0], "w_mlp_in": a["w_mlp_in_2"], "w_mlp_out": a["w_mlp_out_2"],
        "consts": consts, "masks": masks, "bands": bands, "rope2": rope2,
    }
    arrays = {f"in_{k}": np.ascontiguousarray(v) for k, v in arrays.items()}
    nc = bacc.Bacc("TRN2", target_bir_lowering=False, num_devices=1)
    args = {k[3:]: nc.dram_tensor(k, v.shape, mybir.dt.from_np(v.dtype),
                                  kind="ExternalInput").ap() for k, v in arrays.items()}
    out = nc.dram_tensor("out", (S, D), F32, kind="ExternalOutput").ap()
    build_program(nc, out=out, **args)
    r = run_bass_kernel_spmd(nc, [arrays], core_ids=[0])
    return r.results[0]["out"].reshape(1, S, D)
```
